# Optimizing a Trainium2 kernel written in Bass

```python
import math
import jax
import jax.numpy as jnp
from jax import lax
import numpy as np

D_MODEL = 1024
BATCH = 1
SEQ = 512
DEPTH = 1

CHUNK = 64
PLE_DIM = 256
SB_HEADS = 8
SB_HEAD_DIM = 64
SB_WIDTH = SB_HEADS * SB_HEAD_DIM
SGU_GROUPS = 8
SGU_WIDTH = 512
SGU_GROUP_DIM = SGU_WIDTH // SGU_GROUPS
SGU_BLOCK = 128
QBLK = 128
N_EXPERTS = 32
TOP_K = 4
D_EXPERT = 1024
SWIGLU_ALPHA = 1.702
SWIGLU_LIMIT = 7.0
MOE_BLOCK = 128
EPS = 1e-6
SPLITS = (SB_WIDTH, SB_WIDTH, SB_WIDTH, SGU_WIDTH, SGU_WIDTH, D_MODEL, D_MODEL)
IN_COLS = sum(SPLITS)

kernel_name = 'hybrid_stickbreak_sgu_moe_block'

def rmsnorm(x, g):
    xf = x.astype(jnp.float32)
    y = xf * lax.rsqrt(jnp.mean(xf * xf, axis=-1, keepdims=True) + EPS)
    return (y * g.astype(jnp.float32)).astype(x.dtype)

def layernorm(x, g):
    xf = x.astype(jnp.float32)
    mu = jnp.mean(xf, axis=-1, keepdims=True)
    var = jnp.mean(jnp.square(xf - mu), axis=-1, keepdims=True)
    return ((xf - mu) * lax.rsqrt(var + EPS) * g.astype(jnp.float32)).astype(x.dtype)

def stick_breaking_attention(q, k, v):
    S = q.shape[2]
    scale = 1.0 / math.sqrt(q.shape[-1])
    outs = []
    for qb in range(S // QBLK):
        L = (qb + 1) * QBLK
        qi = q[:, :, qb * QBLK:L]
        z = jnp.einsum('bhtd,bhsd->bhts', qi, k[:, :, :L]).astype(jnp.float32) * scale
        t_pos = qb * QBLK + jnp.arange(QBLK)
        s_pos = jnp.arange(L)
        mask = s_pos[None, :] < t_pos[:, None]
        log_1mb = jnp.where(mask, jax.nn.log_sigmoid(-z), 0.0)
        rest = lax.cumsum(log_1mb, axis=3, reverse=True) - log_1mb
        w = jnp.where(mask, jnp.exp(jax.nn.log_sigmoid(z) + rest), 0.0)
        outs.append(jnp.einsum('bhts,bhsd->bhtd', w.astype(v.dtype), v[:, :, :L]))
    return jnp.concatenate(outs, axis=2)

def spatial_gating(u, vs, norm_g, w_s, b_s):
    B, S, _ = u.shape
    u = jax.nn.gelu(u)
    vs = layernorm(jax.nn.gelu(vs), norm_g)
    pos = jnp.arange(SGU_BLOCK)
    cmask = (pos[None, :] // CHUNK) <= (pos[:, None] // CHUNK)
    w_m = jnp.where(cmask[None], w_s, 0.0).astype(vs.dtype)
    vg = vs.reshape(B, S // SGU_BLOCK, SGU_BLOCK, SGU_GROUPS, SGU_GROUP_DIM)
    sv = jnp.einsum('gts,bnsgc->bntgc', w_m, vg) + b_s.T[None, None, :, :, None]
    return u * sv.reshape(B, S, SGU_WIDTH)

def token_mixer(a, w_in, w_out_a, w_out_b, w_out, sgu_norm, sgu_w, sgu_b):
    B, S, _ = a.shape
    zz = a @ w_in
    idx = list(np.cumsum(SPLITS)[:-1])
    q, k, v, u, vs, ga, gb = jnp.split(zz, idx, axis=-1)
    heads = lambda t: t.reshape(B, S, SB_HEADS, SB_HEAD_DIM).transpose(0, 2, 1, 3)
    o_a = stick_breaking_attention(heads(q), heads(k), heads(v))
    o_a = o_a.transpose(0, 2, 1, 3).reshape(B, S, SB_WIDTH)
    o_b = spatial_gating(u, vs, sgu_norm, sgu_w, sgu_b)
    merged = jax.nn.sigmoid(ga) * (o_a @ w_out_a) + jax.nn.sigmoid(gb) * (o_b @ w_out_b)
    return merged @ w_out

def moe(c, w_router, b_router, w1, b1, w2, b2):
    B, S, D = c.shape
    T = B * S
    cf = c.reshape(T, D)
    logits = (cf @ w_router + b_router).astype(jnp.float32)
    top_vals, top_idx = lax.top_k(logits, TOP_K)
    gates = jax.nn.softmax(top_vals, axis=-1).astype(c.dtype)
    e_flat = top_idx.reshape(-1)
    g_flat = gates.reshape(-1)
    tok_flat = jnp.repeat(jnp.arange(T), TOP_K)
    order = jnp.argsort(e_flat)
    e_sorted = e_flat[order]
    counts = jnp.bincount(e_flat, length=N_EXPERTS)
    offsets = jnp.cumsum(counts) - counts
    padded = ((counts + MOE_BLOCK - 1) // MOE_BLOCK) * MOE_BLOCK
    pad_end = jnp.cumsum(padded)
    pad_off = pad_end - padded
    rank = jnp.arange(T * TOP_K) - offsets[e_sorted]
    dest = pad_off[e_sorted] + rank
    n_blocks = -(-(T * TOP_K + N_EXPERTS * (MOE_BLOCK - 1)) // MOE_BLOCK)
    n_slots = n_blocks * MOE_BLOCK
    slot_tok = jnp.zeros((n_slots,), jnp.int32).at[dest].set(tok_flat[order].astype(jnp.int32))
    slot_gate = jnp.zeros((n_slots,), c.dtype).at[dest].set(g_flat[order])
    starts = jnp.arange(n_blocks) * MOE_BLOCK
    block_e = jnp.minimum(jnp.sum(starts[:, None] >= pad_end[None, :], axis=1), N_EXPERTS - 1)
    xs = cf[slot_tok].reshape(n_blocks, MOE_BLOCK, D)

    def expert_block(args):
        xb, e = args
        hh = xb @ w1[e] + b1[e]
        x_glu = jnp.minimum(hh[:, ::2], SWIGLU_LIMIT)
        x_lin = jnp.clip(hh[:, 1::2], -SWIGLU_LIMIT, SWIGLU_LIMIT)
        act = x_glu * jax.nn.sigmoid(SWIGLU_ALPHA * x_glu) * (x_lin + 1.0)
        return act @ w2[e] + b2[e]

    ys = lax.map(expert_block, (xs, block_e)).reshape(n_slots, D)
    out = jnp.zeros((T, D), c.dtype).at[slot_tok].add(ys * slot_gate[:, None])
    return out.reshape(B, S, D)

def setup_inputs(seed: int = 0) -> dict:
    key = jax.random.key(seed)
    ks = jax.random.split(key, 24)
    f32 = jnp.float32
    nrm = lambda k, shape, s: jax.random.normal(k, shape, f32) * s
    gain = lambda k, shape: 1.0 + 0.02 * jax.random.normal(k, shape, f32)
    return {
        'x': jax.random.normal(ks[0], (BATCH, SEQ, D_MODEL), f32),
        'p': jax.random.normal(ks[1], (DEPTH, BATCH, SEQ, PLE_DIM), f32),
        'g_mix': gain(ks[2], (DEPTH, D_MODEL)),
        'w_in': nrm(ks[3], (DEPTH, D_MODEL, IN_COLS), D_MODEL ** -0.5),
        'w_out_a': nrm(ks[4], (DEPTH, SB_WIDTH, D_MODEL), SB_WIDTH ** -0.5),
        'w_out_b': nrm(ks[5], (DEPTH, SGU_WIDTH, D_MODEL), SGU_WIDTH ** -0.5),
        'w_out': nrm(ks[6], (DEPTH, D_MODEL, D_MODEL), D_MODEL ** -0.5),
        'sgu_norm': gain(ks[7], (DEPTH, SGU_WIDTH)),
        'sgu_w': nrm(ks[8], (DEPTH, SGU_GROUPS, SGU_BLOCK, SGU_BLOCK), SGU_BLOCK ** -0.5),
        'sgu_b': 1.0 + 0.02 * jax.random.normal(ks[9], (DEPTH, SGU_GROUPS, SGU_BLOCK), f32),
        'g_moe': gain(ks[10], (DEPTH, D_MODEL)),
        'w_router': nrm(ks[11], (DEPTH, D_MODEL, N_EXPERTS), D_MODEL ** -0.5),
        'b_router': nrm(ks[12], (DEPTH, N_EXPERTS), 0.01),
        'w1': nrm(ks[13], (DEPTH, N_EXPERTS, D_MODEL, 2 * D_EXPERT), D_MODEL ** -0.5),
        'b1': nrm(ks[14], (DEPTH, N_EXPERTS, 2 * D_EXPERT), 0.02),
        'w2': nrm(ks[15], (DEPTH, N_EXPERTS, D_EXPERT, D_MODEL), D_EXPERT ** -0.5),
        'b2': nrm(ks[16], (DEPTH, N_EXPERTS, D_MODEL), 0.02),
        'g_ple': gain(ks[17], (DEPTH, D_MODEL)),
        'w_ple_gate': nrm(ks[18], (DEPTH, D_MODEL, D_MODEL), D_MODEL ** -0.5),
        'w_ple_proj': nrm(ks[19], (DEPTH, PLE_DIM, D_MODEL), PLE_DIM ** -0.5),
        'g_final': gain(ks[20], (D_MODEL,)),
    }

def reference(x, p, g_mix, w_in, w_out_a, w_out_b, w_out, sgu_norm, sgu_w, sgu_b,
              g_moe, w_router, b_router, w1, b1, w2, b2, g_ple, w_ple_gate, w_ple_proj, g_final):
    h = x
    for i in range(DEPTH):
        a = rmsnorm(h, g_mix[i])
        h = h + token_mixer(a, w_in[i], w_out_a[i], w_out_b[i], w_out[i],
                            sgu_norm[i], sgu_w[i], sgu_b[i])
        c = rmsnorm(h, g_moe[i])
        h = h + moe(c, w_router[i], b_router[i], w1[i], b1[i], w2[i], b2[i])
        pg = jax.nn.sigmoid(rmsnorm(h, g_ple[i]) @ w_ple_gate[i])
        h = h + pg * (p[i] @ w_ple_proj[i])
    return rmsnorm(h, g_final)


_drawn_inputs = setup_inputs


def setup_inputs(seed=0):
    import zlib

    import numpy as np

    out = dict(_drawn_inputs(seed))
    spreads = {}
    factors = {'b1': 6.145, 'b2': 7.048, 'g_ple': 45.33, 'g_final': 8.691}
    for name, (base, spread) in spreads.items():
        noise = np.random.default_rng([zlib.crc32(name.encode()), seed]).standard_normal(out[name].shape)
        drawn = base * np.exp(spread * noise) if base else spread * noise
        out[name] = jnp.asarray(drawn.astype(out[name].dtype))
    for name, factor in factors.items():
        out[name] = (out[name] * factor).astype(out[name].dtype)
    return out
```

```python
from contextlib import ExitStack

import concourse.bass as bass
from concourse import mybir

ALU = mybir.AluOpType
ACT = mybir.ActivationFunctionType
F32 = mybir.dt.float32
BF16 = mybir.dt.bfloat16
I32 = mybir.dt.int32
U32 = mybir.dt.uint32
AX_X = mybir.AxisListType.X

P = 128
EPS = 1e-6
SWIGLU_ALPHA = 1.702
SWIGLU_LIMIT = 7.0
TOP_K = 4
SLOTS = 64
SGU_CHUNK = 64


def hybrid_block(nc, x, p, g_mix, w_in, w_out_a, w_out_b, w_out, sgu_norm, sgu_w, sgu_b, g_moe, w_router,
                 b_router, w1, b1, w2, b2, g_ple, w_ple_gate, w_ple_proj, g_final, out, dbg=None):
    T, D = x.shape[1], x.shape[2]
    NT = T // P
    KD = D // P
    WIDTH = w_out_a.shape[1]
    KW = WIDTH // P
    HD = 64
    HP = WIDTH // (2 * HD)
    GROUPS = sgu_w.shape[1]
    E = w_router.shape[2]
    DE = w2.shape[2]
    PLE = p.shape[3]
    KP = PLE // P
    MAX_BLOCKS = (E * (SLOTS - 1) + T * TOP_K) // SLOTS
    NG = MAX_BLOCKS + 1
    ROWS = T + SLOTS
    CH = KD * WIDTH
    assert CH == 4096 and D == 1024 and DE == 1024 and NT == 4 and E == 32

    with ExitStack() as ctx:
        def sb(name, shape, dt=F32):
            return ctx.enter_context(nc.sbuf_tensor(name, shape, dt))

        def sem(name):
            return ctx.enter_context(nc.semaphore(name))

        c_rows = nc.dram_tensor("c_rows", (T, D), F32).ap()
        acc_rows = nc.dram_tensor("acc_rows", (ROWS, D), F32).ap()
        acc_halves = acc_rows.rearrange("r (h n) -> (r h) n", h=2)

        arena = sb("arena", [P, 11 * CH])

        def chunk(i, lo=0, n=CH):
            return arena[:, i * CH + lo:i * CH + lo + n]

        w1_buf = [[arena[:, (2 * e + b) * 2 * CH:(2 * e + b + 1) * 2 * CH].rearrange("p (k n) -> p k n", k=KD)
                   for b in range(2)] for e in range(2)]
        w2lo_buf = [chunk(8 + e).rearrange("p (k n) -> p k n", k=4) for e in range(2)]
        w2hi_buf = chunk(10).rearrange("p (k n) -> p k n", k=4)

        aT = chunk(0).rearrange("p (k t) -> p k t", k=KD)
        gateB = chunk(1).rearrange("p (k t) -> p k t", k=KD)
        gateA = chunk(4).rearrange("p (k t) -> p k t", k=KD)
        qT = chunk(8, 0, 2048).rearrange("p (k t) -> p k t", k=KW)
        uT = chunk(8, 2048, 2048).rearrange("p (k t) -> p k t", k=KW)
        vs = chunk(10, 0, 2048).rearrange("p (t c) -> p t c", t=NT)
        wmT = chunk(10, 2048, 1024).rearrange("p (g t) -> p g t", g=GROUPS)
        wm_raw = chunk(10, 3072, 1024).rearrange("p (g s) -> p g s", g=GROUPS)
        kT = chunk(5, 0, 2048).rearrange("p (k t) -> p k t", k=KW)
        v = chunk(5, 2048, 2048).rearrange("p (t c) -> p t c", t=NT)
        h = chunk(5).rearrange("p (t c) -> p t c", t=NT)
        xs = chunk(9).rearrange("p (t c) -> p t c", t=NT)
        bias_f32 = chunk(1, 0, 3072)
        junk = chunk(1, 3072, 1024)
        oaT, obT, merged = qT, uT, gateA

        ident = sb("ident", [P, P])
        tri = sb("tri", [P, P])
        neg1 = sb("neg1", [P, P])
        ones_b = sb("ones_b", [P, P], BF16)
        upper_b = sb("upper_b", [P, P], BF16)
        xg = sb("xg", [P, 1024])
        xT = sb("xT", [P, KD, SLOTS])
        act_work = sb("act_work", [P, 3 * 512])
        glu, sig, lin = (act_work[:, 512 * i:512 * i + 512].rearrange("p (b n) -> p b n", b=2) for i in range(3))
        out_work = sb("out_work", [P, 2 * 512])
        actT = out_work[:, 0:512].rearrange("p (b c s) -> p b c s", b=2, c=2)
        y_sb = out_work[:, 512:1024]
        bias_sb = sb("bias_sb", [96, 3072], BF16)
        sel_sb = sb("sel_sb", [96, E], BF16)
        sel_cur = sb("sel_cur", [96, 2, SLOTS], BF16)
        g_mix_c = sb("g_mix_c", [P, KD])
        g_ple_c = sb("g_ple_c", [P, KD])
        sgu_g_c = sb("sgu_g_c", [P, KW])
        sgu_b_bc = out_work[:, 0:512].rearrange("p (g t) -> p g t", g=GROUPS // 2)
        b_router_bc = sb("b_router_bc", [P, E])
        w_router_sb = sb("w_router_sb", [P, KD, E])
        small = sb("small", [P, 64])
        bn6 = sb("bn6", [P, NT, 6])
        bn2 = sb("bn2", [P, NT, 2])
        iota_i = sb("iota_i", [P, NG], I32)
        iota_f = sb("iota_f", [P, NG])
        tok1_f = sb("tok1_f", [P, NT])
        pad_c = sb("pad_c", [P, 2])
        pad_i = sb("pad_i", [P, 6], I32)
        tok_idx = sb("tok_idx", [P, NG], I32)
        dst_idx = sb("dst_idx", [P, NG], I32)
        gate_tab = sb("gate_tab", [P, NG])
        cum_i = sb("cum_i", [P, E + 1], I32)
        perm_i = sb("perm_i", [P, E + 1], I32)
        g_idx = sb("g_idx", [SLOTS, 1], I32)
        s_idx = sb("s_idx", [P, 1], I32)
        g_moe_bc = xg
        place_oh = out_work[:, :].rearrange("p (pos e) -> p pos e", e=E)
        place_v = act_work[:, 0:E * E].rearrange("p (pos e) -> p pos e", e=E)
        ATT = (NT + 3 + 2 + 1) * P
        att_e = [chunk(9, 0, ATT), chunk(9, ATT, ATT)]
        att_s = [chunk(9, 2 * ATT, ATT), act_work[:, 0:ATT]]
        cT = out_work[:, :].rearrange("p (k t) -> p k t", k=KD)
        route = chunk(9).rearrange("p (j n) -> p j n", j=NT * TOP_K)
        lg = sb("lg", [P, NT, E])
        top_v = sb("top_v", [P, NT, 8])
        top_i = sb("top_i", [P, NT, 8], U32)
        top_f = sb("top_f", [P, NT, 8])
        onehot = xT[:, :, :].rearrange("p k s -> p (k s)").rearrange("p (t k e) -> p t k e", t=NT, k=TOP_K)
        mask = sb("mask", [P, NT, E])
        mask_b = sb("mask_b", [P, NT, E], BF16)
        gates = sb("gates", [P, NT, TOP_K])
        gsum = sb("gsum", [P, NT])
        grec = sb("grec", [P, NT])
        nmax = sb("nmax", [P, NT])
        n_blk = sb("n_blk", [P, 2, E])
        cum_f = sb("cum_f", [P, E + 1])
        heavy = sb("heavy", [P, 6, E])
        n_heavy = sb("n_heavy", [P, 8])
        base64 = sb("base64", [P, E])
        zeros_e = sb("zeros_e", [P, E])
        posm = sb("posm", [P, NT, E])
        pos = sb("pos", [P, NT * TOP_K])
        pos_i = sb("pos_i", [P, 3, NT * TOP_K], I32)
        pos_f = sb("pos_f", [P, 2, NT * TOP_K])
        tab_t = xT[:, 0:2, :]

        ps = ctx.enter_context(nc.psum_tensor("ps", [P, 8, 512], F32))

        s = {n: sem(n) for n in (
            "x_in", "small_in", "g_bc_in", "wm_in", "bias_in", "x_again", "const_dve", "const_pool", "ident_ok",
            "sq_done", "rms_ok", "sqrt_done", "xn_ok", "xT_tr", "aT_act", "aT_dve", "wm_tr", "wmT_ok",
            "unit_done", "evac_act", "evac_dve", "z_done", "tri_done",
            "abs_ok", "ln_ok", "exp_ok", "sp_ok", "sp_masked", "w_ok", "w_masked",
            "ln_stats", "ln_std", "vs_ok", "ob_ok", "ob_tmp", "merged_ok", "oa_ok",
            "h_ok", "h_sq", "h_var", "h_std", "c_ok", "c_tr", "cT_ok", "logit_done", "c_written", "acc_done",
            "top_ok", "gexp_ok", "mask_ok", "rank_done", "route_ok", "table_done", "tables_ok",
            "dve_step", "act_step", "pool_step", "bias_ok",
            "tx_done", "xg_in", "xT_ok", "hA_done", "hB_done", "glu_ok", "sig_ok", "act_ok",
            "tA_done", "actT_ok", "mm2lo_done", "y_done", "y_ok", "y_free", "sel_ok", "moe_step", "tx_turn", "dma_turn",
            "ple_in", "acc_in", "p_tr", "pT_ok", "t_sq", "t_var", "t_std", "hn_ok", "hn_tr", "hnT_act", "hnT_dve",
            "pg_done", "pg_sig", "h2_ok", "f_sq", "f_var", "f_std", "out_ok", "out_written",
        )}
        PIECES = 12
        piece_in = [sem(f"piece_in_{j}") for j in range(4)]
        ring_in = {c: sem(f"ring_in_{c}") for c in (2, 3, 6, 7)}

        GROUP_BUF = {"q": 2, "k": 3, "v": 6, "vs": 7, "u": 2, "ga0": 3, "ga1": 6, "gb0": 7, "gb1": 2,
                     "woa": 3, "wob": 2, "wo0": 7, "wo1": 6}
        LOAD_ORDER = ["q", "k", "v", "vs", "u", "ga0", "ga1", "gb0", "gb1", "woa", "wo1", "wo0", "wob"]
        COLS = {"q": 0, "k": 1, "v": 2, "u": 3, "vs": 4, "ga0": 5, "ga1": 6, "gb0": 7, "gb1": 8}
        fill = [(g, j) for g in ("vs", "u", "ga0", "ga1", "gb0", "gb1") for j in range(4)]
        units = [(g, j) for g in ("q", "k", "v") for j in range(4)]
        pe_plan = [("unit", u) for u in units]
        PER = len(fill) // HP // 2
        for hp in range(HP):
            pe_plan.append(("z", hp))
            pe_plan += [("unit", u) for u in fill[2 * PER * hp:2 * PER * hp + PER]]
            pe_plan.append(("tri", hp))
            pe_plan += [("unit", u) for u in fill[2 * PER * hp + PER:2 * PER * (hp + 1)]]
            pe_plan.append(("unit", ("out", hp)))
            if hp == 2:
                pe_plan += [("unit", ("sv", j)) for j in range(GROUPS // 2)]
            if hp == 0:
                pe_plan.append(("ln", 0))
        pe_plan += [("unit", ("woa", j)) for j in range(KD)] + [("unit", ("wob", j)) for j in range(KD)]
        units = [a for k, a in pe_plan if k == "unit"]
        MIX_UNITS = len(units)
        units += [("wo", j) for j in range(2 * NT)]
        ON_ACT = ("q", "v", "vs", "u", "ga0", "ga1", "gb0", "gb1", "out")
        evac_of, counts = {}, {"evac_act": 0, "evac_dve": 0}
        for u in units:
            e = "evac_act" if u[0] in ON_ACT else "evac_dve"
            counts[e] += 1
            evac_of[u] = (e, counts[e])
        unit_no = {u: i + 1 for i, u in enumerate(units)}

        def unit_bank(u):
            return ps[:, 6 + (unit_no[u] - 1) % 2, :]

        last_unit = {g: (g, 3) for g in COLS} | {"woa": ("woa", KD - 1), "wob": ("wob", KD - 1)}
        ring_count = {}
        seen = {c: 0 for c in ring_in}
        prev_in_buf, last_of = {}, {}
        for g in LOAD_ORDER:
            c = GROUP_BUF[g]
            seen[c] += 1
            ring_count[g] = 16 * seen[c]
            prev_in_buf[g] = last_of.get(c)
            last_of[c] = g

        def ring_wait(eng, g):
            eng.wait_ge(ring_in[GROUP_BUF[g]], ring_count[g])

        OFF = {0: 0, 1: 512, 3: 896, 2: 1024}

        w_in_v = w_in[0].rearrange("(k p) n -> p k n", p=P)

        def ring_view(g, k=KD):
            return chunk(GROUP_BUF[g]).rearrange("p (k n) -> p k n", k=k)

        x_v = x[0].rearrange("(t p) d -> p t d", p=P)
        out_v = out[0].rearrange("(t p) d -> p t d", p=P)
        w1_v = w1[0].rearrange("e (k p) n -> p e k n", p=P)
        w2_v = w2[0].rearrange("e (k p) n -> p e k n", p=P)

        wg = w1_buf[0][0]
        wproj = chunk(2, 0, 2048).rearrange("p (k n) -> p k n", k=KP)
        p_sb = chunk(2, 2048, 1024).rearrange("p (t c) -> p t c", t=NT)
        gf_bc = chunk(2, 3072, 1024)
        pT = chunk(3, 0, 1024).rearrange("p (k t) -> p k t", k=KP)
        hf = chunk(4).rearrange("p (t c) -> p t c", t=NT)
        hnT = [chunk(5, 1024 * i, 1024).rearrange("p (k t) -> p k t", k=KD) for i in range(2)]
        hn = [chunk(5, 2048 + 1024 * i, 1024) for i in range(2)]
        outs_sb = chunk(6).rearrange("p (t c) -> p t c", t=NT)
        sg = [chunk(7, 1024 * i, 1024) for i in range(2)]
        pp = chunk(3, 1024, 1024)
        acc_in = [sem(f"acc_in_{t}") for t in range(NT)]

        block = ctx.enter_context(nc.Block())

        @block.sync
        def _(sp):
            for t in range(NT):
                sp.dma_start(xs[:, t, :], x_v[:, t, :]).then_inc(s["x_in"], 16)
            with nc.allow_non_contiguous_dma(reason="gains by feature on partitions: 20 kB once"):
                sp.dma_start(g_mix_c[:], g_mix[0].rearrange("(k p) -> p k", p=P)).then_inc(s["small_in"], 16)
                sp.dma_start(sgu_g_c[:], sgu_norm[0].rearrange("(k p) -> p k", p=P)).then_inc(s["small_in"], 16)
                sp.dma_start(g_ple_c[:], g_ple[0].rearrange("(k p) -> p k", p=P)).then_inc(s["small_in"], 16)
            for j in range(GROUPS):
                sp.dma_start(sgu_b_bc[64 * (j % 2):64 * (j % 2) + 64, j // 2, :],
                             sgu_b[0, j:j + 1, :].to_broadcast([64, P])).then_inc(s["small_in"], 16)
            sp.dma_start(b_router_bc[:], b_router[0:1, :].to_broadcast([P, E])).then_inc(s["small_in"], 16)
            sp.dma_start(w_router_sb[:], w_router[0].rearrange("(k p) e -> p k e", p=P)).then_inc(s["small_in"], 16)
            sp.dma_start(wm_raw, sgu_w[0].rearrange("g t s -> t g s")).then_inc(s["wm_in"], 16)

            def load_group(g):
                if prev_in_buf[g]:
                    sp.wait_ge(s["unit_done"], unit_no[last_unit[prev_in_buf[g]]])
                if g in COLS:
                    src = w_in_v[:, :, COLS[g] * WIDTH:(COLS[g] + 1) * WIDTH]
                elif g in ("woa", "wob"):
                    w = w_out_a if g == "woa" else w_out_b
                    src = w[0].rearrange("(k p) n -> p k n", p=P)
                else:
                    n = int(g[2])
                    src = w_out[0].rearrange("(k p) n -> p k n", p=P)[:, 4 * n:4 * n + 4, :]
                dst = ring_view(g, src.shape[1])
                sp.dma_start(dst, src).then_inc(ring_in[GROUP_BUF[g]], 16)

            for g in LOAD_ORDER[:4]:
                load_group(g)
            sp.dma_start(g_moe_bc[:], g_moe[0:1, :].to_broadcast([P, D])).then_inc(s["g_bc_in"], 16)
            for i in range(3):
                sp.dma_start(bias_f32[32 * i:32 * i + 32, 0:2 * DE], b1[0]).then_inc(s["bias_in"], 16)
                sp.dma_start(bias_f32[32 * i:32 * i + 32, 2 * DE:3 * DE], b2[0]).then_inc(s["bias_in"], 16)
            for g in LOAD_ORDER[4:-1]:
                load_group(g)
            sp.wait_ge(s["unit_done"], unit_no[("out", HP - 1)])
            for t in range(NT):
                sp.dma_start(xs[:, t, :], x_v[:, t, :]).then_inc(s["x_again"], 16)
            load_group(LOAD_ORDER[-1])

            def load_expert(pos_, e, par, first, w1a_free, w1b_free, w2lo_free, w2hi_free):
                free = {0: w1a_free, 4: w1b_free, 8: w2lo_free, 10: w2hi_free}
                for j in range(PIECES):
                    if j in free:
                        free[j]()
                    if j >= 3:
                        sp.wait_ge(piece_in[(j - 3) % 4], 16 * (3 * pos_ + (j - 3) // 4 + 1))
                    elif not first:
                        sp.wait_ge(piece_in[(j + 1) % 4], 16 * (3 * pos_))
                    if j < 8:
                        k = slice(2 * (j % 4), 2 * (j % 4) + 2)
                        dst, src = w1_buf[par][j // 4][:, k, :], w1_v[:, e, k, DE * (j // 4):DE * (j // 4 + 1)]
                    else:
                        k = 2 * (j % 2)
                        dst = (w2lo_buf[par] if j < 10 else w2hi_buf)[:, k:k + 2, :]
                        src = w2_v[:, e, 2 * (j - 8):2 * (j - 8) + 2, :]
                    sp.dma_start(dst, src).then_inc(piece_in[j % 4], 16)

            load_expert(0, 0, 0, True,
                        lambda: sp.wait_ge(s["merged_ok"], KD),
                        lambda: sp.wait_ge(s["unit_done"], unit_no[("wob", KD - 1)]),
                        lambda: sp.wait_ge(s["unit_done"], unit_no[("wob", KD - 1)]),
                        lambda: sp.wait_ge(s["ob_ok"], GROUPS // 2))

            def h_left():
                sp.wait_ge(s["unit_done"], len(units))
                sp.wait_ge(s["acc_done"], 16 * (NT + 1))
                sp.wait_ge(s["c_ok"], NT)

            cum1 = [None]

            def first_done():
                cum1[0] = sp.value_load(cum_i[0:1, 1:2], min_val=1, max_val=MAX_BLOCKS)
                sp.wait_ge(s["y_done"], cum1[0])

            load_expert(1, 1, 1, False, h_left, lambda: None,
                        lambda: sp.wait_ge(s["tables_ok"], 1), first_done)
            with sp.Fori(1, E // 2) as i:
                for par in range(2):
                    two_back = sp.value_load(cum_i[0:1, bass.ds(2 * i + par - 1, 1)], min_val=1, max_val=MAX_BLOCKS)
                    one_back = sp.value_load(cum_i[0:1, bass.ds(2 * i + par, 1)], min_val=1, max_val=MAX_BLOCKS)
                    expert = sp.value_load(perm_i[0:1, bass.ds(2 * i + par, 1)], min_val=0, max_val=E - 1)
                    load_expert(2 * i + par, expert, par, False,
                                lambda: sp.wait_ge(s["hA_done"], two_back),
                                lambda: sp.wait_ge(s["hB_done"], two_back),
                                lambda: sp.wait_ge(s["mm2lo_done"], two_back),
                                lambda: sp.wait_ge(s["y_done"], one_back))
            e30 = sp.value_load(cum_i[0:1, E - 1:E], min_val=1, max_val=MAX_BLOCKS)
            sp.wait_ge(s["hA_done"], e30)
            sp.dma_start(w1_buf[0][0], w_ple_gate[0].rearrange("(k p) n -> p k n", p=P)).then_inc(s["ple_in"], 16)
            sp.wait_ge(s["hB_done"], e30)
            sp.dma_start(wproj, w_ple_proj[0].rearrange("(k p) n -> p k n", p=P)).then_inc(s["ple_in"], 16)
            sp.dma_start(p_sb, p[0, 0].rearrange("(t p) d -> p t d", p=P)).then_inc(s["ple_in"], 16)
            sp.dma_start(gf_bc, g_final.rearrange("(a d) -> a d", a=1).to_broadcast([P, D])).then_inc(s["ple_in"], 16)
            nb = sp.value_load(cum_i[0:1, E:E + 1], min_val=1, max_val=MAX_BLOCKS)
            sp.wait_ge(s["acc_done"], 16 * (NT + 1) + nb * 16)
            for t in range(NT):
                sp.dma_start(hf[:, t, :], acc_rows[t * P:(t + 1) * P, :]).then_inc(acc_in[t], 16)
            for t in range(NT):
                sp.wait_ge(s["out_ok"], t + 1)
                sp.dma_start(out_v[:, t, :], outs_sb[:, t, :]).then_inc(s["out_written"], 16)
            sp.wait_ge(s["out_written"], 16 * NT)


        @block.tensor
        def _(pe):
            def wait_unit_bank(u):
                n = unit_no[u]
                if n > 2:
                    e, c = evac_of[units[n - 3]]
                    pe.wait_ge(s[e], c)

            pe.wait_ge(s["ident_ok"], 1)
            for t in range(NT):
                pe.wait_ge(s["xn_ok"], t + 1)
                for k in range(KD):
                    last = pe.transpose(ps[:, k, t * P:(t + 1) * P], xs[:, t, k * P:(k + 1) * P], ident[:, :])
            last.then_inc(s["xT_tr"], 1)
            pe.wait_ge(s["aT_act"], KD // 2)
            pe.wait_ge(s["aT_dve"], KD // 2)
            pe.wait_ge(s["wm_in"], 16)
            for g in range(GROUPS):
                last = pe.transpose(ps[:, g // 4, (g % 4) * P:(g % 4 + 1) * P], wm_raw[:, g, :], ident[:, :])
            last.then_inc(s["wm_tr"], 1)

            def product_T(u, w, j, rhs, nk):
                for k in range(nk):
                    last = pe.matmul(unit_bank(u), w[:, k, j * P:(j + 1) * P], rhs[:, k, :],
                                     start=(k == 0), stop=(k == nk - 1))
                return last

            def unit(u):
                g, j = u
                wait_unit_bank(u)
                if g in ("q", "k", "u", "ga0", "ga1", "gb0", "gb1"):
                    if j == 0:
                        ring_wait(pe, g)
                    last = product_T(u, ring_view(g), j, aT, KD)
                elif g in ("v", "vs"):
                    if j == 0:
                        ring_wait(pe, g)
                    w = ring_view(g)
                    for k in range(KD):
                        last = pe.matmul(unit_bank(u), aT[:, k, j * P:(j + 1) * P], w[:, k, :],
                                         start=(k == 0), stop=(k == KD - 1))
                elif g == "out":
                    pe.wait_ge(s["w_masked"], 2 * (j + 1))
                    for t in range(NT):
                        for i in range(2):
                            last = pe.matmul(unit_bank(u)[HD * i:HD * i + HD, t * P:],
                                             v[:, t, (2 * j + i) * HD:(2 * j + i + 1) * HD],
                                             att_e[i][:, OFF[t]:OFF[t] + (NT - t) * P],
                                             start=(t == 0), stop=(t == NT - 1), skip_group_check=True)
                elif g == "sv":
                    pe.wait_ge(s["vs_ok"], NT)
                    pe.wait_ge(s["wmT_ok"], 1)
                    for t in range(NT):
                        for i in range(2):
                            last = pe.matmul(unit_bank(u)[64 * i:64 * i + 64, t * P:(t + 1) * P],
                                             vs[:, t, (2 * j + i) * 64:(2 * j + i + 1) * 64],
                                             wmT[:, 2 * j + i, :], start=True, stop=True, skip_group_check=True)
                elif g == "woa":
                    if j == 0:
                        ring_wait(pe, g)
                        e, c = evac_of[("out", HP - 1)]
                        pe.wait_ge(s[e], c)
                    last = product_T(u, ring_view(g, KW), j, oaT, KW)
                elif g == "wob":
                    if j == 0:
                        ring_wait(pe, g)
                        pe.wait_ge(s["ob_ok"], GROUPS // 2)
                    last = product_T(u, ring_view(g, KW), j, obT, KW)
                else:
                    t, n = j // 2, j % 2
                    if j == 0:
                        ring_wait(pe, "wo0")
                        ring_wait(pe, "wo1")
                        pe.wait_ge(s["merged_ok"], KD)
                    for k in range(KD):
                        last = pe.matmul(unit_bank(u), merged[:, k, t * P:(t + 1) * P],
                                         ring_view(f"wo{k // 4}", 4)[:, k % 4, n * 512:(n + 1) * 512],
                                         start=(k == 0), stop=(k == KD - 1))
                last.then_inc(s["unit_done"], 1)

            for kind, a in pe_plan:
                if kind == "unit":
                    unit(a)
                elif kind == "z":
                    e, c = evac_of[("q", a)]
                    pe.wait_ge(s[e], c)
                    e, c = evac_of[("k", a)]
                    pe.wait_ge(s[e], c)
                    if a == 0:
                        pe.wait_ge(s["wmT_ok"], 1)
                    else:
                        pe.wait_ge(s["w_ok"], 2 * a)
                    for t in (0, 1, 3, 2):
                        for i in range(2):
                            z = ps[:, 3 * i:3 * i + 3, :].rearrange("p b n -> p (b n)")
                            last = pe.matmul(z[:, OFF[t]:OFF[t] + (NT - t) * P],
                                             kT[HD * i:HD * i + HD, a, t * P:(t + 1) * P],
                                             qT[HD * i:HD * i + HD, a, t * P:],
                                             start=(t != 3), stop=False, skip_group_check=True)
                    last.then_inc(s["z_done"], 1)
                elif kind == "tri":
                    for i in range(2):
                        pe.wait_ge(s["sp_masked"], 2 * a + i + 1)
                        z = ps[:, 3 * i:3 * i + 3, :].rearrange("p b n -> p (b n)")
                        sp_ = att_s[i]
                        for t in range(NT):
                            for t2 in range(t, NT):
                                n = (NT - t2) * P
                                end = OFF[t] + (NT - t) * P
                                last = pe.matmul(z[:, end - n:end], (tri if t2 == t else neg1)[:, :],
                                                 sp_[:, OFF[t2]:OFF[t2] + n], start=False, stop=(t2 == NT - 1),
                                                 skip_group_check=True)
                        last.then_inc(s["tri_done"], 1)

            def c_transposes(t):
                pe.wait_ge(s["c_ok"], t + 1)
                for k in range(KD):
                    last = pe.transpose(ps[:, k // 4, (k % 4) * P:(k % 4 + 1) * P], xs[:, t, k * P:(k + 1) * P],
                                        ident[:, :])
                last.then_inc(s["c_tr"], 1)

            def logits(t):
                pe.wait_ge(s["cT_ok"], t + 1)
                for k in range(KD):
                    last = pe.matmul(ps[:, 2, t * E:(t + 1) * E], cT[:, k, :], w_router_sb[:, k, :],
                                     start=(k == 0), stop=(k == KD - 1))
                last.then_inc(s["logit_done"], 1)

            def wo(t):
                unit(("wo", 2 * t))
                unit(("wo", 2 * t + 1))

            wo(0)
            wo(1)
            c_transposes(0)
            wo(2)
            logits(0)
            c_transposes(1)
            wo(3)
            logits(1)
            for t in range(2, NT):
                c_transposes(t)
                logits(t)

            pe.wait_ge(s["mask_ok"], 1)
            for t in range(NT):
                for t2 in range(t + 1):
                    pe.matmul(ps[:, 3, t * E:(t + 1) * E], (upper_b if t2 == t else ones_b)[:, :], mask_b[:, t2, :],
                              start=(t2 == 0), stop=(t2 == t))
            for t in range(NT):
                last = pe.matmul(ps[:, 3, NT * E:(NT + 1) * E], ones_b[:, :], mask_b[:, t, :],
                                 start=(t == 0), stop=(t == NT - 1))
            last.then_inc(s["rank_done"], 1)
            for j in range(NT * TOP_K):
                if j % TOP_K == 0:
                    pe.wait_ge(s["route_ok"], j // TOP_K + 1)
                last = pe.matmul(ps[:, 0, 0:2 * NG], route[:, j, 0:P], route[:, j, P:P + 2 * NG],
                                 start=(j == 0), stop=(j == NT * TOP_K - 1))
            last.then_inc(s["table_done"], 1)

            def x_transposes():
                for k in range(KD):
                    last = pe.transpose(ps[:, 3, k * SLOTS:(k + 1) * SLOTS], xg[0:SLOTS, k * P:(k + 1) * P],
                                        ident[0:SLOTS, 0:SLOTS])
                last.then_inc(s["tx_done"], 1)

            def act_transposes(g, b):
                pe.wait_ge(s["act_ok"], 2 * g + b + 1)
                for c in range(2):
                    last = pe.transpose(ps[:, 4 + b, c * P:(c + 1) * P], glu[:, b, c * P:(c + 1) * P], ident[:, :])
                last.then_inc(s["tA_done"], 1)

            pe.wait_ge(s["xg_in"], 16)
            x_transposes()

            def experts_block(g, e, par):
                pe.wait_ge(s["sel_ok"], e + 1)
                pe.wait_ge(s["xT_ok"], g + 1)
                for b in range(2):
                    for half in range(2):
                        col = DE * b + 512 * half
                        pe.matmul(ps[64 * half:64 * half + 64, b, :], sel_cur[:, par, :], bias_sb[:, col:col + 512],
                                  start=True, stop=False, skip_group_check=True)
                    for k in range(KD):
                        if k % 2 == 0:
                            pe.wait_ge(piece_in[k // 2], 16 * (3 * e + b + 1))
                        for half in range(2):
                            last = pe.matmul(ps[64 * half:64 * half + 64, b, :], xT[:, k, :],
                                             w1_buf[par][b][:, k, 512 * half:512 * half + 512],
                                             start=False, stop=(k == KD - 1), skip_group_check=True)
                    last.then_inc(s["hA_done" if b == 0 else "hB_done"], 1)
                act_transposes(g, 0)
                pe.wait_ge(s["xg_in"], 16 * g + 32)
                pe.sem_inc(s["tx_turn"], 1)
                x_transposes()
                pe.wait_ge(s["y_ok"], g + 1)
                for half in range(2):
                    col = 2 * DE + 512 * half
                    pe.matmul(ps[64 * half:64 * half + 64, 2, :], sel_cur[:, par, :],
                              bias_sb[:, col:col + 512], start=True, stop=False, skip_group_check=True)
                for b in range(2):
                    pe.wait_ge(s["actT_ok"], 2 * g + b + 1)
                    w2 = (w2lo_buf[par], w2hi_buf)[b]
                    for k in range(4):
                        if b == 0 and k == 2:
                            act_transposes(g, 1)
                        if k % 2 == 0:
                            pe.wait_ge(piece_in[2 * b + k // 2], 16 * (3 * e + 3))
                        for half in range(2):
                            last = pe.matmul(ps[64 * half:64 * half + 64, 2, :],
                                             actT[:, b, k % 2, 64 * (k // 2):64 * (k // 2) + 64],
                                             w2[:, k, 512 * half:512 * half + 512],
                                             start=False, stop=(b == 1 and k == 3), skip_group_check=True)
                    last.then_inc(s["mm2lo_done" if b == 0 else "y_done"], 1)

            with pe.Fori(0, E // 2) as i:
                for par in range(2):
                    e = 2 * i + par
                    first = pe.value_load(cum_i[0:1, bass.ds(e, 1)], min_val=0, max_val=MAX_BLOCKS)
                    end = pe.value_load(cum_i[0:1, bass.ds(e + 1, 1)], min_val=1, max_val=MAX_BLOCKS)
                    with pe.Fori(first, end) as g:
                        experts_block(g, e, par)

            pe.wait_ge(s["ple_in"], 64)
            for k in range(KP):
                for t in range(NT):
                    last = pe.transpose(ps[:, 6 + k, t * P:(t + 1) * P], p_sb[:, t, k * P:(k + 1) * P], ident[:, :])
            last.then_inc(s["p_tr"], 1)
            pe.wait_ge(s["pT_ok"], 1)

            def hn_transposes(t):
                pe.wait_ge(s["hn_ok"], t + 1)
                if t:
                    pe.wait_ge(s["hnT_act"], t)
                    pe.wait_ge(s["hnT_dve"], t)
                for k in range(KD):
                    last = pe.transpose(ps[:, k // 4, (k % 4) * P:(k % 4 + 1) * P], hn[t % 2][:, k * P:(k + 1) * P],
                                        ident[:, :])
                last.then_inc(s["hn_tr"], 1)

            def gate(t):
                if t:
                    pe.wait_ge(s["h2_ok"], t)
                pe.wait_ge(s["hnT_act"], t + 1)
                pe.wait_ge(s["hnT_dve"], t + 1)
                for n in range(2):
                    for k in range(KP):
                        pe.matmul(ps[:, 6 + n, :], pT[:, k, t * P:(t + 1) * P], wproj[:, k, n * 512:(n + 1) * 512],
                                  start=(k == 0), stop=(k == KP - 1))
                for n in range(2):
                    for k in range(KD):
                        last = pe.matmul(ps[:, 2 + n, :], hnT[t % 2][:, k, :], wg[:, k, n * 512:(n + 1) * 512],
                                         start=(k == 0), stop=(k == KD - 1))
                last.then_inc(s["pg_done"], 1)

            hn_transposes(0)
            for t in range(NT):
                if t + 1 < NT:
                    hn_transposes(t + 1)
                gate(t)

        @block.scalar
        def _(act):
            act.wait_ge(s["x_in"], 16 * NT)
            for t in range(NT):
                last = act.activation(ps[:, 2 * t:2 * t + 2, :].rearrange("p b n -> p (b n)"), xs[:, t, :],
                                      ACT.Square, accum_out=small[:, t:t + 1])
            last.then_inc(s["sq_done"], 1)
            act.wait_ge(s["rms_ok"], 1)
            act.activation(small[:, 4:8], small[:, 4:8], ACT.Sqrt).then_inc(s["sqrt_done"], 1)
            act.wait_ge(s["small_in"], 16 * (5 + GROUPS))
            act.wait_ge(s["xT_tr"], 1)
            for k in range(0, KD, 2):
                act.activation(aT[:, k, :], ps[:, k, :], ACT.Copy, scale=g_mix_c[:, k:k + 1]).then_inc(s["aT_act"], 1)

            def evac(u):
                g, j = u
                act.wait_ge(s["unit_done"], unit_no[u])
                bank = unit_bank(u)
                if g == "q":
                    ins = act.activation(qT[:, j, :], bank, ACT.Copy, scale=float(HD) ** -0.5)
                elif g == "v":
                    ins = act.activation(v[:, j, :], bank, ACT.Copy)
                elif g == "out":
                    ins = act.activation(oaT[:, j, :], bank, ACT.Copy)
                elif g == "vs":
                    ins = act.activation(vs[:, j, :], bank, ACT.Gelu_apprx_tanh)
                elif g == "u":
                    ins = act.activation(uT[:, j, :], bank, ACT.Gelu_apprx_tanh)
                else:
                    if g == "gb0" and j == 0:
                        act.wait_ge(s["bias_ok"], 1)
                    dst = gateA if g[1] == "a" else gateB
                    ins = act.activation(dst[:, 4 * int(g[2]) + j, :], bank, ACT.Exp, scale=-1.0)
                ins.then_inc(s["evac_act"], 1)

            for kind, a in pe_plan:
                if kind == "unit" and a[0] in ON_ACT:
                    evac(a)
                elif kind == "z":
                    for i in range(2):
                        z = ps[:, 3 * i:3 * i + 3, :].rearrange("p b n -> p (b n)")
                        if i == 0:
                            act.wait_ge(s["z_done"], a + 1)
                            if a:
                                act.wait_ge(s["unit_done"], unit_no[("out", a - 1)])
                        act.activation(att_e[i], z[:, 0:ATT], ACT.Abs).then_inc(s["abs_ok"], 1)
                        act.wait_ge(s["abs_ok"], 2 * a + i + 1)
                        act.activation(att_e[i], att_e[i], ACT.Exp, scale=-1.0).then_inc(s["exp_ok"], 1)
                        act.wait_ge(s["exp_ok"], 2 * a + i + 1)
                        act.activation(att_e[i], att_e[i], ACT.Ln, bias=1.0).then_inc(s["ln_ok"], 1)
                elif kind == "tri":
                    for i in range(2):
                        z = ps[:, 3 * i:3 * i + 3, :].rearrange("p b n -> p (b n)")
                        act.wait_ge(s["tri_done"], 2 * a + i + 1)
                        act.activation(att_e[i], z[:, 0:ATT], ACT.Exp).then_inc(s["w_ok"], 1)
                elif kind == "ln":
                    act.wait_ge(s["ln_stats"], 1)
                    act.activation(small[:, 12:16], small[:, 8:12], ACT.Sqrt).then_inc(s["ln_std"], 1)

            def square_h(t):
                act.wait_ge(s["h_ok"], 2 * (t + 1))
                act.activation(ps[:, 4:6, :].rearrange("p b n -> p (b n)"), h[:, t, :], ACT.Square,
                               accum_out=small[:, 20 + t:21 + t]).then_inc(s["h_sq"], 1)
                act.wait_ge(s["h_var"], t + 1)
                act.activation(small[:, 28 + t:29 + t], small[:, 24 + t:25 + t], ACT.Sqrt).then_inc(s["h_std"], 1)

            def cT_copy(t):
                act.wait_ge(s["c_tr"], t + 1)
                act.activation(cT[:, :, :].rearrange("p k t -> p (k t)"), ps[:, 0:2, :].rearrange("p b n -> p (b n)"),
                               ACT.Copy).then_inc(s["cT_ok"], 1)

            square_h(0)
            square_h(1)
            cT_copy(0)
            square_h(2)
            cT_copy(1)
            square_h(3)
            cT_copy(2)
            cT_copy(3)
            act.wait_ge(s["top_ok"], 1)
            for t in range(NT):
                last = act.activation(gates[:, t, :], top_v[:, t, 0:TOP_K], ACT.Exp, bias=nmax[:, t:t + 1],
                                      accum_out=gsum[:, t:t + 1])
            last.then_inc(s["gexp_ok"], 1)

            def x_copy():
                act.activation(xT[:, :, :].rearrange("p k s -> p (k s)"), ps[:, 3, :], ACT.Copy).then_inc(s["xT_ok"], 1)

            act.wait_ge(s["tx_done"], 1)
            x_copy()
            n_all = act.value_load(cum_i[0:1, E:E + 1], min_val=1, max_val=MAX_BLOCKS)
            with act.Fori(0, n_all) as g:
                for b in range(2):
                    act.wait_ge(s["glu_ok"], 2 * g + b + 1)
                    act.activation(sig[:, b, :], glu[:, b, :], ACT.Sigmoid, scale=SWIGLU_ALPHA).then_inc(s["sig_ok"], 1)
                for b in range(2):
                    act.wait_ge(s["tA_done"], 2 * g + b + 1)
                    act.activation(actT[:, b, :, :].rearrange("p c s -> p (c s)"), ps[:, 4 + b, 0:2 * P],
                                   ACT.Copy).then_inc(s["actT_ok"], 1)
                    if b == 0:
                        act.wait_ge(s["tx_done"], g + 2)
                        x_copy()

            act.wait_ge(s["p_tr"], 1)
            act.activation(pT[:, :, :].rearrange("p k t -> p (k t)"), ps[:, 6:8, :].rearrange("p b n -> p (b n)"),
                           ACT.Copy).then_inc(s["pT_ok"], 1)

            def square_f(t):
                act.wait_ge(acc_in[t], 16)
                act.activation(ps[:, 4:6, :].rearrange("p b n -> p (b n)"), hf[:, t, :], ACT.Square,
                               accum_out=small[:, 32 + t:33 + t]).then_inc(s["t_sq"], 1)
                act.wait_ge(s["t_var"], t + 1)
                act.activation(small[:, 40 + t:41 + t], small[:, 36 + t:37 + t], ACT.Sqrt).then_inc(s["t_std"], 1)

            def hnT_copy(t):
                act.wait_ge(s["hn_tr"], t + 1)
                for k in range(KD // 2):
                    last = act.activation(hnT[t % 2][:, k, :], ps[:, k // 4, (k % 4) * P:(k % 4 + 1) * P], ACT.Copy,
                                          scale=g_ple_c[:, k:k + 1])
                last.then_inc(s["hnT_act"], 1)

            square_f(0)
            hnT_copy(0)
            square_f(1)
            for t in range(NT):
                if t + 1 < NT:
                    hnT_copy(t + 1)
                if t + 2 < NT:
                    square_f(t + 2)
                act.wait_ge(s["pg_done"], t + 1)
                act.activation(sg[t % 2], ps[:, 2:4, :].rearrange("p b n -> p (b n)"),
                               ACT.Sigmoid).then_inc(s["pg_sig"], 1)
                act.wait_ge(s["h2_ok"], t + 1)
                act.activation(ps[:, 4:6, :].rearrange("p b n -> p (b n)"), hf[:, t, :], ACT.Square,
                               accum_out=small[:, 44 + t:45 + t]).then_inc(s["f_sq"], 1)
                act.wait_ge(s["f_var"], t + 1)
                act.activation(small[:, 52 + t:53 + t], small[:, 48 + t:49 + t], ACT.Sqrt).then_inc(s["f_std"], 1)

        @block.vector
        def _(dve):
            done = [0]

            def link(ins):
                done[0] += 1
                ins.then_inc(s["dve_step"], 1)
                dve.wait_ge(s["dve_step"], done[0])

            link(dve.memset(zeros_e[:], 0.0))
            dve.wait_ge(s["sq_done"], 1)
            dve.tensor_scalar(small[:, 4:8], small[:, 0:4], 1.0 / D, EPS, ALU.mult, ALU.add).then_inc(s["rms_ok"], 1)
            dve.wait_ge(s["sqrt_done"], 1)
            link(dve.reciprocal(small[:, 16:20], small[:, 4:8]))
            for t in range(NT):
                dve.tensor_scalar(xs[:, t, :], xs[:, t, :], small[:, 16 + t:17 + t], None,
                                  ALU.mult).then_inc(s["xn_ok"], 1)
            dve.wait_ge(s["small_in"], 16 * (5 + GROUPS))
            dve.wait_ge(s["xT_tr"], 1)
            for k in range(1, KD, 2):
                dve.tensor_scalar(aT[:, k, :], ps[:, k, :], g_mix_c[:, k:k + 1], None, ALU.mult).then_inc(s["aT_dve"], 1)
            dve.wait_ge(s["wm_tr"], 1)
            link(dve.tensor_copy(wmT[:, :, :].rearrange("p g t -> p (g t)"),
                                 ps[:, 0:2, :].rearrange("p b n -> p (b n)")))
            dve.memset(wmT[SGU_CHUNK:P, :, 0:SGU_CHUNK], 0.0).then_inc(s["wmT_ok"], 1)

            def evac(u):
                g, j = u
                dve.wait_ge(s["unit_done"], unit_no[u])
                bank = unit_bank(u)
                if g == "k":
                    dve.tensor_copy(kT[:, j, :], bank).then_inc(s["evac_dve"], 1)
                elif g == "sv":
                    b3 = bank.rearrange("p (t n) -> p t n", t=NT)
                    bias = sgu_b_bc[:, j:j + 1, :].to_broadcast([P, NT, P])
                    link(dve.scalar_tensor_tensor(out=b3, in0=b3, scalar=sgu_g_c[:, j:j + 1], in1=bias,
                                                  op0=ALU.mult, op1=ALU.add))
                    e, c = evac_of[("u", j)]
                    dve.wait_ge(s[e], c)
                    link(dve.tensor_tensor(obT[:, j, :], bank, uT[:, j, :], ALU.mult))
                    dve.sem_inc(s["ob_ok"], 1)
                    dve.sem_inc(s["evac_dve"], 1)
                elif g in ("woa", "wob"):
                    gt = gateA if g == "woa" else gateB
                    link(dve.tensor_tensor(gt[:, j, :], gt[:, j, :], bank, ALU.mult))
                    dve.sem_inc(s["evac_dve"], 1)
                    if g == "wob":
                        dve.tensor_tensor(merged[:, j, :], gateA[:, j, :], gateB[:, j, :],
                                          ALU.add).then_inc(s["merged_ok"], 1)

            def sigmoid(u):
                g, j = u
                e, c = evac_of[u]
                dve.wait_ge(s[e], c)
                gt = (gateA if g[1] == "a" else gateB)[:, 4 * int(g[2]) + j, :]
                link(dve.tensor_scalar(gt, gt, 1.0, None, ALU.add))
                link(dve.reciprocal(gt, gt))

            for kind, a in pe_plan:
                if kind == "unit" and a[0] not in ON_ACT:
                    evac(a)
                elif kind == "unit" and a[0] in ("ga0", "ga1", "gb0", "gb1"):
                    sigmoid(a)
                elif kind == "unit" and a == ("vs", 3):
                    dve.wait_ge(s["evac_act"], evac_of[a][1])
                    for t in range(NT):
                        link(dve.bn_stats(bn6[:, t, :], vs[:, t, :]))
                        link(dve.bn_aggr(bn2[:, t, :], bn6[:, t, :]))
                    dve.tensor_scalar(small[:, 8:12], bn2[:, :, 1], EPS, None, ALU.add).then_inc(s["ln_stats"], 1)
                elif kind == "ln":
                    dve.wait_ge(s["ln_std"], 1)
                    link(dve.reciprocal(small[:, 56:60], small[:, 12:16]))
                    for t in range(NT):
                        dve.tensor_scalar(vs[:, t, :], vs[:, t, :], bn2[:, t, 0:1], small[:, 56 + t:57 + t],
                                          ALU.subtract, ALU.mult).then_inc(s["vs_ok"], 1)
                elif kind == "z":
                    zs = [ps[:, 3 * i:3 * i + 3, :].rearrange("p b n -> p (b n)")[:, 0:ATT] for i in range(2)]
                    for i in range(2):
                        dve.wait_ge(s["ln_ok"], 2 * a + i + 1)
                        dve.scalar_tensor_tensor(out=att_s[i], in0=zs[i], scalar=0.0, in1=att_e[i],
                                                 op0=ALU.max, op1=ALU.add).then_inc(s["sp_ok"], 1)

            dve.wait_ge(s["x_again"], 16 * NT)
            dve.wait_ge(s["g_bc_in"], 16)
            for t in range(NT):
                for n in range(2):
                    u = ("wo", 2 * t + n)
                    dve.wait_ge(s["unit_done"], unit_no[u])
                    sl = slice(n * 512, (n + 1) * 512)
                    link(dve.tensor_tensor(h[:, t, sl], unit_bank(u), xs[:, t, sl], ALU.add))
                    dve.sem_inc(s["evac_dve"], 1)
                    dve.sem_inc(s["h_ok"], 1)
                dve.wait_ge(s["h_sq"], t + 1)
                dve.tensor_scalar(small[:, 24 + t:25 + t], small[:, 20 + t:21 + t], 1.0 / D, EPS, ALU.mult,
                                  ALU.add).then_inc(s["h_var"], 1)
                dve.wait_ge(s["h_std"], t + 1)
                link(dve.reciprocal(small[:, 60 + t % 2:61 + t % 2], small[:, 28 + t:29 + t]))
                dve.scalar_tensor_tensor(out=xs[:, t, :], in0=h[:, t, :], scalar=small[:, 60 + t % 2:61 + t % 2],
                                         in1=g_moe_bc[:, :], op0=ALU.mult, op1=ALU.mult).then_inc(s["c_ok"], 1)

            dve.wait_ge(s["logit_done"], NT)
            for t in range(NT):
                link(dve.tensor_tensor(lg[:, t, :], ps[:, 2, t * E:(t + 1) * E], b_router_bc[:, :], ALU.add))
                link(dve.max(top_v[:, t, :], lg[:, t, :]))
                link(dve.max_index(top_i[:, t, :], top_v[:, t, :], lg[:, t, :]))
            dve.tensor_scalar(nmax[:, :], top_v[:, :, 0], -1.0, None, ALU.mult).then_inc(s["top_ok"], 1)
            link(dve.tensor_copy(top_f[:, :, :], top_i[:, :, :]))
            dve.wait_ge(s["const_pool"], 1)
            link(dve.tensor_copy(iota_f[:, :], iota_i[:, :]))
            for t in range(NT):
                last = dve.tensor_tensor(onehot[:, t, :, :], top_f[:, t, 0:TOP_K].unsqueeze(2).to_broadcast([P, TOP_K, E]),
                                         iota_f[:, 0:E].unsqueeze(1).to_broadcast([P, TOP_K, E]), ALU.is_equal)
            link(last)
            for t in range(NT):
                last = dve.tensor_reduce(mask[:, t, :], onehot[:, t, :, :].rearrange("p k e -> p e k"), AX_X, ALU.add)
            link(last)
            dve.tensor_copy(mask_b[:, :, :], mask[:, :, :]).then_inc(s["mask_ok"], 1)
            dve.wait_ge(s["gexp_ok"], 1)
            link(dve.reciprocal(grec[:, :], gsum[:, :]))
            link(dve.tensor_tensor(gates[:, :, :], gates[:, :, :], grec[:, :].unsqueeze(2).to_broadcast([P, NT, TOP_K]),
                                   ALU.mult))
            dve.wait_ge(s["rank_done"], 1)
            cnt = ps[:, 3, NT * E:(NT + 1) * E]
            link(dve.tensor_scalar(n_blk[:, 1, :], cnt, float(SLOTS), 1.0, ALU.is_gt, ALU.add))
            for j in range(2, T // SLOTS):
                link(dve.scalar_tensor_tensor(out=n_blk[:, j % 2, :], in0=cnt, scalar=float(SLOTS * j),
                                              in1=n_blk[:, (j - 1) % 2, :], op0=ALU.is_gt, op1=ALU.add))
            nb = n_blk[:, (T // SLOTS - 1) % 2, :]
            N2 = E - 2
            hv, cnt_h, hi_n, lo_n, t0, t1 = (heavy[:, i, 2:E] for i in range(6))
            n_h, n_l, n_m, x_h, x_l, x_l1 = (n_heavy[:, i:i + 1] for i in range(6))
            link(dve.tensor_scalar(hv, nb[:, 2:E], 1.0, None, ALU.is_gt))
            link(dve.tensor_tensor_scan(cnt_h, zeros_e[:, 2:E], hv, 0.0, ALU.add, ALU.add))
            dve.tensor_copy(n_h, heavy[:, 1, E - 1:E])
            link(dve.tensor_scalar(n_l, heavy[:, 1, E - 1:E], -1.0, float(N2), ALU.mult, ALU.add))
            link(dve.tensor_tensor(n_m, n_h, n_l, ALU.min))
            dve.tensor_tensor(x_h, n_h, n_m, ALU.subtract)
            link(dve.tensor_tensor(x_l, n_l, n_m, ALU.subtract))
            dve.tensor_scalar(x_l1, x_l, -1.0, None, ALU.add)
            dve.tensor_tensor(hi_n, cnt_h, hv, ALU.subtract)
            link(dve.tensor_scalar(heavy[:, 0, 0:2], zeros_e[:, 0:2], 0.0, None, ALU.mult))
            link(dve.tensor_tensor(lo_n, iota_f[:, 0:N2], hi_n, ALU.subtract))
            dve.tensor_scalar(t0, hi_n, x_h, 0.0, ALU.subtract, ALU.max)
            link(dve.tensor_scalar(t1, lo_n, x_l1, 0.0, ALU.subtract, ALU.max))
            dve.scalar_tensor_tensor(out=t0, in0=t0, scalar=x_l, in1=hi_n, op0=ALU.add, op1=ALU.add)
            link(dve.scalar_tensor_tensor(out=t1, in0=t1, scalar=x_h, in1=lo_n, op0=ALU.add, op1=ALU.add))
            link(dve.tensor_tensor(t0, t0, t1, ALU.subtract))
            link(dve.tensor_tensor(t0, t0, hv, ALU.mult))
            place = heavy[:, 4, :]
            link(dve.scalar_tensor_tensor(out=t0, in0=t0, scalar=2.0, in1=t1, op0=ALU.add, op1=ALU.add))
            link(dve.tensor_copy(heavy[:, 4, 0:2], iota_f[:, 0:2]))
            link(dve.tensor_tensor(place_oh, place.unsqueeze(1).to_broadcast([P, E, E]),
                                   iota_f[:, 0:E].unsqueeze(2).to_broadcast([P, E, E]), ALU.is_equal))
            link(dve.tensor_tensor(place_v, place_oh, nb.unsqueeze(1).to_broadcast([P, E, E]), ALU.mult))
            link(dve.tensor_reduce(heavy[:, 2, :], place_v, AX_X, ALU.add))
            link(dve.memset(cum_f[:, 0:1], 0.0))
            link(dve.tensor_tensor_scan(cum_f[:, 1:E + 1], zeros_e[:, :], heavy[:, 2, :], 0.0, ALU.add, ALU.add))
            link(dve.tensor_copy(cum_i[:, :], cum_f[:, :]))
            link(dve.scalar_tensor_tensor(out=place_v, in0=place_oh, scalar=float(SLOTS),
                                          in1=cum_f[:, 0:E].unsqueeze(2).to_broadcast([P, E, E]),
                                          op0=ALU.mult, op1=ALU.mult))
            link(dve.tensor_reduce(base64[:, :], place_v.rearrange("p pos e -> p e pos"), AX_X, ALU.add))
            link(dve.tensor_tensor(posm[:, :, :], ps[:, 3, 0:NT * E].rearrange("p (t e) -> p t e", t=NT),
                                   base64[:, :].unsqueeze(1).to_broadcast([P, NT, E]), ALU.add))
            dve.wait_ge(s["c_written"], 16 * NT)
            for t in range(NT):
                last = dve.tensor_tensor(onehot[:, t, :, :], onehot[:, t, :, :],
                                         posm[:, t, :].unsqueeze(1).to_broadcast([P, TOP_K, E]), ALU.mult)
            link(last)
            link(dve.tensor_reduce(pos[:, :], onehot[:, :, :, :].rearrange("p t k e -> p (t k) e"), AX_X, ALU.add))
            link(dve.tensor_copy(pos_i[:, 0, :], pos[:, :]))
            link(dve.tensor_scalar(pos_i[:, 1, :], pos_i[:, 0, :], 6, None, ALU.arith_shift_right))
            link(dve.tensor_scalar(pos_i[:, 2, :], pos_i[:, 0, :], SLOTS - 1, None, ALU.bitwise_and))
            link(dve.tensor_copy(pos_f[:, :, :], pos_i[:, 1:3, :]))
            for t in range(NT):
                ks = slice(TOP_K * t, TOP_K * t + TOP_K)
                shape = [P, TOP_K, NG]
                io = iota_f[:, :].unsqueeze(1).to_broadcast(shape)
                hot = route[:, ks, P:P + NG]
                for d in range(2):
                    dve.tensor_tensor(route[:, ks, SLOTS * d:SLOTS * d + SLOTS], io,
                                      pos_f[:, 1, ks].unsqueeze(2).to_broadcast(shape), ALU.is_equal)
                link(dve.tensor_tensor(hot, io, pos_f[:, 0, ks].unsqueeze(2).to_broadcast(shape), ALU.is_equal))
                link(dve.tensor_tensor(route[:, ks, P + NG:P + 2 * NG], hot,
                                       gates[:, t, :].unsqueeze(2).to_broadcast(shape), ALU.mult))
                dve.tensor_scalar(hot, hot, tok1_f[:, t:t + 1], None, ALU.mult).then_inc(s["route_ok"], 1)
            link(dve.tensor_tensor(place_v, place_oh, iota_f[:, 0:E].unsqueeze(1).to_broadcast([P, E, E]), ALU.mult))
            link(dve.tensor_reduce(heavy[:, 3, :], place_v, AX_X, ALU.add))
            link(dve.memset(perm_i[:, E:E + 1], 0))
            link(dve.tensor_copy(perm_i[:, 0:E], heavy[:, 3, :]))
            dve.wait_ge(s["table_done"], 1)
            tab = ps[:, 0, 0:NG]
            dve.tensor_scalar(tok_idx[:, :], tab, -1.0, 0.0, ALU.add, ALU.max)
            dve.tensor_copy(gate_tab[:, :], ps[:, 0, NG:2 * NG])
            dve.tensor_scalar(tab_t[:, 0, :], tab, 0.0, pad_c[:, 0:1], ALU.is_equal, ALU.mult)
            link(dve.tensor_scalar(tab_t[:, 1, :], tab, 2.0, pad_c[:, 1:2], ALU.mult, ALU.add))
            link(dve.tensor_tensor(dst_idx[:, :], tab_t[:, 0, :], tab_t[:, 1, :], ALU.add))
            dve.tensor_copy(sel_cur[:, 0, :], sel_sb[:, 0:1].to_broadcast([96, SLOTS])).then_inc(s["sel_ok"], 1)
            dve.sem_inc(s["tables_ok"], 1)
            dve.sem_inc(s["y_ok"], 1)

            STEPS = 10

            def experts_block(g):
                for b in range(2):
                    hh = ps[:, b, :].rearrange("p (n two) -> p n two", two=2)
                    dve.wait_ge(s["hA_done" if b == 0 else "hB_done"], g + 1)
                    dve.tensor_scalar(glu[:, b, :], hh[:, :, 0], SWIGLU_LIMIT, None, ALU.min).then_inc(s["glu_ok"], 1)
                    dve.tensor_scalar(lin[:, b, :], hh[:, :, 1], SWIGLU_LIMIT, -SWIGLU_LIMIT, ALU.min,
                                      ALU.max).then_inc(s["moe_step"], 1)
                    dve.wait_ge(s["sig_ok"], 2 * g + b + 1)
                    dve.tensor_tensor(glu[:, b, :], glu[:, b, :], sig[:, b, :], ALU.mult).then_inc(s["moe_step"], 1)
                    dve.wait_ge(s["moe_step"], 4 * g + 2 * b + 2)
                    dve.scalar_tensor_tensor(out=glu[:, b, :], in0=lin[:, b, :], scalar=1.0, in1=glu[:, b, :],
                                             op0=ALU.add, op1=ALU.mult).then_inc(s["act_ok"], 1)
                dve.wait_ge(s["y_done"], g + 1)
                dve.wait_ge(s["acc_done"], 16 * g + 16 * (NT + 1))
                dve.tensor_scalar(y_sb[:, :], ps[:, 2, :], gate_tab[:, bass.ds(g, 1)], None,
                                  ALU.mult).then_inc(s["y_ok"], 1)

            with dve.Fori(0, E // 2) as i:
                for par in range(2):
                    e = 2 * i + par
                    first = dve.value_load(cum_i[0:1, bass.ds(e, 1)], min_val=0, max_val=MAX_BLOCKS)
                    end = dve.value_load(cum_i[0:1, bass.ds(e + 1, 1)], min_val=1, max_val=MAX_BLOCKS)
                    nxt = dve.value_load(perm_i[0:1, bass.ds(e + 1, 1)], min_val=0, max_val=E - 1)
                    dve.tensor_copy(sel_cur[:, 1 - par, :],
                                    sel_sb[:, bass.ds(nxt, 1)].to_broadcast([96, SLOTS])).then_inc(s["sel_ok"], 1)
                    with dve.Fori(first, end) as g:
                        experts_block(g)

            base = done[0]

            def norm_f(t):
                dve.wait_ge(s["t_sq"], t + 1)
                dve.tensor_scalar(small[:, 36 + t:37 + t], small[:, 32 + t:33 + t], 1.0 / D, EPS, ALU.mult,
                                  ALU.add).then_inc(s["t_var"], 1)
                dve.wait_ge(s["t_std"], t + 1)
                link(dve.reciprocal(small[:, 62:63], small[:, 40 + t:41 + t]))
                dve.tensor_scalar(hn[t % 2], hf[:, t, :], small[:, 62:63], None, ALU.mult).then_inc(s["hn_ok"], 1)

            def hnT_copy(t):
                dve.wait_ge(s["hn_tr"], t + 1)
                for k in range(KD // 2, KD):
                    last = dve.tensor_scalar(hnT[t % 2][:, k, :], ps[:, k // 4, (k % 4) * P:(k % 4 + 1) * P],
                                             g_ple_c[:, k:k + 1], None, ALU.mult)
                last.then_inc(s["hnT_dve"], 1)

            norm_f(0)
            hnT_copy(0)
            norm_f(1)
            for t in range(NT):
                if t + 1 < NT:
                    hnT_copy(t + 1)
                if t + 2 < NT:
                    norm_f(t + 2)
                sgt = sg[t % 2]
                dve.wait_ge(s["pg_sig"], t + 1)
                link(dve.tensor_tensor(sgt, sgt, ps[:, 6:8, :].rearrange("p b n -> p (b n)"), ALU.mult))
                dve.tensor_tensor(hf[:, t, :], hf[:, t, :], sgt, ALU.add).then_inc(s["h2_ok"], 1)
                dve.wait_ge(s["f_sq"], t + 1)
                dve.tensor_scalar(small[:, 48 + t:49 + t], small[:, 44 + t:45 + t], 1.0 / D, EPS, ALU.mult,
                                  ALU.add).then_inc(s["f_var"], 1)
                dve.wait_ge(s["f_std"], t + 1)
                link(dve.reciprocal(small[:, 63:64], small[:, 52 + t:53 + t]))
                dve.scalar_tensor_tensor(out=outs_sb[:, t, :], in0=hf[:, t, :], scalar=small[:, 63:64], in1=gf_bc,
                                         op0=ALU.mult, op1=ALU.mult).then_inc(s["out_ok"], 1)

        @block.gpsimd
        def _(pool):
            done = [0]

            def link(ins):
                done[0] += 1
                ins.then_inc(s["pool_step"], 1)
                pool.wait_ge(s["pool_step"], done[0])

            link(pool.memset(ident[:], 0.0))
            pool.affine_select(out=ident[:], in_=ident[:], pattern=[[-1, P]], compare_op=ALU.not_equal, fill=1.0,
                               base=0, channel_multiplier=1).then_inc(s["ident_ok"], 1)
            pool.memset(neg1[:], -1.0)
            pool.memset(tri[:], -1.0)
            pool.memset(ones_b[:], 1.0)
            pool.memset(upper_b[:], 1.0)
            link(pool.memset(sel_sb[:], 0.0))
            link(pool.affine_select(out=tri[:], in_=tri[:], pattern=[[-1, P]], compare_op=ALU.is_ge, fill=0.0,
                                    base=0, channel_multiplier=1))
            link(pool.affine_select(out=upper_b[:], in_=upper_b[:], pattern=[[1, P]], compare_op=ALU.is_gt, fill=0.0,
                                    base=0, channel_multiplier=-1))
            for j in range(3):
                v_ = sel_sb[32 * j:32 * j + 32, :]
                link(pool.affine_select(out=v_, in_=v_, pattern=[[-1, E]], compare_op=ALU.not_equal, fill=1.0,
                                        base=0, channel_multiplier=1))
            link(pool.iota(iota_i[:], pattern=[[1, NG]], base=0, channel_multiplier=0))
            link(pool.iota(pad_i[:, 0:NT], pattern=[[P, NT]], base=1, channel_multiplier=1))
            for half in range(2):
                sl = slice(64 * half, 64 * half + 64)
                link(pool.iota(pad_i[sl, 4:5], pattern=[[1, 1]], base=2 * T + 2, channel_multiplier=2))
                link(pool.iota(pad_i[sl, 5:6], pattern=[[1, 1]], base=half - 2, channel_multiplier=0))
            pool.tensor_copy(tok1_f[:, :], pad_i[:, 0:NT])
            link(pool.tensor_copy(pad_c[:, :], pad_i[:, 4:6]))
            pool.sem_inc(s["const_pool"], 1)

            pool.wait_ge(s["bias_in"], 16 * 6)
            link(pool.tensor_copy(bias_sb[:, :], bias_f32[0:96, :]))
            for j in (1, 2):
                for r in range(j, 3):
                    rows = slice(32 * r, 32 * r + 32)
                    link(pool.tensor_tensor(bias_f32[rows, :], bias_f32[rows, :], bias_sb[rows, :], ALU.subtract))
                    link(pool.tensor_copy(bias_sb[rows, :], bias_f32[rows, :]))
            pool.sem_inc(s["bias_ok"], 1)

            pool.dma_start(acc_rows[T:ROWS, :], x[0, 0:SLOTS, :]).then_inc(s["acc_done"], 16)

            def mask_diagonals(a):
                for t in range(NT):
                    d = a[:, OFF[t]:OFF[t] + P]
                    last = pool.affine_select(out=d, in_=d, pattern=[[1, P]], compare_op=ALU.is_gt, fill=0.0,
                                              base=0, channel_multiplier=-1)
                return last

            for hp in range(HP):
                for i in range(2):
                    pool.wait_ge(s["sp_ok"], 2 * hp + i + 1)
                    mask_diagonals(att_s[i]).then_inc(s["sp_masked"], 1)
                for i in range(2):
                    pool.wait_ge(s["w_ok"], 2 * hp + i + 1)
                    mask_diagonals(att_e[i]).then_inc(s["w_masked"], 1)
            for t in range(NT):
                pool.wait_ge(s["h_ok"], 2 * (t + 1))
                pool.dma_start(acc_rows[t * P:(t + 1) * P, :], h[:, t, :]).then_inc(s["acc_done"], 16)
                pool.wait_ge(s["c_ok"], t + 1)
                pool.dma_start(c_rows[t * P:(t + 1) * P, :], xs[:, t, :]).then_inc(s["c_written"], 16)

            def gather():
                pool.indirect_dma_start(out=xg[0:SLOTS, :], out_offset=None, in_=c_rows,
                                        in_offset=bass.IndirectOffsetOnAxis(ap=g_idx[:, 0:1], axis=0),
                                        ).then_inc(s["xg_in"], 16)

            pool.wait_ge(s["tables_ok"], 1)
            link(pool.tensor_copy(g_idx[:, :], tok_idx[0:SLOTS, 0:1]))
            pool.wait_ge(s["c_written"], 16 * NT)
            gather()
            base = done[0]

            def gather_next(g, n):
                pool.wait_ge(s["tx_done"], g + 1)
                pool.tensor_copy(g_idx[:, :], tok_idx[0:SLOTS, bass.ds(g + 1, 1)]).then_inc(s["pool_step"], 1)
                pool.wait_ge(s["pool_step"], base + n)
                pool.sem_inc(s["dma_turn"], 1)
                gather()

            def scatter(g, n):
                pool.wait_ge(s["acc_done"], 16 * g + 16 * (NT + 1))
                pool.tensor_copy(s_idx[:, :], dst_idx[:, bass.ds(g, 1)]).then_inc(s["pool_step"], 1)
                pool.wait_ge(s["pool_step"], base + n)
                pool.wait_ge(s["y_ok"], g + 2)
                pool.sem_inc(s["dma_turn"], 1)
                pool.indirect_dma_start(out=acc_halves, out_offset=bass.IndirectOffsetOnAxis(ap=s_idx[:, 0:1], axis=0),
                                        in_=y_sb[:, :], in_offset=None, compute_op=ALU.add).then_inc(s["acc_done"], 16)

            gather_next(0, 1)
            n_all = pool.value_load(cum_i[0:1, E:E + 1], min_val=E, max_val=MAX_BLOCKS)
            with pool.Fori(1, n_all) as g:
                gather_next(g, 2 * g)
                scatter(g - 1, 2 * g + 1)
            scatter(n_all - 1, 2 * n_all)


_INS = ["x", "p", "g_mix", "w_in", "w_out_a", "w_out_b", "w_out", "sgu_norm", "sgu_w", "sgu_b", "g_moe", "w_router",
        "b_router", "w1", "b1", "w2", "b2", "g_ple", "w_ple_gate", "w_ple_proj", "g_final"]


def kernel(**inputs):
    import numpy as _np
    import concourse.bacc as _bacc
    from concourse import mybir as _mybir
    from concourse.bass_utils import run_bass_kernel_spmd as _run

    nc = _bacc.Bacc("TRN2", target_bir_lowering=False, num_devices=1)
    arrays, args = {}, []
    for name in _INS:
        a = _np.ascontiguousarray(inputs[name])
        arrays[f"in_{name}_dram"] = a
        args.append(nc.dram_tensor(f"in_{name}_dram", a.shape, _mybir.dt.from_np(a.dtype), kind="ExternalInput").ap())
    shape = inputs["x"].shape
    args.append(nc.dram_tensor("out_0_dram", shape, _mybir.dt.float32, kind="ExternalOutput").ap())
    hybrid_block(nc, *args)
    r = _run(nc, [arrays], core_ids=[0])
    return r.results[0]["out_0_dram"]
```

```python
from contextlib import ExitStack

import concourse.bass as bass
from concourse import mybir

ALU = mybir.AluOpType
ACT = mybir.ActivationFunctionType
F32 = mybir.dt.float32
BF16 = mybir.dt.bfloat16
I32 = mybir.dt.int32
U32 = mybir.dt.uint32
AX_X = mybir.AxisListType.X

P = 128
EPS = 1e-6
SWIGLU_ALPHA = 1.702
SWIGLU_LIMIT = 7.0
TOP_K = 4
SLOTS = 64
SGU_CHUNK = 64


def hybrid_block(nc, x, p, g_mix, w_in, w_out_a, w_out_b, w_out, sgu_norm, sgu_w, sgu_b, g_moe, w_router,
                 b_router, w1, b1, w2, b2, g_ple, w_ple_gate, w_ple_proj, g_final, out, dbg=None):
    T, D = x.shape[1], x.shape[2]
    NT = T // P
    KD = D // P
    WIDTH = w_out_a.shape[1]
    KW = WIDTH // P
    HD = 64
    HP = WIDTH // (2 * HD)
    GROUPS = sgu_w.shape[1]
    E = w_router.shape[2]
    DE = w2.shape[2]
    PLE = p.shape[3]
    KP = PLE // P
    MAX_BLOCKS = (E * (SLOTS - 1) + T * TOP_K) // SLOTS
    NG = MAX_BLOCKS + 1
    ROWS = T + SLOTS
    CH = KD * WIDTH
    assert CH == 4096 and D == 1024 and DE == 1024 and NT == 4 and E == 32

    with ExitStack() as ctx:
        def sb(name, shape, dt=F32):
            return ctx.enter_context(nc.sbuf_tensor(name, shape, dt))

        def sem(name):
            return ctx.enter_context(nc.semaphore(name))

        c_rows = nc.dram_tensor("c_rows", (T, D), F32).ap()
        acc_rows = nc.dram_tensor("acc_rows", (ROWS, D), F32).ap()
        pp_rows = nc.dram_tensor("pp_rows", (T, D), F32).ap()
        acc_halves = acc_rows.rearrange("r (h n) -> (r h) n", h=2)

        arena = sb("arena", [P, 11 * CH])

        def chunk(i, lo=0, n=CH):
            return arena[:, i * CH + lo:i * CH + lo + n]

        w1_buf = arena[:, 0:8 * CH].rearrange("p (e b k n) -> p e b k n", e=2, b=2, k=KD)
        w2lo_buf = arena[:, 8 * CH:10 * CH].rearrange("p (e k n) -> p e k n", e=2, k=4)
        w2hi_buf = chunk(10).rearrange("p (k n) -> p k n", k=4)

        aT = chunk(0).rearrange("p (k t) -> p k t", k=KD)
        gateB = chunk(1).rearrange("p (k t) -> p k t", k=KD)
        gateA = chunk(4).rearrange("p (k t) -> p k t", k=KD)
        qT = chunk(8, 0, 2048).rearrange("p (k t) -> p k t", k=KW)
        uT = chunk(8, 2048, 2048).rearrange("p (k t) -> p k t", k=KW)
        vs = chunk(10, 0, 2048).rearrange("p (t c) -> p t c", t=NT)
        wmT = chunk(10, 2048, 1024).rearrange("p (g t) -> p g t", g=GROUPS)
        wm_raw = chunk(10, 3072, 1024).rearrange("p (g s) -> p g s", g=GROUPS)
        kT = chunk(5, 0, 2048).rearrange("p (k t) -> p k t", k=KW)
        v = chunk(5, 2048, 2048).rearrange("p (t c) -> p t c", t=NT)
        h = chunk(5).rearrange("p (t c) -> p t c", t=NT)
        xs = chunk(9).rearrange("p (t c) -> p t c", t=NT)
        bias_f32 = chunk(1, 0, 3072)
        junk = chunk(1, 3072, 1024)
        oaT, obT, merged = qT, uT, gateA

        ident = sb("ident", [P, P])
        tri = sb("tri", [P, P])
        neg1 = sb("neg1", [P, P])
        ones_b = sb("ones_b", [P, P], BF16)
        upper_b = sb("upper_b", [P, P], BF16)
        xg = sb("xg", [P, 1024])
        xT = sb("xT", [P, KD, SLOTS])
        act_work = sb("act_work", [P, 3 * 512])
        glu, sig, lin = (act_work[:, 512 * i:512 * i + 512].rearrange("p (b n) -> p b n", b=2) for i in range(3))
        out_work = sb("out_work", [P, 2 * 512])
        actT = out_work[:, 0:512].rearrange("p (b c s) -> p b c s", b=2, c=2)
        y_sb = out_work[:, 512:1024]
        bias_sb = sb("bias_sb", [96, 3072], BF16)
        sel_sb = sb("sel_sb", [96, E], BF16)
        sel_cur = sb("sel_cur", [96, 2, SLOTS], BF16)
        g_mix_c = sb("g_mix_c", [P, KD])
        g_ple_c = sb("g_ple_c", [P, KD])
        sgu_g_c = sb("sgu_g_c", [P, KW])
        sgu_b_bc = out_work[:, 0:512].rearrange("p (g t) -> p g t", g=GROUPS // 2)
        b_router_bc = sb("b_router_bc", [P, E])
        w_router_sb = sb("w_router_sb", [P, KD, E])
        small = sb("small", [P, 64])
        bn6 = sb("bn6", [P, NT, 6])
        bn2 = sb("bn2", [P, NT, 2])
        iota_i = sb("iota_i", [P, NG], I32)
        iota_f = sb("iota_f", [P, NG])
        tok1_f = sb("tok1_f", [P, NT])
        pad_c = sb("pad_c", [P, 2])
        pad_i = sb("pad_i", [P, 6], I32)
        tok_idx = sb("tok_idx", [P, NG], I32)
        dst_idx = sb("dst_idx", [P, NG], I32)
        gate_tab = sb("gate_tab", [P, NG])
        cum_i = sb("cum_i", [P, E + 1], I32)
        side_i = sb("side_i", [P, E + 1], I32)
        perm_i = sb("perm_i", [P, E + 1], I32)
        g_idx = sb("g_idx", [SLOTS, 1], I32)
        s_idx = sb("s_idx", [P, 1], I32)
        g_moe_bc = xg
        place_oh = out_work[:, :].rearrange("p (pos e) -> p pos e", e=E)
        place_v = act_work[:, 0:E * E].rearrange("p (pos e) -> p pos e", e=E)
        ATT = (NT + 3 + 2 + 1) * P
        att_e = [chunk(9, 0, ATT), chunk(9, ATT, ATT)]
        att_s = [chunk(9, 2 * ATT, ATT), act_work[:, 0:ATT]]
        cT = out_work[:, :].rearrange("p (k t) -> p k t", k=KD)
        route = chunk(9).rearrange("p (j n) -> p j n", j=NT * TOP_K)
        lg = sb("lg", [P, NT, E])
        top_v = sb("top_v", [P, NT, 8])
        top_i = sb("top_i", [P, NT, 8], U32)
        top_f = sb("top_f", [P, NT, 8])
        onehot = xT[:, :, :].rearrange("p k s -> p (k s)").rearrange("p (t k e) -> p t k e", t=NT, k=TOP_K)
        mask = sb("mask", [P, NT, E])
        mask_b = sb("mask_b", [P, NT, E], BF16)
        gates = sb("gates", [P, NT, TOP_K])
        gsum = sb("gsum", [P, NT])
        grec = sb("grec", [P, NT])
        nmax = sb("nmax", [P, NT])
        n_blk = sb("n_blk", [P, 2, E])
        cum_f = sb("cum_f", [P, E + 1])
        heavy = sb("heavy", [P, 6, E])
        n_heavy = sb("n_heavy", [P, 8])
        base64 = sb("base64", [P, E])
        zeros_e = sb("zeros_e", [P, E])
        posm = sb("posm", [P, NT, E])
        pos = sb("pos", [P, NT * TOP_K])
        pos_i = sb("pos_i", [P, 3, NT * TOP_K], I32)
        pos_f = lg[:, 0, 0:2 * NT * TOP_K].rearrange("p (a j) -> p a j", a=2)
        load_i = pos_i[:, :, :].rearrange("p a j -> p (a j)")[:, 0:E]
        tab_t = xT[:, 0:2, :]

        ps = ctx.enter_context(nc.psum_tensor("ps", [P, 8, 512], F32))

        s = {n: sem(n) for n in (
            "small_in", "g_bc_in", "wm_in", "bias_in", "x_again", "const_dve", "const_pool", "ident_ok",
            "sq_done", "rms_ok", "sqrt_done", "xn_ok", "xT_tr", "aT_act", "aT_dve", "wm_tr", "wmT_ok",
            "unit_done", "evac_act", "evac_dve", "z_done", "tri_done",
            "abs_ok", "ln_ok", "exp_ok", "sp_ok", "sp_masked", "w_ok", "w_masked",
            "ln_stats", "ln_std", "vs_ok", "ob_ok", "ob_tmp", "merged_ok", "oa_ok",
            "h_ok", "h_sq", "h_var", "h_std", "c_ok", "c_tr", "cT_ok", "logit_done", "c_written", "acc_done",
            "top_ok", "gexp_ok", "mask_ok", "rank_done", "route_ok", "table_done", "tables_ok",
            "dve_step", "act_step", "pool_step", "bias_ok",
            "tx_done", "xg_in", "xT_ok", "hA_done", "hB_done", "glu_ok", "sig_ok", "act_ok",
            "tA_done", "actT_ok", "mm2lo_done", "y_done", "y_ok", "y_free", "sel_ok", "moe_step", "tx_turn", "dma_turn", "load_turn",
            "p_in", "p_tr", "pT_ok", "pp_done", "pp_ok", "pp_written", "pp_in", "t_sq", "t_var", "t_std", "t_rec",
            "h_tr", "hT_act", "hT_dve",
            "pg_done", "pg_sig", "h2_ok", "f_sq", "f_var", "f_std", "out_ok", "out_written",
        )}
        w1_in = [sem(f"w1_in_{j}") for j in range(4)]
        w2lo_in = [sem(f"w2lo_in_{j}") for j in range(2)]
        w2hi_in = [sem(f"w2hi_in_{j}") for j in range(2)]
        x_in = [sem(f"x_in_{t}") for t in range(NT)]
        ring_in = {c: sem(f"ring_in_{c}") for c in (2, 3, 6, 7)}

        GROUP_BUF = {"q": 2, "k": 3, "v": 6, "vs": 7, "u": 2, "ga0": 3, "ga1": 6, "gb0": 7, "gb1": 2,
                     "woa": 3, "wob": 2, "wo0": 7, "wo1": 6}
        LOAD_ORDER = ["q", "k", "v", "vs", "u", "ga0", "ga1", "gb0", "gb1", "woa", "wo1", "wo0", "wob"]
        COLS = {"q": 0, "k": 1, "v": 2, "u": 3, "vs": 4, "ga0": 5, "ga1": 6, "gb0": 7, "gb1": 8}
        fill = [(g, j) for g in ("vs", "u", "ga0", "ga1", "gb0", "gb1") for j in range(4)]
        units = [(g, j) for g in ("q", "k", "v") for j in range(4)]
        pe_plan = [("unit", u) for u in units]
        PER = len(fill) // HP // 2
        for hp in range(HP):
            pe_plan.append(("z", hp))
            pe_plan += [("unit", u) for u in fill[2 * PER * hp:2 * PER * hp + PER]]
            pe_plan.append(("tri", hp))
            pe_plan += [("unit", u) for u in fill[2 * PER * hp + PER:2 * PER * (hp + 1)]]
            pe_plan.append(("unit", ("out", hp)))
            if hp == 2:
                pe_plan += [("unit", ("sv", j)) for j in range(GROUPS // 2)]
            if hp == 0:
                pe_plan.append(("ln", 0))
        pe_plan += [("unit", ("woa", j)) for j in range(KD)] + [("unit", ("wob", j)) for j in range(KD)]
        units = [a for k, a in pe_plan if k == "unit"]
        MIX_UNITS = len(units)
        units += [("wo", j) for j in range(2 * NT)]
        ON_ACT = ("q", "v", "vs", "u", "ga0", "ga1", "gb0", "gb1", "out")
        evac_of, counts = {}, {"evac_act": 0, "evac_dve": 0}
        for u in units:
            e = "evac_act" if u[0] in ON_ACT else "evac_dve"
            counts[e] += 1
            evac_of[u] = (e, counts[e])
        unit_no = {u: i + 1 for i, u in enumerate(units)}

        def unit_bank(u):
            return ps[:, 6 + (unit_no[u] - 1) % 2, :]

        last_unit = {g: (g, 3) for g in COLS} | {"woa": ("woa", KD - 1), "wob": ("wob", KD - 1)}
        ring_count = {}
        seen = {c: 0 for c in ring_in}
        prev_in_buf, last_of = {}, {}
        for g in LOAD_ORDER:
            c = GROUP_BUF[g]
            seen[c] += 1
            ring_count[g] = 16 * seen[c]
            prev_in_buf[g] = last_of.get(c)
            last_of[c] = g

        def tr_bank(t):
            return 6 * (t % 2)

        def logit_ps(t):
            return ps[:, 3 if t == NT - 1 else 2, t * E:(t + 1) * E]

        def ring_wait(eng, g):
            eng.wait_ge(ring_in[GROUP_BUF[g]], ring_count[g])

        OFF = {0: 0, 1: 512, 3: 896, 2: 1024}

        w_in_v = w_in[0].rearrange("(k p) n -> p k n", p=P)

        def ring_view(g, k=KD):
            return chunk(GROUP_BUF[g]).rearrange("p (k n) -> p k n", k=k)

        x_v = x[0].rearrange("(t p) d -> p t d", p=P)
        out_v = out[0].rearrange("(t p) d -> p t d", p=P)
        w1_v = w1[0].rearrange("e (k p) n -> p e k n", p=P)
        w2_v = w2[0].rearrange("e (k p) n -> p e k n", p=P)

        wproj = chunk(10, 0, 2048).rearrange("p (k n) -> p k n", k=KP)
        p_sb = chunk(10, 2048, 1024).rearrange("p (t c) -> p t c", t=NT)
        pT = chunk(10, 3072, 1024).rearrange("p (k t) -> p k t", k=KP)
        pp_out = chunk(7).rearrange("p (t n) -> p t n", t=NT)
        wg = w1_buf[:, 0, 0]
        pp = chunk(8).rearrange("p (t n) -> p t n", t=NT)
        gf_bc = chunk(2, 0, 1024)
        hf = chunk(4).rearrange("p (t c) -> p t c", t=NT)
        hT = [chunk(5, 1024 * t, 1024).rearrange("p (k t) -> p k t", k=KD) for t in range(NT)]
        outs_sb = chunk(6).rearrange("p (t c) -> p t c", t=NT)
        sg = [chunk(7, 1024 * i, 1024) for i in range(2)]
        wg_in = [sem(f"wg_in_{n}") for n in range(2)]
        acc_in = [sem(f"acc_in_{t}") for t in range(NT)]

        block = ctx.enter_context(nc.Block())

        @block.sync
        def _(sp):
            for t in range(NT):
                sp.dma_start(xs[:, t, :], x_v[:, t, :]).then_inc(x_in[t], 16)
            with nc.allow_non_contiguous_dma(reason="gains by feature on partitions: 20 kB once"):
                sp.dma_start(g_mix_c[:], g_mix[0].rearrange("(k p) -> p k", p=P)).then_inc(s["small_in"], 16)
                sp.dma_start(sgu_g_c[:], sgu_norm[0].rearrange("(k p) -> p k", p=P)).then_inc(s["small_in"], 16)
                sp.dma_start(g_ple_c[:], g_ple[0].rearrange("(k p) -> p k", p=P)).then_inc(s["small_in"], 16)
            for j in range(GROUPS):
                sp.dma_start(sgu_b_bc[64 * (j % 2):64 * (j % 2) + 64, j // 2, :],
                             sgu_b[0, j:j + 1, :].to_broadcast([64, P])).then_inc(s["small_in"], 16)
            sp.dma_start(b_router_bc[:], b_router[0:1, :].to_broadcast([P, E])).then_inc(s["small_in"], 16)
            sp.dma_start(w_router_sb[:], w_router[0].rearrange("(k p) e -> p k e", p=P)).then_inc(s["small_in"], 16)
            sp.dma_start(wm_raw, sgu_w[0].rearrange("g t s -> t g s")).then_inc(s["wm_in"], 16)

            def load_group(g):
                if prev_in_buf[g]:
                    sp.wait_ge(s["unit_done"], unit_no[last_unit[prev_in_buf[g]]])
                if g in COLS:
                    src = w_in_v[:, :, COLS[g] * WIDTH:(COLS[g] + 1) * WIDTH]
                elif g in ("woa", "wob"):
                    w = w_out_a if g == "woa" else w_out_b
                    src = w[0].rearrange("(k p) n -> p k n", p=P)
                else:
                    n = int(g[2])
                    src = w_out[0].rearrange("(k p) n -> p k n", p=P)[:, 4 * n:4 * n + 4, :]
                dst = ring_view(g, src.shape[1])
                sp.dma_start(dst, src).then_inc(ring_in[GROUP_BUF[g]], 16)

            for g in LOAD_ORDER[:4]:
                load_group(g)
            sp.dma_start(g_moe_bc[:], g_moe[0:1, :].to_broadcast([P, D])).then_inc(s["g_bc_in"], 16)
            for i in range(3):
                sp.dma_start(bias_f32[32 * i:32 * i + 32, 0:2 * DE], b1[0]).then_inc(s["bias_in"], 16)
                sp.dma_start(bias_f32[32 * i:32 * i + 32, 2 * DE:3 * DE], b2[0]).then_inc(s["bias_in"], 16)
            for g in LOAD_ORDER[4:-1]:
                load_group(g)
            sp.wait_ge(s["unit_done"], unit_no[("out", HP - 1)])
            for t in range(NT):
                sp.dma_start(xs[:, t, :], x_v[:, t, :]).then_inc(s["x_again"], 16)
            load_group(LOAD_ORDER[-1])
            sp.wait_ge(s["ob_ok"], GROUPS // 2)
            sp.dma_start(wproj, w_ple_proj[0].rearrange("(k p) n -> p k n", p=P)).then_inc(s["p_in"], 16)
            sp.dma_start(p_sb, p[0, 0].rearrange("(t p) d -> p t d", p=P)).then_inc(s["p_in"], 16)

            def arrival(j, n):
                if j < 8:
                    return w1_in[j % 4], 16 * (2 * n + j // 4 + 1)
                return (w2lo_in if j < 10 else w2hi_in)[j % 2], 16 * (n + 1)

            def load_piece(j, e, side):
                k = slice(2 * (j % 4), 2 * (j % 4) + 2)
                if j < 8:
                    dst = w1_buf[:, side, j // 4, k, :]
                    src = w1_v[:, e, k, DE * (j // 4):DE * (j // 4 + 1)]
                else:
                    h2 = slice(2 * (j % 2), 2 * (j % 2) + 2)
                    dst = w2lo_buf[:, side, h2, :] if j < 10 else w2hi_buf[:, h2, :]
                    src = w2_v[:, e, 2 * (j - 8):2 * (j - 8) + 2, :]
                sp.dma_start(dst, src).then_inc(arrival(j, 0)[0], 16)

            def load_first(js, e):
                for i, j in enumerate(js):
                    if i >= 3:
                        sp.wait_ge(*arrival(js[i - 3], e))
                    load_piece(j, e, e)

            sp.wait_ge(s["merged_ok"], KD)
            sp.wait_ge(s["unit_done"], unit_no[("wob", KD - 1)])
            load_first(range(10), 0)
            sp.wait_ge(s["unit_done"], len(units))
            sp.wait_ge(s["acc_done"], 16 * (NT + 1))
            sp.wait_ge(s["c_ok"], NT)
            load_first(range(6), 1)
            sp.wait_ge(s["pp_ok"], NT)
            sp.dma_start(pp_rows.rearrange("(t p) n -> p t n", p=P), pp_out).then_inc(s["pp_written"], 16)
            sp.wait_ge(s["pp_written"], 16)
            sp.wait_ge(s["tables_ok"], 1)
            sp.wait_ge(s["xg_in"], 16)
            load_first(range(6, 10), 1)
            first_expert = sp.value_load(perm_i[0:1, 0:1], min_val=0, max_val=1)
            for j in (10, 11):
                load_piece(j, first_expert, None)

            with sp.Fori(2, E) as pos_:
                two_back = sp.value_load(cum_i[0:1, bass.ds(pos_ - 1, 1)], min_val=1, max_val=MAX_BLOCKS)
                last_expert = sp.value_load(perm_i[0:1, bass.ds(pos_ - 1, 1)], min_val=0, max_val=E - 1)
                expert = sp.value_load(perm_i[0:1, bass.ds(pos_, 1)], min_val=0, max_val=E - 1)
                side = sp.value_load(side_i[0:1, bass.ds(pos_, 1)], min_val=0, max_val=1)
                AT = 4
                order = [(j, pos_) for j in range(AT)] + [(j, pos_ - 1) for j in (10, 11)] + \
                    [(j, pos_) for j in range(AT, 10)]
                seq = [(j, p_ - 1) for j, p_ in order[-3:]] + order
                for i, (j, p_) in enumerate(order):
                    if j == 0:
                        sp.wait_ge(s["hA_done"], two_back)
                    elif j == 4:
                        sp.wait_ge(s["hB_done"], two_back)
                    elif j == 8:
                        sp.wait_ge(s["mm2lo_done"], two_back)
                    elif j == 10:
                        sp.wait_ge(s["y_done"], two_back)
                    sp.wait_ge(*arrival(*seq[i]))
                    sp.sem_inc(s["load_turn"], 1)
                    load_piece(j, expert if j < 10 else last_expert, side)
            last_expert = sp.value_load(perm_i[0:1, E - 1:E], min_val=0, max_val=E - 1)
            one_back = sp.value_load(cum_i[0:1, E - 1:E], min_val=1, max_val=MAX_BLOCKS)
            sp.wait_ge(s["y_done"], one_back)
            sp.sem_inc(s["load_turn"], 1)
            for j in (10, 11):
                load_piece(j, last_expert, None)
            nb = sp.value_load(cum_i[0:1, E:E + 1], min_val=1, max_val=MAX_BLOCKS)
            wg_v = w_ple_gate[0].rearrange("(k p) n -> p k n", p=P)
            sp.wait_ge(s["hA_done"], nb)
            sp.dma_start(wg[:, :, 0:512], wg_v[:, :, 0:512]).then_inc(wg_in[0], 16)
            sp.wait_ge(s["acc_done"], 16 * (NT + 1) + nb * 16)
            for t in range(NT):
                sp.dma_start(hf[:, t, :], acc_rows[t * P:(t + 1) * P, :]).then_inc(acc_in[t], 16)
                if t == 1:
                    sp.dma_start(wg[:, :, 512:], wg_v[:, :, 512:]).then_inc(wg_in[1], 16)
            sp.dma_start(gf_bc, g_final.rearrange("(a d) -> a d", a=1).to_broadcast([P, D])).then_inc(s["pp_in"], 16)
            sp.dma_start(pp, pp_rows.rearrange("(t p) n -> p t n", p=P)).then_inc(s["pp_in"], 16)
            for t in range(NT):
                for n in range(2):
                    sl = slice(512 * n, 512 * n + 512)
                    sp.wait_ge(s["out_ok"], 2 * t + n + 1)
                    sp.dma_start(out_v[:, t, sl], outs_sb[:, t, sl]).then_inc(s["out_written"], 16)
            sp.wait_ge(s["out_written"], 32 * NT)

        @block.tensor
        def _(pe):
            def wait_unit_bank(u):
                n = unit_no[u]
                if n > 2:
                    e, c = evac_of[units[n - 3]]
                    pe.wait_ge(s[e], c)

            pe.wait_ge(s["ident_ok"], 1)
            for t in range(NT):
                pe.wait_ge(s["xn_ok"], t + 1)
                for k in range(KD):
                    last = pe.transpose(ps[:, k, t * P:(t + 1) * P], xs[:, t, k * P:(k + 1) * P], ident[:, :])
            last.then_inc(s["xT_tr"], 1)
            pe.wait_ge(s["aT_act"], KD // 2)
            pe.wait_ge(s["aT_dve"], KD // 2)
            pe.wait_ge(s["wm_in"], 16)
            for g in range(GROUPS):
                last = pe.transpose(ps[:, g // 4, (g % 4) * P:(g % 4 + 1) * P], wm_raw[:, g, :], ident[:, :])
            last.then_inc(s["wm_tr"], 1)

            def product_T(u, w, j, rhs, nk):
                for k in range(nk):
                    last = pe.matmul(unit_bank(u), w[:, k, j * P:(j + 1) * P], rhs[:, k, :],
                                     start=(k == 0), stop=(k == nk - 1))
                return last

            def unit(u):
                g, j = u
                wait_unit_bank(u)
                if g in ("q", "k", "u", "ga0", "ga1", "gb0", "gb1"):
                    if j == 0:
                        ring_wait(pe, g)
                    last = product_T(u, ring_view(g), j, aT, KD)
                elif g in ("v", "vs"):
                    if j == 0:
                        ring_wait(pe, g)
                    w = ring_view(g)
                    for k in range(KD):
                        last = pe.matmul(unit_bank(u), aT[:, k, j * P:(j + 1) * P], w[:, k, :],
                                         start=(k == 0), stop=(k == KD - 1))
                elif g == "out":
                    pe.wait_ge(s["w_masked"], 2 * (j + 1))
                    for t in range(NT):
                        for i in range(2):
                            last = pe.matmul(unit_bank(u)[HD * i:HD * i + HD, t * P:],
                                             v[:, t, (2 * j + i) * HD:(2 * j + i + 1) * HD],
                                             att_e[i][:, OFF[t]:OFF[t] + (NT - t) * P],
                                             start=(t == 0), stop=(t == NT - 1), skip_group_check=True)
                elif g == "sv":
                    pe.wait_ge(s["vs_ok"], NT)
                    pe.wait_ge(s["wmT_ok"], 1)
                    for t in range(NT):
                        for i in range(2):
                            last = pe.matmul(unit_bank(u)[64 * i:64 * i + 64, t * P:(t + 1) * P],
                                             vs[:, t, (2 * j + i) * 64:(2 * j + i + 1) * 64],
                                             wmT[:, 2 * j + i, :], start=True, stop=True, skip_group_check=True)
                elif g == "woa":
                    if j == 0:
                        ring_wait(pe, g)
                        e, c = evac_of[("out", HP - 1)]
                        pe.wait_ge(s[e], c)
                    last = product_T(u, ring_view(g, KW), j, oaT, KW)
                elif g == "wob":
                    if j == 0:
                        ring_wait(pe, g)
                        pe.wait_ge(s["ob_ok"], GROUPS // 2)
                    last = product_T(u, ring_view(g, KW), j, obT, KW)
                else:
                    t, n = j // 2, j % 2
                    if j == 0:
                        ring_wait(pe, "wo0")
                        ring_wait(pe, "wo1")
                        pe.wait_ge(s["merged_ok"], KD)
                    for k in range(KD):
                        last = pe.matmul(unit_bank(u), merged[:, k, t * P:(t + 1) * P],
                                         ring_view(f"wo{k // 4}", 4)[:, k % 4, n * 512:(n + 1) * 512],
                                         start=(k == 0), stop=(k == KD - 1))
                last.then_inc(s["unit_done"], 1)

            for kind, a in pe_plan:
                if kind == "unit":
                    unit(a)
                elif kind == "z":
                    e, c = evac_of[("q", a)]
                    pe.wait_ge(s[e], c)
                    e, c = evac_of[("k", a)]
                    pe.wait_ge(s[e], c)
                    if a == 0:
                        pe.wait_ge(s["wmT_ok"], 1)
                    else:
                        pe.wait_ge(s["w_ok"], 2 * a)
                    for t in (0, 1, 3, 2):
                        for i in range(2):
                            z = ps[:, 3 * i:3 * i + 3, :].rearrange("p b n -> p (b n)")
                            last = pe.matmul(z[:, OFF[t]:OFF[t] + (NT - t) * P],
                                             kT[HD * i:HD * i + HD, a, t * P:(t + 1) * P],
                                             qT[HD * i:HD * i + HD, a, t * P:],
                                             start=(t != 3), stop=False, skip_group_check=True)
                    last.then_inc(s["z_done"], 1)
                elif kind == "tri":
                    for i in range(2):
                        pe.wait_ge(s["sp_masked"], 2 * a + i + 1)
                        z = ps[:, 3 * i:3 * i + 3, :].rearrange("p b n -> p (b n)")
                        sp_ = att_s[i]
                        for t in range(NT):
                            for t2 in range(t, NT):
                                n = (NT - t2) * P
                                end = OFF[t] + (NT - t) * P
                                last = pe.matmul(z[:, end - n:end], (tri if t2 == t else neg1)[:, :],
                                                 sp_[:, OFF[t2]:OFF[t2] + n], start=False, stop=(t2 == NT - 1),
                                                 skip_group_check=True)
                        last.then_inc(s["tri_done"], 1)

            def c_transposes(t):
                pe.wait_ge(s["c_ok"], t + 1)
                for k in range(KD):
                    last = pe.transpose(ps[:, k // 4, (k % 4) * P:(k % 4 + 1) * P], xs[:, t, k * P:(k + 1) * P],
                                        ident[:, :])
                last.then_inc(s["c_tr"], 1)

            def logits(t):
                pe.wait_ge(s["cT_ok"], t + 1)
                for k in range(KD):
                    last = pe.matmul(logit_ps(t), cT[:, k, :], w_router_sb[:, k, :],
                                     start=(k == 0), stop=(k == KD - 1))
                last.then_inc(s["logit_done"], 1)

            wo = [("wo", j) for j in range(2 * NT)]
            for u in wo[0:4]:
                unit(u)
            c_transposes(0)
            unit(wo[4])
            logits(0)
            c_transposes(1)
            unit(wo[5])
            logits(1)
            unit(wo[6])
            c_transposes(2)
            unit(wo[7])
            logits(2)
            c_transposes(3)
            pe.wait_ge(s["p_in"], 32)
            pe.wait_ge(s["h_ok"], 2 * NT)
            for k in range(KP):
                for t in range(NT):
                    last = pe.transpose(ps[:, 6 + k, t * P:(t + 1) * P], p_sb[:, t, k * P:(k + 1) * P], ident[:, :])
            last.then_inc(s["p_tr"], 1)
            logits(3)

            pe.wait_ge(s["mask_ok"], 2)
            for t in range(NT):
                for t2 in range(t + 1):
                    pe.matmul(ps[:, 2, t * E:(t + 1) * E], (upper_b if t2 == t else ones_b)[:, :], mask_b[:, t2, :],
                              start=(t2 == 0), stop=(t2 == t))
            for t in range(NT):
                last = pe.matmul(ps[:, 2, NT * E:(NT + 1) * E], ones_b[:, :], mask_b[:, t, :],
                                 start=(t == 0), stop=(t == NT - 1))
            last.then_inc(s["rank_done"], 1)
            pe.wait_ge(s["pT_ok"], 1)
            for t in range(NT):
                if t > 1:
                    pe.wait_ge(s["pp_ok"], t - 1)
                for n in range(2):
                    for k in range(KP):
                        last = pe.matmul(ps[:, 4 + 2 * (t % 2) + n, :], pT[:, k, t * P:(t + 1) * P],
                                         wproj[:, k, n * 512:(n + 1) * 512], start=(k == 0), stop=(k == KP - 1))
                last.then_inc(s["pp_done"], 1)
            for j in range(NT * TOP_K):
                if j % TOP_K == 0:
                    pe.wait_ge(s["route_ok"], j // TOP_K + 1)
                last = pe.matmul(ps[:, 0, 0:2 * NG], route[:, j, 0:P], route[:, j, P:P + 2 * NG],
                                 start=(j == 0), stop=(j == NT * TOP_K - 1))
            last.then_inc(s["table_done"], 1)

            def x_transposes():
                for k in range(KD):
                    last = pe.transpose(ps[:, 3, k * SLOTS:(k + 1) * SLOTS], xg[0:SLOTS, k * P:(k + 1) * P],
                                        ident[0:SLOTS, 0:SLOTS])
                last.then_inc(s["tx_done"], 1)

            def act_transposes(g, b):
                pe.wait_ge(s["act_ok"], 2 * g + b + 1)
                for c in range(2):
                    last = pe.transpose(ps[:, 4 + b, c * P:(c + 1) * P], glu[:, b, c * P:(c + 1) * P], ident[:, :])
                last.then_inc(s["tA_done"], 1)

            pe.wait_ge(s["xg_in"], 16)
            x_transposes()

            def experts_block(g, e, n_load, side):
                pe.wait_ge(s["sel_ok"], e + 1)
                pe.wait_ge(s["xT_ok"], g + 1)
                for b in range(2):
                    for half in range(2):
                        col = DE * b + 512 * half
                        pe.matmul(ps[64 * half:64 * half + 64, b, :], sel_cur[:, side, :], bias_sb[:, col:col + 512],
                                  start=True, stop=False, skip_group_check=True)
                    for k in range(KD):
                        if b == 1 and k == 4:
                            act_transposes(g, 0)
                        if k % 2 == 0:
                            pe.wait_ge(w1_in[k // 2], 32 * n_load + 16 * (b + 1))
                        for half in range(2):
                            last = pe.matmul(ps[64 * half:64 * half + 64, b, :], xT[:, k, :],
                                             w1_buf[:, side, b, k, 512 * half:512 * half + 512],
                                             start=False, stop=(k == KD - 1), skip_group_check=True)
                    last.then_inc(s["hA_done" if b == 0 else "hB_done"], 1)
                pe.wait_ge(s["xg_in"], 16 * g + 32)
                pe.sem_inc(s["tx_turn"], 1)
                x_transposes()
                pe.wait_ge(s["y_ok"], g + 1)
                for half in range(2):
                    col = 2 * DE + 512 * half
                    pe.matmul(ps[64 * half:64 * half + 64, 2, :], sel_cur[:, side, :],
                              bias_sb[:, col:col + 512], start=True, stop=False, skip_group_check=True)
                for b in range(2):
                    pe.wait_ge(s["actT_ok"], 2 * g + b + 1)
                    w2 = (w2lo_buf[:, side], w2hi_buf)[b]
                    for k in range(4):
                        if b == 0 and k == 2:
                            act_transposes(g, 1)
                        if k % 2 == 0:
                            if b == 0:
                                pe.wait_ge(w2lo_in[k // 2], 16 * n_load + 16)
                            else:
                                pe.wait_ge(w2hi_in[k // 2], 16 * e + 16)
                        for half in range(2):
                            last = pe.matmul(ps[64 * half:64 * half + 64, 2, :],
                                             actT[:, b, k % 2, 64 * (k // 2):64 * (k // 2) + 64],
                                             w2[:, k, 512 * half:512 * half + 512],
                                             start=False, stop=(b == 1 and k == 3), skip_group_check=True)
                    last.then_inc(s["mm2lo_done" if b == 0 else "y_done"], 1)

            with pe.Fori(0, E) as e:
                first = pe.value_load(cum_i[0:1, bass.ds(e, 1)], min_val=0, max_val=MAX_BLOCKS)
                end = pe.value_load(cum_i[0:1, bass.ds(e + 1, 1)], min_val=1, max_val=MAX_BLOCKS)
                n_load = pe.value_load(load_i[0:1, bass.ds(e, 1)], min_val=0, max_val=E - 1)
                side = pe.value_load(side_i[0:1, bass.ds(e, 1)], min_val=0, max_val=1)
                with pe.If(side == 0):
                    with pe.Fori(first, end) as g:
                        experts_block(g, e, n_load, 0)
                with pe.Else():
                    with pe.Fori(first, end) as g:
                        experts_block(g, e, n_load, 1)

            def h_transposes(t):
                pe.wait_ge(acc_in[t], 16)
                if t > 1:
                    pe.wait_ge(s["hT_act"], t - 1)
                    pe.wait_ge(s["hT_dve"], t - 1)
                for k in range(KD):
                    last = pe.transpose(ps[:, tr_bank(t) + k // 4, (k % 4) * P:(k % 4 + 1) * P],
                                        hf[:, t, k * P:(k + 1) * P], ident[:, :])
                last.then_inc(s["h_tr"], 1)

            def gate(t):
                pe.wait_ge(s["hT_act"], t + 1)
                pe.wait_ge(s["hT_dve"], t + 1)
                for n in range(2):
                    if t == 0:
                        pe.wait_ge(wg_in[n], 16)
                    if t:
                        pe.wait_ge(s["pg_sig"], 2 * (t - 1) + n + 1)
                    for k in range(KD):
                        last = pe.matmul(ps[:, 2 + n, :], hT[t][:, k, :], wg[:, k, n * 512:(n + 1) * 512],
                                         start=(k == 0), stop=(k == KD - 1))
                    last.then_inc(s["pg_done"], 1)

            h_transposes(0)
            for t in range(NT):
                if t + 1 < NT:
                    h_transposes(t + 1)
                gate(t)

        @block.scalar
        def _(act):
            for t in range(NT):
                act.wait_ge(x_in[t], 16)
                act.activation(junk, xs[:, t, :], ACT.Square, accum_out=small[:, t:t + 1]).then_inc(s["sq_done"], 1)
                act.wait_ge(s["rms_ok"], t + 1)
                act.activation(small[:, 4 + t:5 + t], small[:, 4 + t:5 + t], ACT.Sqrt).then_inc(s["sqrt_done"], 1)
            act.wait_ge(s["small_in"], 16 * (5 + GROUPS))
            act.wait_ge(s["xT_tr"], 1)
            for k in range(0, KD, 2):
                act.activation(aT[:, k, :], ps[:, k, :], ACT.Copy, scale=g_mix_c[:, k:k + 1]).then_inc(s["aT_act"], 1)

            def evac(u):
                g, j = u
                act.wait_ge(s["unit_done"], unit_no[u])
                bank = unit_bank(u)
                if g == "q":
                    ins = act.activation(qT[:, j, :], bank, ACT.Copy, scale=float(HD) ** -0.5)
                elif g == "v":
                    ins = act.activation(v[:, j, :], bank, ACT.Copy)
                elif g == "out":
                    ins = act.activation(oaT[:, j, :], bank, ACT.Copy)
                elif g == "vs":
                    ins = act.activation(vs[:, j, :], bank, ACT.Gelu_apprx_tanh)
                elif g == "u":
                    ins = act.activation(uT[:, j, :], bank, ACT.Gelu_apprx_tanh)
                else:
                    if g == "gb0" and j == 0:
                        act.wait_ge(s["bias_ok"], 1)
                    dst = gateA if g[1] == "a" else gateB
                    ins = act.activation(dst[:, 4 * int(g[2]) + j, :], bank, ACT.Exp, scale=-1.0)
                ins.then_inc(s["evac_act"], 1)

            for kind, a in pe_plan:
                if kind == "unit" and a[0] in ON_ACT:
                    evac(a)
                elif kind == "z":
                    for i in range(2):
                        z = ps[:, 3 * i:3 * i + 3, :].rearrange("p b n -> p (b n)")
                        if i == 0:
                            act.wait_ge(s["z_done"], a + 1)
                            if a:
                                act.wait_ge(s["unit_done"], unit_no[("out", a - 1)])
                        act.activation(att_e[i], z[:, 0:ATT], ACT.Abs).then_inc(s["abs_ok"], 1)
                        act.wait_ge(s["abs_ok"], 2 * a + i + 1)
                        act.activation(att_e[i], att_e[i], ACT.Exp, scale=-1.0).then_inc(s["exp_ok"], 1)
                        act.wait_ge(s["exp_ok"], 2 * a + i + 1)
                        act.activation(att_e[i], att_e[i], ACT.Ln, bias=1.0).then_inc(s["ln_ok"], 1)
                elif kind == "tri":
                    for i in range(2):
                        z = ps[:, 3 * i:3 * i + 3, :].rearrange("p b n -> p (b n)")
                        act.wait_ge(s["tri_done"], 2 * a + i + 1)
                        act.activation(att_e[i], z[:, 0:ATT], ACT.Exp).then_inc(s["w_ok"], 1)
                elif kind == "ln":
                    act.wait_ge(s["ln_stats"], 1)
                    act.activation(small[:, 12:16], small[:, 8:12], ACT.Sqrt).then_inc(s["ln_std"], 1)

            def square_h(t):
                act.wait_ge(s["h_ok"], 2 * (t + 1))
                act.activation(ps[:, 4:6, :].rearrange("p b n -> p (b n)"), h[:, t, :], ACT.Square,
                               accum_out=small[:, 20 + t:21 + t]).then_inc(s["h_sq"], 1)
                act.wait_ge(s["h_var"], t + 1)
                act.activation(small[:, 28 + t:29 + t], small[:, 24 + t:25 + t], ACT.Sqrt).then_inc(s["h_std"], 1)

            def cT_copy(t):
                act.wait_ge(s["c_tr"], t + 1)
                act.activation(cT[:, :, :].rearrange("p k t -> p (k t)"), ps[:, 0:2, :].rearrange("p b n -> p (b n)"),
                               ACT.Copy).then_inc(s["cT_ok"], 1)

            square_h(0)
            square_h(1)
            cT_copy(0)
            cT_copy(1)
            square_h(2)
            cT_copy(2)
            square_h(3)
            cT_copy(3)
            act.wait_ge(s["p_tr"], 1)
            act.activation(pT[:, :, :].rearrange("p k t -> p (k t)"), ps[:, 6:8, :].rearrange("p b n -> p (b n)"),
                           ACT.Copy).then_inc(s["pT_ok"], 1)
            for t in range(NT):
                if t in (0, NT - 1):
                    act.wait_ge(s["top_ok"], 1 + t // (NT - 1))
                last = act.activation(gates[:, t, :], top_v[:, t, 0:TOP_K], ACT.Exp, bias=nmax[:, t:t + 1],
                                      accum_out=gsum[:, t:t + 1])
            last.then_inc(s["gexp_ok"], 1)
            for t in range(NT):
                act.wait_ge(s["pp_done"], t + 1)
                act.activation(pp_out[:, t, :], ps[:, 4 + 2 * (t % 2):6 + 2 * (t % 2), :].rearrange("p b n -> p (b n)"),
                               ACT.Copy).then_inc(s["pp_ok"], 1)

            def x_copy():
                act.activation(xT[:, :, :].rearrange("p k s -> p (k s)"), ps[:, 3, :], ACT.Copy).then_inc(s["xT_ok"], 1)

            act.wait_ge(s["tx_done"], 1)
            x_copy()
            n_all = act.value_load(cum_i[0:1, E:E + 1], min_val=1, max_val=MAX_BLOCKS)
            with act.Fori(0, n_all) as g:
                for b in range(2):
                    act.wait_ge(s["glu_ok"], 2 * g + b + 1)
                    act.activation(sig[:, b, :], glu[:, b, :], ACT.Sigmoid, scale=SWIGLU_ALPHA).then_inc(s["sig_ok"], 1)
                    if b == 1:
                        act.wait_ge(s["tx_done"], g + 2)
                        x_copy()
                    act.wait_ge(s["tA_done"], 2 * g + b + 1)
                    act.activation(actT[:, b, :, :].rearrange("p c s -> p (c s)"), ps[:, 4 + b, 0:2 * P],
                                   ACT.Copy).then_inc(s["actT_ok"], 1)

            def hT_copy(t):
                act.wait_ge(s["h_tr"], t + 1)
                for k in range(KD // 2):
                    last = act.activation(hT[t][:, k, :], ps[:, tr_bank(t), k * P:(k + 1) * P], ACT.Copy,
                                          scale=g_ple_c[:, k:k + 1])
                last.then_inc(s["hT_act"], 1)

            hT_copy(0)
            hT_copy(1)
            for t in range(NT):
                act.wait_ge(acc_in[t], 16)
                if t:
                    act.wait_ge(s["t_sq"], t)
                act.activation(ps[:, 4:6, :].rearrange("p b n -> p (b n)"), hf[:, t, :], ACT.Square,
                               accum_out=small[:, 32 + t:33 + t]).then_inc(s["t_sq"], 1)
            act.wait_ge(s["t_var"], 1)
            act.activation(small[:, 40:40 + NT], small[:, 36:36 + NT], ACT.Sqrt).then_inc(s["t_std"], 1)
            act.wait_ge(s["t_rec"], 1)
            for t in range(NT):
                for n in range(2):
                    act.wait_ge(s["pg_done"], 2 * t + n + 1)
                    act.activation(sg[t % 2][:, 512 * n:512 * n + 512], ps[:, 2 + n, :], ACT.Sigmoid,
                                   scale=small[:, 32 + t:33 + t]).then_inc(s["pg_sig"], 1)
                    if n == 0 and t + 2 < NT:
                        hT_copy(t + 2)
                if t == NT - 1:
                    act.activation(small[:, 56:57], small[:, 36:37], ACT.Sqrt)
                for n in range(2):
                    act.wait_ge(s["h2_ok"], 2 * t + n + 1)
                    act.activation(ps[:, 4 + n, :], hf[:, t, 512 * n:512 * n + 512], ACT.Square,
                                   accum_out=small[:, 44 + 2 * n:45 + 2 * n]).then_inc(s["f_sq"], 1)
                act.wait_ge(s["f_var"], t + 1)
                act.activation(small[:, 52 + t:53 + t], small[:, 48 + t:49 + t], ACT.Sqrt).then_inc(s["f_std"], 1)

        @block.vector
        def _(dve):
            done = [0]

            def link(ins):
                done[0] += 1
                ins.then_inc(s["dve_step"], 1)
                dve.wait_ge(s["dve_step"], done[0])

            link(dve.memset(zeros_e[:], 0.0))
            for t in range(NT):
                dve.wait_ge(s["sq_done"], t + 1)
                dve.tensor_scalar(small[:, 4 + t:5 + t], small[:, t:t + 1], 1.0 / D, EPS, ALU.mult,
                                  ALU.add).then_inc(s["rms_ok"], 1)
                dve.wait_ge(s["sqrt_done"], t + 1)
                link(dve.reciprocal(small[:, 16 + t:17 + t], small[:, 4 + t:5 + t]))
                dve.tensor_scalar(xs[:, t, :], xs[:, t, :], small[:, 16 + t:17 + t], None,
                                  ALU.mult).then_inc(s["xn_ok"], 1)
            dve.wait_ge(s["small_in"], 16 * (5 + GROUPS))
            dve.wait_ge(s["xT_tr"], 1)
            for k in range(1, KD, 2):
                dve.tensor_scalar(aT[:, k, :], ps[:, k, :], g_mix_c[:, k:k + 1], None, ALU.mult).then_inc(s["aT_dve"], 1)
            dve.wait_ge(s["wm_tr"], 1)
            link(dve.tensor_copy(wmT[:, :, :].rearrange("p g t -> p (g t)"),
                                 ps[:, 0:2, :].rearrange("p b n -> p (b n)")))
            dve.memset(wmT[SGU_CHUNK:P, :, 0:SGU_CHUNK], 0.0).then_inc(s["wmT_ok"], 1)

            def evac(u):
                g, j = u
                dve.wait_ge(s["unit_done"], unit_no[u])
                bank = unit_bank(u)
                if g == "k":
                    dve.tensor_copy(kT[:, j, :], bank).then_inc(s["evac_dve"], 1)
                elif g == "sv":
                    b3 = bank.rearrange("p (t n) -> p t n", t=NT)
                    bias = sgu_b_bc[:, j:j + 1, :].to_broadcast([P, NT, P])
                    link(dve.scalar_tensor_tensor(out=b3, in0=b3, scalar=sgu_g_c[:, j:j + 1], in1=bias,
                                                  op0=ALU.mult, op1=ALU.add))
                    e, c = evac_of[("u", j)]
                    dve.wait_ge(s[e], c)
                    link(dve.tensor_tensor(obT[:, j, :], bank, uT[:, j, :], ALU.mult))
                    dve.sem_inc(s["ob_ok"], 1)
                    dve.sem_inc(s["evac_dve"], 1)
                elif g in ("woa", "wob"):
                    gt = gateA if g == "woa" else gateB
                    link(dve.tensor_tensor(gt[:, j, :], gt[:, j, :], bank, ALU.mult))
                    dve.sem_inc(s["evac_dve"], 1)
                    if g == "wob":
                        dve.tensor_tensor(merged[:, j, :], gateA[:, j, :], gateB[:, j, :],
                                          ALU.add).then_inc(s["merged_ok"], 1)

            def sigmoid(u):
                g, j = u
                e, c = evac_of[u]
                dve.wait_ge(s[e], c)
                gt = (gateA if g[1] == "a" else gateB)[:, 4 * int(g[2]) + j, :]
                link(dve.tensor_scalar(gt, gt, 1.0, None, ALU.add))
                link(dve.reciprocal(gt, gt))

            for kind, a in pe_plan:
                if kind == "unit" and a[0] not in ON_ACT:
                    evac(a)
                elif kind == "unit" and a[0] in ("ga0", "ga1", "gb0", "gb1"):
                    sigmoid(a)
                elif kind == "unit" and a == ("vs", 3):
                    dve.wait_ge(s["evac_act"], evac_of[a][1])
                    for t in range(NT):
                        link(dve.bn_stats(bn6[:, t, :], vs[:, t, :]))
                        link(dve.bn_aggr(bn2[:, t, :], bn6[:, t, :]))
                    dve.tensor_scalar(small[:, 8:12], bn2[:, :, 1], EPS, None, ALU.add).then_inc(s["ln_stats"], 1)
                elif kind == "ln":
                    dve.wait_ge(s["ln_std"], 1)
                    link(dve.reciprocal(small[:, 56:60], small[:, 12:16]))
                    for t in range(NT):
                        dve.tensor_scalar(vs[:, t, :], vs[:, t, :], bn2[:, t, 0:1], small[:, 56 + t:57 + t],
                                          ALU.subtract, ALU.mult).then_inc(s["vs_ok"], 1)
                elif kind == "z":
                    zs = [ps[:, 3 * i:3 * i + 3, :].rearrange("p b n -> p (b n)")[:, 0:ATT] for i in range(2)]
                    for i in range(2):
                        dve.wait_ge(s["ln_ok"], 2 * a + i + 1)
                        dve.scalar_tensor_tensor(out=att_s[i], in0=zs[i], scalar=0.0, in1=att_e[i],
                                                 op0=ALU.max, op1=ALU.add).then_inc(s["sp_ok"], 1)

            dve.wait_ge(s["x_again"], 16 * NT)
            dve.wait_ge(s["g_bc_in"], 16)
            for t in range(NT):
                for n in range(2):
                    u = ("wo", 2 * t + n)
                    dve.wait_ge(s["unit_done"], unit_no[u])
                    sl = slice(n * 512, (n + 1) * 512)
                    link(dve.tensor_tensor(h[:, t, sl], unit_bank(u), xs[:, t, sl], ALU.add))
                    dve.sem_inc(s["evac_dve"], 1)
                    dve.sem_inc(s["h_ok"], 1)
                dve.wait_ge(s["h_sq"], t + 1)
                dve.tensor_scalar(small[:, 24 + t:25 + t], small[:, 20 + t:21 + t], 1.0 / D, EPS, ALU.mult,
                                  ALU.add).then_inc(s["h_var"], 1)
                dve.wait_ge(s["h_std"], t + 1)
                link(dve.reciprocal(small[:, 60 + t % 2:61 + t % 2], small[:, 28 + t:29 + t]))
                dve.scalar_tensor_tensor(out=xs[:, t, :], in0=h[:, t, :], scalar=small[:, 60 + t % 2:61 + t % 2],
                                         in1=g_moe_bc[:, :], op0=ALU.mult, op1=ALU.mult).then_inc(s["c_ok"], 1)

            dve.wait_ge(s["const_pool"], 1)
            link(dve.tensor_copy(iota_f[:, :], iota_i[:, :]))
            for ts in (range(NT - 1), range(NT - 1, NT)):
                sl = slice(ts[0], ts[-1] + 1)
                dve.wait_ge(s["logit_done"], ts[-1] + 1)
                for t in ts:
                    last = dve.tensor_tensor(lg[:, t, :], logit_ps(t), b_router_bc[:, :], ALU.add)
                link(last)
                for t in ts:
                    last = dve.max(top_v[:, t, :], lg[:, t, :])
                link(last)
                dve.tensor_scalar(nmax[:, sl], top_v[:, sl, 0], -1.0, None, ALU.mult).then_inc(s["top_ok"], 1)
                for t in ts:
                    last = dve.max_index(top_i[:, t, :], top_v[:, t, :], lg[:, t, :])
                link(last)
                link(dve.tensor_copy(top_f[:, sl, :], top_i[:, sl, :]))
                for t in ts:
                    last = dve.tensor_tensor(onehot[:, t, :, :],
                                             top_f[:, t, 0:TOP_K].unsqueeze(2).to_broadcast([P, TOP_K, E]),
                                             iota_f[:, 0:E].unsqueeze(1).to_broadcast([P, TOP_K, E]), ALU.is_equal)
                link(last)
                for t in ts:
                    last = dve.tensor_reduce(mask[:, t, :], onehot[:, t, :, :].rearrange("p k e -> p e k"), AX_X,
                                             ALU.add)
                link(last)
                dve.tensor_copy(mask_b[:, sl, :], mask[:, sl, :]).then_inc(s["mask_ok"], 1)
            dve.wait_ge(s["gexp_ok"], 1)
            link(dve.reciprocal(grec[:, :], gsum[:, :]))
            link(dve.tensor_tensor(gates[:, :, :], gates[:, :, :], grec[:, :].unsqueeze(2).to_broadcast([P, NT, TOP_K]),
                                   ALU.mult))
            dve.wait_ge(s["rank_done"], 1)
            cnt = ps[:, 2, NT * E:(NT + 1) * E]
            link(dve.tensor_scalar(n_blk[:, 1, :], cnt, float(SLOTS), 1.0, ALU.is_gt, ALU.add))
            for j in range(2, T // SLOTS):
                link(dve.scalar_tensor_tensor(out=n_blk[:, j % 2, :], in0=cnt, scalar=float(SLOTS * j),
                                              in1=n_blk[:, (j - 1) % 2, :], op0=ALU.is_gt, op1=ALU.add))
            nb = n_blk[:, (T // SLOTS - 1) % 2, :]
            N2 = E - 2
            hv, cnt_h, hi_n, lo_n, t0, t1 = (heavy[:, i, 2:E] for i in range(6))
            n_h, n_l, n_m, x_h, x_h1 = (n_heavy[:, i:i + 1] for i in range(5))
            link(dve.tensor_scalar(hv, nb[:, 2:E], 1.0, None, ALU.is_gt))
            link(dve.tensor_tensor_scan(cnt_h, zeros_e[:, 2:E], hv, 0.0, ALU.add, ALU.add))
            dve.tensor_copy(n_h, heavy[:, 1, E - 1:E])
            link(dve.tensor_scalar(n_l, heavy[:, 1, E - 1:E], -1.0, float(N2), ALU.mult, ALU.add))
            link(dve.tensor_tensor(n_m, n_h, n_l, ALU.min))
            link(dve.tensor_tensor(x_h, n_h, n_m, ALU.subtract))
            dve.tensor_scalar(x_h1, x_h, -1.0, None, ALU.add)
            dve.tensor_tensor(hi_n, cnt_h, hv, ALU.subtract)
            dve.tensor_tensor(heavy[:, 4, 0:1], nb[:, 1:2], nb[:, 0:1], ALU.is_lt)
            link(dve.tensor_tensor(heavy[:, 4, 1:2], nb[:, 1:2], nb[:, 0:1], ALU.is_ge))
            link(dve.tensor_tensor(lo_n, iota_f[:, 0:N2], hi_n, ALU.subtract))
            dve.tensor_scalar(t0, hi_n, x_h1, 0.0, ALU.subtract, ALU.max)
            link(dve.tensor_scalar(t1, lo_n, n_m, None, ALU.min))
            dve.tensor_tensor(t0, t0, hi_n, ALU.add)
            link(dve.scalar_tensor_tensor(out=t1, in0=t1, scalar=x_h, in1=lo_n, op0=ALU.add, op1=ALU.add))
            link(dve.tensor_tensor(t0, t0, t1, ALU.subtract))
            link(dve.tensor_tensor(t0, t0, hv, ALU.mult))
            place = heavy[:, 4, :]
            link(dve.scalar_tensor_tensor(out=t0, in0=t0, scalar=2.0, in1=t1, op0=ALU.add, op1=ALU.add))
            link(dve.tensor_tensor(place_oh, place.unsqueeze(1).to_broadcast([P, E, E]),
                                   iota_f[:, 0:E].unsqueeze(2).to_broadcast([P, E, E]), ALU.is_equal))
            link(dve.tensor_tensor(place_v, place_oh, nb.unsqueeze(1).to_broadcast([P, E, E]), ALU.mult))
            link(dve.tensor_reduce(heavy[:, 2, :], place_v, AX_X, ALU.add))
            link(dve.memset(cum_f[:, 0:1], 0.0))
            link(dve.tensor_tensor_scan(cum_f[:, 1:E + 1], zeros_e[:, :], heavy[:, 2, :], 0.0, ALU.add, ALU.add))
            link(dve.tensor_copy(cum_i[:, :], cum_f[:, :]))
            link(dve.scalar_tensor_tensor(out=place_v, in0=place_oh, scalar=float(SLOTS),
                                          in1=cum_f[:, 0:E].unsqueeze(2).to_broadcast([P, E, E]),
                                          op0=ALU.mult, op1=ALU.mult))
            link(dve.tensor_reduce(base64[:, :], place_v.rearrange("p pos e -> p e pos"), AX_X, ALU.add))
            link(dve.tensor_tensor(posm[:, :, :], ps[:, 2, 0:NT * E].rearrange("p (t e) -> p t e", t=NT),
                                   base64[:, :].unsqueeze(1).to_broadcast([P, NT, E]), ALU.add))
            dve.wait_ge(s["c_written"], 16 * NT)
            for t in range(NT):
                last = dve.tensor_tensor(onehot[:, t, :, :], onehot[:, t, :, :],
                                         posm[:, t, :].unsqueeze(1).to_broadcast([P, TOP_K, E]), ALU.mult)
            link(last)
            link(dve.tensor_reduce(pos[:, :], onehot[:, :, :, :].rearrange("p t k e -> p (t k) e"), AX_X, ALU.add))
            link(dve.tensor_copy(pos_i[:, 0, :], pos[:, :]))
            link(dve.tensor_scalar(pos_i[:, 1, :], pos_i[:, 0, :], 6, None, ALU.arith_shift_right))
            link(dve.tensor_scalar(pos_i[:, 2, :], pos_i[:, 0, :], SLOTS - 1, None, ALU.bitwise_and))
            link(dve.tensor_copy(pos_f[:, :, :], pos_i[:, 1:3, :]))
            for t in range(NT):
                ks = slice(TOP_K * t, TOP_K * t + TOP_K)
                shape = [P, TOP_K, NG]
                io = iota_f[:, :].unsqueeze(1).to_broadcast(shape)
                hot = route[:, ks, P:P + NG]
                for d in range(2):
                    dve.tensor_tensor(route[:, ks, SLOTS * d:SLOTS * d + SLOTS], io,
                                      pos_f[:, 1, ks].unsqueeze(2).to_broadcast(shape), ALU.is_equal)
                link(dve.tensor_tensor(hot, io, pos_f[:, 0, ks].unsqueeze(2).to_broadcast(shape), ALU.is_equal))
                link(dve.tensor_tensor(route[:, ks, P + NG:P + 2 * NG], hot,
                                       gates[:, t, :].unsqueeze(2).to_broadcast(shape), ALU.mult))
                dve.tensor_scalar(hot, hot, tok1_f[:, t:t + 1], None, ALU.mult).then_inc(s["route_ok"], 1)
            link(dve.tensor_tensor(place_v, place_oh, iota_f[:, 0:E].unsqueeze(1).to_broadcast([P, E, E]), ALU.mult))
            link(dve.tensor_reduce(heavy[:, 3, :], place_v, AX_X, ALU.add))
            link(dve.tensor_scalar(cum_f[:, :], iota_f[:, 0:E + 1], heavy[:, 3, 0:1], None, ALU.add))
            link(dve.tensor_copy(side_i[:, :], cum_f[:, :]))
            link(dve.tensor_scalar(side_i[:, :], side_i[:, :], 1, None, ALU.bitwise_and))
            dve.tensor_copy(load_i[:, 2:E], iota_i[:, 2:E])
            dve.tensor_copy(load_i[:, 0:2], heavy[:, 3, 0:2])
            link(dve.memset(perm_i[:, E:E + 1], 0))
            link(dve.tensor_copy(perm_i[:, 0:E], heavy[:, 3, :]))
            dve.wait_ge(s["table_done"], 1)
            tab = ps[:, 0, 0:NG]
            dve.tensor_scalar(tok_idx[:, :], tab, -1.0, 0.0, ALU.add, ALU.max)
            dve.tensor_copy(gate_tab[:, :], ps[:, 0, NG:2 * NG])
            dve.tensor_scalar(tab_t[:, 0, :], tab, 0.0, pad_c[:, 0:1], ALU.is_equal, ALU.mult)
            link(dve.tensor_scalar(tab_t[:, 1, :], tab, 2.0, pad_c[:, 1:2], ALU.mult, ALU.add))
            link(dve.tensor_tensor(dst_idx[:, :], tab_t[:, 0, :], tab_t[:, 1, :], ALU.add))
            dve.sem_inc(s["tables_ok"], 1)
            dve.sem_inc(s["y_ok"], 1)

            STEPS = 10

            def experts_block(g):
                for b in range(2):
                    hh = ps[:, b, :].rearrange("p (n two) -> p n two", two=2)
                    dve.wait_ge(s["hA_done" if b == 0 else "hB_done"], g + 1)
                    dve.tensor_scalar(glu[:, b, :], hh[:, :, 0], SWIGLU_LIMIT, None, ALU.min).then_inc(s["glu_ok"], 1)
                    dve.tensor_scalar(lin[:, b, :], hh[:, :, 1], SWIGLU_LIMIT, -SWIGLU_LIMIT, ALU.min,
                                      ALU.max).then_inc(s["moe_step"], 1)
                    dve.wait_ge(s["sig_ok"], 2 * g + b + 1)
                    dve.tensor_tensor(glu[:, b, :], glu[:, b, :], sig[:, b, :], ALU.mult).then_inc(s["moe_step"], 1)
                    dve.wait_ge(s["moe_step"], 4 * g + 2 * b + 2)
                    dve.scalar_tensor_tensor(out=glu[:, b, :], in0=lin[:, b, :], scalar=1.0, in1=glu[:, b, :],
                                             op0=ALU.add, op1=ALU.mult).then_inc(s["act_ok"], 1)
                dve.wait_ge(s["y_done"], g + 1)
                dve.wait_ge(s["acc_done"], 16 * g + 16 * (NT + 1))
                dve.tensor_scalar(y_sb[:, :], ps[:, 2, :], gate_tab[:, bass.ds(g, 1)], None,
                                  ALU.mult).then_inc(s["y_ok"], 1)

            def selector(e):
                side = dve.value_load(side_i[0:1, bass.ds(e, 1)], min_val=0, max_val=1)
                expert = dve.value_load(perm_i[0:1, bass.ds(e, 1)], min_val=0, max_val=E - 1)
                dve.tensor_copy(sel_cur[:, bass.ds(side, 1), :].rearrange("p o s -> p (o s)"),
                                sel_sb[:, bass.ds(expert, 1)].to_broadcast([96, SLOTS])).then_inc(s["sel_ok"], 1)

            selector(0)
            with dve.Fori(0, E) as e:
                first = dve.value_load(cum_i[0:1, bass.ds(e, 1)], min_val=0, max_val=MAX_BLOCKS)
                end = dve.value_load(cum_i[0:1, bass.ds(e + 1, 1)], min_val=1, max_val=MAX_BLOCKS)
                selector(e + 1)
                with dve.Fori(first, end) as g:
                    experts_block(g)

            def hT_copy(t):
                dve.wait_ge(s["h_tr"], t + 1)
                for k in range(KD // 2, KD):
                    last = dve.tensor_scalar(hT[t][:, k, :], ps[:, tr_bank(t) + 1, (k % 4) * P:(k % 4 + 1) * P],
                                             g_ple_c[:, k:k + 1], None, ALU.mult)
                last.then_inc(s["hT_dve"], 1)

            hT_copy(0)
            hT_copy(1)
            dve.wait_ge(s["t_sq"], NT)
            dve.tensor_scalar(small[:, 36:36 + NT], small[:, 32:32 + NT], 1.0 / D, EPS, ALU.mult,
                              ALU.add).then_inc(s["t_var"], 1)
            dve.wait_ge(s["t_std"], 1)
            dve.reciprocal(small[:, 32:32 + NT], small[:, 40:40 + NT]).then_inc(s["t_rec"], 1)
            for t in range(NT):
                if 2 <= t + 1 < NT:
                    hT_copy(t + 1)
                if t == 0:
                    dve.wait_ge(s["pp_in"], 32)
                for n in range(2):
                    sl = slice(512 * n, 512 * n + 512)
                    dve.wait_ge(s["pg_sig"], 2 * t + n + 1)
                    link(dve.tensor_tensor(sg[t % 2][:, sl], sg[t % 2][:, sl], pp[:, t, sl], ALU.mult))
                    dve.tensor_tensor(hf[:, t, sl], hf[:, t, sl], sg[t % 2][:, sl], ALU.add).then_inc(s["h2_ok"], 1)
                dve.wait_ge(s["f_sq"], 2 * t + 2)
                link(dve.tensor_tensor(small[:, 48 + t:49 + t], small[:, 44:45], small[:, 46:47], ALU.add))
                dve.tensor_scalar(small[:, 48 + t:49 + t], small[:, 48 + t:49 + t], 1.0 / D, EPS, ALU.mult,
                                  ALU.add).then_inc(s["f_var"], 1)
                dve.wait_ge(s["f_std"], t + 1)
                link(dve.reciprocal(small[:, 63:64], small[:, 52 + t:53 + t]))
                for n in range(2):
                    sl = slice(512 * n, 512 * n + 512)
                    dve.scalar_tensor_tensor(out=outs_sb[:, t, sl], in0=hf[:, t, sl], scalar=small[:, 63:64],
                                             in1=gf_bc[:, sl], op0=ALU.mult, op1=ALU.mult).then_inc(s["out_ok"], 1)

        @block.gpsimd
        def _(pool):
            done = [0]

            def link(ins):
                done[0] += 1
                ins.then_inc(s["pool_step"], 1)
                pool.wait_ge(s["pool_step"], done[0])

            link(pool.memset(ident[:], 0.0))
            pool.affine_select(out=ident[:], in_=ident[:], pattern=[[-1, P]], compare_op=ALU.not_equal, fill=1.0,
                               base=0, channel_multiplier=1).then_inc(s["ident_ok"], 1)
            pool.memset(neg1[:], -1.0)
            pool.memset(tri[:], -1.0)
            pool.memset(ones_b[:], 1.0)
            pool.memset(upper_b[:], 1.0)
            link(pool.memset(sel_sb[:], 0.0))
            link(pool.affine_select(out=tri[:], in_=tri[:], pattern=[[-1, P]], compare_op=ALU.is_ge, fill=0.0,
                                    base=0, channel_multiplier=1))
            link(pool.affine_select(out=upper_b[:], in_=upper_b[:], pattern=[[1, P]], compare_op=ALU.is_gt, fill=0.0,
                                    base=0, channel_multiplier=-1))
            for j in range(3):
                v_ = sel_sb[32 * j:32 * j + 32, :]
                link(pool.affine_select(out=v_, in_=v_, pattern=[[-1, E]], compare_op=ALU.not_equal, fill=1.0,
                                        base=0, channel_multiplier=1))
            link(pool.iota(iota_i[:], pattern=[[1, NG]], base=0, channel_multiplier=0))
            link(pool.iota(pad_i[:, 0:NT], pattern=[[P, NT]], base=1, channel_multiplier=1))
            for half in range(2):
                sl = slice(64 * half, 64 * half + 64)
                link(pool.iota(pad_i[sl, 4:5], pattern=[[1, 1]], base=2 * T + 2, channel_multiplier=2))
                link(pool.iota(pad_i[sl, 5:6], pattern=[[1, 1]], base=half - 2, channel_multiplier=0))
            pool.tensor_copy(tok1_f[:, :], pad_i[:, 0:NT])
            link(pool.tensor_copy(pad_c[:, :], pad_i[:, 4:6]))
            pool.sem_inc(s["const_pool"], 1)

            pool.wait_ge(s["bias_in"], 16 * 6)
            link(pool.tensor_copy(bias_sb[:, :], bias_f32[0:96, :]))
            for j in (1, 2):
                for r in range(j, 3):
                    rows = slice(32 * r, 32 * r + 32)
                    link(pool.tensor_tensor(bias_f32[rows, :], bias_f32[rows, :], bias_sb[rows, :], ALU.subtract))
                    link(pool.tensor_copy(bias_sb[rows, :], bias_f32[rows, :]))
            pool.sem_inc(s["bias_ok"], 1)

            pool.dma_start(acc_rows[T:ROWS, :], x[0, 0:SLOTS, :]).then_inc(s["acc_done"], 16)

            def mask_diagonals(a):
                for t in range(NT):
                    d = a[:, OFF[t]:OFF[t] + P]
                    last = pool.affine_select(out=d, in_=d, pattern=[[1, P]], compare_op=ALU.is_gt, fill=0.0,
                                              base=0, channel_multiplier=-1)
                return last

            for hp in range(HP):
                for i in range(2):
                    pool.wait_ge(s["sp_ok"], 2 * hp + i + 1)
                    mask_diagonals(att_s[i]).then_inc(s["sp_masked"], 1)
                for i in range(2):
                    pool.wait_ge(s["w_ok"], 2 * hp + i + 1)
                    mask_diagonals(att_e[i]).then_inc(s["w_masked"], 1)
            for t in range(NT):
                pool.wait_ge(s["h_ok"], 2 * (t + 1))
                pool.dma_start(acc_rows[t * P:(t + 1) * P, :], h[:, t, :]).then_inc(s["acc_done"], 16)
                pool.wait_ge(s["c_ok"], t + 1)
                pool.dma_start(c_rows[t * P:(t + 1) * P, :], xs[:, t, :]).then_inc(s["c_written"], 16)

            def gather():
                pool.indirect_dma_start(out=xg[0:SLOTS, :], out_offset=None, in_=c_rows,
                                        in_offset=bass.IndirectOffsetOnAxis(ap=g_idx[:, 0:1], axis=0),
                                        ).then_inc(s["xg_in"], 16)

            pool.wait_ge(s["tables_ok"], 1)
            link(pool.tensor_copy(g_idx[:, :], tok_idx[0:SLOTS, 0:1]))
            pool.wait_ge(s["c_written"], 16 * NT)
            gather()
            base = done[0]

            def gather_next(g, n):
                pool.wait_ge(s["tx_done"], g + 1)
                pool.tensor_copy(g_idx[:, :], tok_idx[0:SLOTS, bass.ds(g + 1, 1)]).then_inc(s["pool_step"], 1)
                pool.wait_ge(s["pool_step"], base + n)
                pool.sem_inc(s["dma_turn"], 1)
                gather()

            def scatter(g, n):
                pool.wait_ge(s["acc_done"], 16 * g + 16 * (NT + 1))
                pool.tensor_copy(s_idx[:, :], dst_idx[:, bass.ds(g, 1)]).then_inc(s["pool_step"], 1)
                pool.wait_ge(s["pool_step"], base + n)
                pool.wait_ge(s["y_ok"], g + 2)
                pool.sem_inc(s["dma_turn"], 1)
                pool.indirect_dma_start(out=acc_halves, out_offset=bass.IndirectOffsetOnAxis(ap=s_idx[:, 0:1], axis=0),
                                        in_=y_sb[:, :], in_offset=None, compute_op=ALU.add).then_inc(s["acc_done"], 16)

            gather_next(0, 1)
            n_all = pool.value_load(cum_i[0:1, E:E + 1], min_val=E, max_val=MAX_BLOCKS)
            with pool.Fori(1, n_all) as g:
                gather_next(g, 2 * g)
                scatter(g - 1, 2 * g + 1)
            scatter(n_all - 1, 2 * n_all)


_INS = ["x", "p", "g_mix", "w_in", "w_out_a", "w_out_b", "w_out", "sgu_norm", "sgu_w", "sgu_b", "g_moe", "w_router",
        "b_router", "w1", "b1", "w2", "b2", "g_ple", "w_ple_gate", "w_ple_proj", "g_final"]


def kernel(**inputs):
    import numpy as _np
    import concourse.bacc as _bacc
    from concourse import mybir as _mybir
    from concourse.bass_utils import run_bass_kernel_spmd as _run

    nc = _bacc.Bacc("TRN2", target_bir_lowering=False, num_devices=1)
    arrays, args = {}, []
    for name in _INS:
        a = _np.ascontiguousarray(inputs[name])
        arrays[f"in_{name}_dram"] = a
        args.append(nc.dram_tensor(f"in_{name}_dram", a.shape, _mybir.dt.from_np(a.dtype), kind="ExternalInput").ap())
    shape = inputs["x"].shape
    args.append(nc.dram_tensor("out_0_dram", shape, _mybir.dt.float32, kind="ExternalOutput").ap())
    hybrid_block(nc, *args)
    r = _run(nc, [arrays], core_ids=[0])
    return r.results[0]["out_0_dram"]
```

```python
from contextlib import ExitStack

import concourse.bass as bass
from concourse import mybir

ALU = mybir.AluOpType
ACT = mybir.ActivationFunctionType
F32 = mybir.dt.float32
F32R = mybir.dt.float32r
BF16 = mybir.dt.bfloat16
I32 = mybir.dt.int32
U32 = mybir.dt.uint32
AX_X = mybir.AxisListType.X

P = 128
EPS = 1e-6
SWIGLU_ALPHA = 1.702
SWIGLU_LIMIT = 7.0
TOP_K = 4
SLOTS = 64
SGU_CHUNK = 64


def hybrid_block(nc, x, p, g_mix, w_in, w_out_a, w_out_b, w_out, sgu_norm, sgu_w, sgu_b, g_moe, w_router,
                 b_router, w1, b1, w2, b2, g_ple, w_ple_gate, w_ple_proj, g_final, out):
    T, D = x.shape[1], x.shape[2]
    NT = T // P
    KD = D // P
    WIDTH = w_out_a.shape[1]
    KW = WIDTH // P
    HD = 64
    HP = WIDTH // (2 * HD)
    GROUPS = sgu_w.shape[1]
    E = w_router.shape[2]
    DE = w2.shape[2]
    PLE = p.shape[3]
    KP = PLE // P
    MAX_BLOCKS = (E * (SLOTS - 1) + T * TOP_K) // SLOTS
    NG = MAX_BLOCKS + 1
    ROWS = T + SLOTS
    CH = KD * WIDTH
    assert CH == 4096 and D == 1024 and DE == 1024 and NT == 4 and E == 32

    with ExitStack() as ctx:
        def sb(name, shape, dt=F32):
            return ctx.enter_context(nc.sbuf_tensor(name, shape, dt))

        def sem(name):
            return ctx.enter_context(nc.semaphore(name))

        c_rows = nc.dram_tensor("c_rows", (T, D), F32).ap()
        acc_rows = nc.dram_tensor("acc_rows", (ROWS, D), F32).ap()
        pp_rows = nc.dram_tensor("pp_rows", (T, D), F32).ap()
        pp_rows_v = pp_rows.rearrange("(t p) n -> p t n", p=P)
        acc_halves = acc_rows.rearrange("r (h n) -> (r h) n", h=2)

        with ExitStack() as end_ctx:
            def at_end(name, n, dt=F32):
                return end_ctx.enter_context(nc.sbuf_tensor(name, [P, n], dt))

            wg = at_end("wg", 2 * CH)[:, :].rearrange("p (k n) -> p k n", k=KD)
            wg_hi = at_end("wg_hi", 2 * CH, F32R)[:, :].rearrange("p (k n) -> p k n", k=KD)
            at_end("end_gap_1", CH)
            h_hi = at_end("h_hi", CH, F32R)[:, :].rearrange("p (t k q) -> p t k q", t=NT, k=KD)
            h_lo = at_end("h_lo", CH, F32R)[:, :].rearrange("p (t k q) -> p t k q", t=NT, k=KD)
            at_end("end_gap_2", 2 * CH)
            wg_lo = at_end("wg_lo", 2 * CH, F32R)[:, :].rearrange("p (k n) -> p k n", k=KD)

        arena = sb("arena", [P, 11 * CH])

        def chunk(i, lo=0, n=CH):
            return arena[:, i * CH + lo:i * CH + lo + n]

        w1_buf = arena[:, 0:8 * CH].rearrange("p (e b k n) -> p e b k n", e=2, b=2, k=KD)
        w2lo_buf = arena[:, 8 * CH:10 * CH].rearrange("p (e k n) -> p e k n", e=2, k=4)
        w2hi_buf = chunk(10).rearrange("p (k n) -> p k n", k=4)

        aT = chunk(0).rearrange("p (k t) -> p k t", k=KD)
        gateB = chunk(1).rearrange("p (k t) -> p k t", k=KD)
        gateA = chunk(4).rearrange("p (k t) -> p k t", k=KD)
        qT = chunk(8, 0, 2048).rearrange("p (k t) -> p k t", k=KW)
        uT = chunk(8, 2048, 2048).rearrange("p (k t) -> p k t", k=KW)
        vs = chunk(10, 0, 2048).rearrange("p (t c) -> p t c", t=NT)
        wmT = chunk(10, 2048, 1024).rearrange("p (g t) -> p g t", g=GROUPS)
        wm_raw = chunk(10, 3072, 1024).rearrange("p (g s) -> p g s", g=GROUPS)
        kT = chunk(5, 0, 2048).rearrange("p (k t) -> p k t", k=KW)
        v = chunk(5, 2048, 2048).rearrange("p (t c) -> p t c", t=NT)
        h = chunk(5).rearrange("p (t c) -> p t c", t=NT)
        xs = chunk(9).rearrange("p (t c) -> p t c", t=NT)
        bias_f32 = chunk(1, 0, 3072)
        junk = chunk(1, 3072, 1024)
        oaT, obT, merged = qT, uT, gateA

        ident = sb("ident", [P, P])
        tri = sb("tri", [P, P])
        neg1 = sb("neg1", [P, P])
        ones_b = sb("ones_b", [P, P], BF16)
        upper_b = sb("upper_b", [P, P], BF16)
        xg = sb("xg", [P, 1024])
        xT = sb("xT", [P, KD, SLOTS])
        act_work = sb("act_work", [P, 3 * 512])
        glu, sig, lin = (act_work[:, 512 * i:512 * i + 512].rearrange("p (b n) -> p b n", b=2) for i in range(3))
        out_work = sb("out_work", [P, 2 * 512])
        actT = out_work[:, 0:512].rearrange("p (b c s) -> p b c s", b=2, c=2)
        y_sb = out_work[:, 512:1024]
        bias_sb = sb("bias_sb", [96, 3072], BF16)
        sel_sb = sb("sel_sb", [96, E], BF16)
        sel_cur = sb("sel_cur", [96, 2, SLOTS], BF16)
        g_mix_c = sb("g_mix_c", [P, KD])
        g_ple_c = sb("g_ple_c", [P, KD])
        sgu_g_c = sb("sgu_g_c", [P, KW])
        sgu_b_bc = out_work[:, 0:512].rearrange("p (g t) -> p g t", g=GROUPS // 2)
        b_router_bc = sb("b_router_bc", [P, E])
        w_router_sb = sb("w_router_sb", [P, KD, E])
        small = sb("small", [P, 64])
        bn6 = sb("bn6", [P, NT, 6])
        bn2 = sb("bn2", [P, NT, 2])
        iota_i = sb("iota_i", [P, NG], I32)
        iota_f = sb("iota_f", [P, NG])
        tok1_f = sb("tok1_f", [P, NT])
        pad_c = sb("pad_c", [P, 2])
        pad_i = sb("pad_i", [P, 6], I32)
        tok_idx = sb("tok_idx", [P, NG], I32)
        dst_idx = sb("dst_idx", [P, NG], I32)
        gate_tab = sb("gate_tab", [P, NG])
        cum_i = sb("cum_i", [P, E + 1], I32)
        side_i = sb("side_i", [P, E + 1], I32)
        perm_i = sb("perm_i", [P, E + 1], I32)
        g_idx = sb("g_idx", [SLOTS, 1], I32)
        s_idx = sb("s_idx", [P, 1], I32)
        g_moe_bc = xg
        place_terms = act_work[:, 1024:1024 + 3 * E + 1]
        place_col = act_work[:, 1152:1154]
        ATT = (NT + 3 + 2 + 1) * P
        att_e = [chunk(9, 0, ATT), chunk(9, ATT, ATT)]
        att_s = [chunk(9, 2 * ATT, ATT), act_work[:, 0:ATT]]
        sp_sum = [[chunk(9, 3 * ATT, 2 * P), out_work[:, 512:512 + P]],
                  [act_work[:, ATT:ATT + 2 * P], out_work[:, 512 + P:512 + 2 * P]]]
        cT = out_work[:, :].rearrange("p (k t) -> p k t", k=KD)
        route = chunk(9).rearrange("p (j n) -> p j n", j=NT * TOP_K)
        lg = sb("lg", [P, NT, E])
        top_v = sb("top_v", [P, NT, 8])
        top_i = sb("top_i", [P, NT, 8], U32)
        top_f = sb("top_f", [P, NT, 8])
        onehot = xT[:, :, :].rearrange("p k s -> p (k s)").rearrange("p (t k e) -> p t k e", t=NT, k=TOP_K)
        mask = sb("mask", [P, NT, E])
        mask_b = sb("mask_b", [P, NT, E], BF16)
        gates = sb("gates", [P, NT, TOP_K])
        gsum = sb("gsum", [P, NT])
        grec = sb("grec", [P, NT])
        nmax = sb("nmax", [P, NT])
        n_blk = sb("n_blk", [P, 2, E])
        cum_f = sb("cum_f", [P, E + 1])
        heavy = sb("heavy", [P, 6, E])
        n_heavy = sb("n_heavy", [P, 8])
        zeros_e = sb("zeros_e", [P, E])
        posm = sb("posm", [P, NT, E])
        pos = sb("pos", [P, NT * TOP_K])
        pos_i = sb("pos_i", [P, 3, NT * TOP_K], I32)
        pos_f = lg[:, 0, 0:2 * NT * TOP_K].rearrange("p (a j) -> p a j", a=2)
        load_i = pos_i[:, :, :].rearrange("p a j -> p (a j)")[:, 0:E]
        tab_t = mask[:, :, :].rearrange("p (a t) e -> p a (t e)", a=2)

        ps = ctx.enter_context(nc.psum_tensor("ps", [P, 8, 512], F32))
        place_sums = ps[:, 1, 0:3 * E + 1]

        s = {n: sem(n) for n in (
            "g_mix_in", "eps_ok",
            "small_in", "g_bc_in", "wm_in", "bias_in", "x_again", "const_pool", "ident_ok",
            "sq_done", "rms_ok", "sqrt_done", "xn_ok", "xT_tr", "aT_act", "aT_dve", "wm_tr", "wmT_ok",
            "unit_done", "evac_act", "evac_dve", "z_done", "tri_done",
            "abs_ok", "ln_ok", "exp_ok", "sp_ok", "sp_masked", "w_ok", "w_masked",
            "ln_stats", "ln_std", "vs_ok", "ob_ok", "merged_ok",
            "h_ok", "h_sq", "h_var", "h_std", "c_ok", "c_tr", "cT_ok", "logit_done", "c_written", "acc_done",
            "top_ok", "gexp_ok", "mask_ok", "rank_done", "route_ok",
            "place_ok", "place_done", "table_done", "first_ok", "tables_ok",
            "dve_step", "pool_step", "bias_ok",
            "tx_done", "xg_in", "xT_ok", "hA_done", "hB_done", "glu_ok", "sig_ok", "act_ok",
            "tA_done", "actT_ok", "mm2lo_done", "y_done", "y_ok", "sel_ok", "moe_step",
            "tx_turn", "dma_turn", "load_turn",
            "p_in", "p_tr", "pT_ok", "pp_done", "pp_ok", "pp_in", "t_sq", "t_var", "t_std", "t_rec",
            "h_tr", "h_hi_act", "h_hi_dve", "h_lo", "wg_hi_ok", "wg_ok", "act_turn",
            "pg_done", "pg_sig", "h2_ok", "f_sq", "f_var", "f_std", "out_ok", "out_written",
        )}
        w1_in = [sem(f"w1_in_{j}") for j in range(4)]
        w2lo_in = [sem(f"w2lo_in_{j}") for j in range(2)]
        w2hi_in = [sem(f"w2hi_in_{j}") for j in range(2)]
        x_in = [sem(f"x_in_{t}") for t in range(NT)]
        ring_in = {c: sem(f"ring_in_{c}") for c in (2, 3, 6, 7)}

        GROUP_BUF = {"q": 2, "k": 3, "v": 6, "vs": 7, "u": 2, "ga0": 3, "ga1": 6, "gb0": 7, "gb1": 2,
                     "woa": 3, "wob": 2, "wo0": 7, "wo1": 6}
        LOAD_ORDER = ["q", "k", "v", "vs", "u", "ga0", "ga1", "gb0", "gb1", "woa", "wo1", "wo0", "wob"]
        COLS = {"q": 0, "k": 1, "v": 2, "u": 3, "vs": 4, "ga0": 5, "ga1": 6, "gb0": 7, "gb1": 8}
        fill = [(g, j) for g in ("vs", "u", "ga0", "ga1", "gb0", "gb1") for j in range(4)]
        units = [(g, j) for g in ("q", "k", "v") for j in range(4)]
        pe_plan = [("unit", u) for u in units]
        PER = len(fill) // HP // 2
        for hp in range(HP):
            pe_plan.append(("z", hp))
            pe_plan += [("unit", u) for u in fill[2 * PER * hp:2 * PER * hp + PER]]
            pe_plan.append(("tri", hp))
            pe_plan += [("unit", u) for u in fill[2 * PER * hp + PER:2 * PER * (hp + 1)]]
            pe_plan.append(("unit", ("out", hp)))
            if hp == 2:
                pe_plan += [("unit", ("sv", j)) for j in range(GROUPS // 2)]
            if hp == 0:
                pe_plan.append(("ln", 0))
        pe_plan += [("unit", ("woa", j)) for j in range(KD)] + [("unit", ("wob", j)) for j in range(KD)]
        units = [a for k, a in pe_plan if k == "unit"]
        units += [("wo", j) for j in range(2 * NT)]
        ON_ACT = ("q", "v", "vs", "u", "ga0", "ga1", "gb0", "gb1", "out")
        evac_of, counts = {}, {"evac_act": 0, "evac_dve": 0}
        for u in units:
            e = "evac_act" if u[0] in ON_ACT else "evac_dve"
            counts[e] += 1
            evac_of[u] = (e, counts[e])
        unit_no = {u: i + 1 for i, u in enumerate(units)}

        def unit_bank(u):
            return ps[:, 6 + (unit_no[u] - 1) % 2, :]

        last_unit = {g: (g, 3) for g in COLS} | {"woa": ("woa", KD - 1), "wob": ("wob", KD - 1)}
        ring_count = {}
        seen = {c: 0 for c in ring_in}
        prev_in_buf, last_of = {}, {}
        for g in LOAD_ORDER:
            c = GROUP_BUF[g]
            seen[c] += 1
            ring_count[g] = 16 * seen[c]
            prev_in_buf[g] = last_of.get(c)
            last_of[c] = g

        aT_order = [KD - 2, KD - 1] + list(range(KD - 2))

        def tr_bank(t):
            return 6 * (t % 2)

        def logit_ps(t):
            return ps[:, 3 if t == NT - 1 else 2, t * E:(t + 1) * E]

        def ring_wait(eng, g):
            eng.wait_ge(ring_in[GROUP_BUF[g]], ring_count[g])

        OFF = {0: 0, 1: 512, 3: 896, 2: 1024}

        w_in_v = w_in[0].rearrange("(k p) n -> p k n", p=P)

        def ring_view(g, k=KD):
            return chunk(GROUP_BUF[g]).rearrange("p (k n) -> p k n", k=k)

        x_v = x[0].rearrange("(t p) d -> p t d", p=P)
        out_v = out[0].rearrange("(t p) d -> p t d", p=P)
        w1_v = w1[0].rearrange("e (k p) n -> p e k n", p=P)
        w2_v = w2[0].rearrange("e (k p) n -> p e k n", p=P)

        wproj = chunk(10, 0, 2048).rearrange("p (k n) -> p k n", k=KP)
        p_sb = chunk(10, 2048, 1024).rearrange("p (t c) -> p t c", t=NT)
        pT = chunk(10, 3072, 1024).rearrange("p (k t) -> p k t", k=KP)
        pp_out = [xg, chunk(10, 2048, 1024), out_work, act_work[:, 0:1024]]
        pp = chunk(8).rearrange("p (t n) -> p t n", t=NT)
        hf = chunk(4).rearrange("p (t c) -> p t c", t=NT)
        outs_sb = chunk(0).rearrange("p (t c) -> p t c", t=NT)
        sg = [chunk(7, 1024 * i, 1024) for i in range(2)]
        gf_bc = chunk(7, 2048, 1024)
        pp_written = [sem(f"pp_written_{t}") for t in range(NT)]
        wg_in = [sem(f"wg_in_{n}") for n in range(2)]
        acc_in = [sem(f"acc_in_{t}") for t in range(NT)]

        block = ctx.enter_context(nc.Block())

        @block.sync
        def _(sp):
            def load_group(g):
                if prev_in_buf[g]:
                    sp.wait_ge(s["unit_done"], unit_no[last_unit[prev_in_buf[g]]])
                if g in COLS:
                    src = w_in_v[:, :, COLS[g] * WIDTH:(COLS[g] + 1) * WIDTH]
                elif g in ("woa", "wob"):
                    w = w_out_a if g == "woa" else w_out_b
                    src = w[0].rearrange("(k p) n -> p k n", p=P)
                else:
                    n = int(g[2])
                    src = w_out[0].rearrange("(k p) n -> p k n", p=P)[:, 4 * n:4 * n + 4, :]
                dst = ring_view(g, src.shape[1])
                sp.dma_start(dst, src).then_inc(ring_in[GROUP_BUF[g]], 16)

            for t in range(NT):
                sp.dma_start(xs[:, t, :], x_v[:, t, :]).then_inc(x_in[t], 16)
            with nc.allow_non_contiguous_dma(reason="gains by feature on partitions: 20 kB once"):
                sp.dma_start(g_mix_c[:], g_mix[0].rearrange("(k p) -> p k", p=P)).then_inc(s["g_mix_in"], 16)
            load_group(LOAD_ORDER[0])
            with nc.allow_non_contiguous_dma(reason="gains by feature on partitions: 20 kB once"):
                sp.dma_start(sgu_g_c[:], sgu_norm[0].rearrange("(k p) -> p k", p=P)).then_inc(s["small_in"], 16)
                sp.dma_start(g_ple_c[:], g_ple[0].rearrange("(k p) -> p k", p=P)).then_inc(s["small_in"], 16)
            for j in range(GROUPS):
                sp.dma_start(sgu_b_bc[64 * (j % 2):64 * (j % 2) + 64, j // 2, :],
                             sgu_b[0, j:j + 1, :].to_broadcast([64, P])).then_inc(s["small_in"], 16)
            sp.dma_start(b_router_bc[:], b_router[0:1, :].to_broadcast([P, E])).then_inc(s["small_in"], 16)
            sp.dma_start(w_router_sb[:], w_router[0].rearrange("(k p) e -> p k e", p=P)).then_inc(s["small_in"], 16)
            sp.dma_start(wm_raw, sgu_w[0].rearrange("g t s -> t g s")).then_inc(s["wm_in"], 16)

            for g in LOAD_ORDER[1:4]:
                load_group(g)
            sp.dma_start(g_moe_bc[:], g_moe[0:1, :].to_broadcast([P, D])).then_inc(s["g_bc_in"], 16)
            for i in range(3):
                sp.dma_start(bias_f32[32 * i:32 * i + 32, 0:2 * DE], b1[0]).then_inc(s["bias_in"], 16)
                sp.dma_start(bias_f32[32 * i:32 * i + 32, 2 * DE:3 * DE], b2[0]).then_inc(s["bias_in"], 16)
            for g in LOAD_ORDER[4:-1]:
                load_group(g)
            sp.wait_ge(s["unit_done"], unit_no[("out", HP - 1)])
            for t in range(NT):
                sp.dma_start(xs[:, t, :], x_v[:, t, :]).then_inc(s["x_again"], 16)
            load_group(LOAD_ORDER[-1])
            sp.wait_ge(s["ob_ok"], GROUPS // 2)
            sp.dma_start(wproj, w_ple_proj[0].rearrange("(k p) n -> p k n", p=P)).then_inc(s["p_in"], 16)
            sp.dma_start(p_sb, p[0, 0].rearrange("(t p) d -> p t d", p=P)).then_inc(s["p_in"], 16)

            def arrival(j, n):
                if j < 8:
                    return w1_in[j % 4], 16 * (2 * n + j // 4 + 1)
                return (w2lo_in if j < 10 else w2hi_in)[j % 2], 16 * (n + 1)

            def load_piece(j, e, side):
                k = slice(2 * (j % 4), 2 * (j % 4) + 2)
                if j < 8:
                    dst = w1_buf[:, side, j // 4, k, :]
                    src = w1_v[:, e, k, DE * (j // 4):DE * (j // 4 + 1)]
                else:
                    h2 = slice(2 * (j % 2), 2 * (j % 2) + 2)
                    dst = w2lo_buf[:, side, h2, :] if j < 10 else w2hi_buf[:, h2, :]
                    src = w2_v[:, e, 2 * (j - 8):2 * (j - 8) + 2, :]
                sp.dma_start(dst, src).then_inc(arrival(j, 0)[0], 16)

            def load_first(js, e, ahead=3):
                for i, j in enumerate(js):
                    if i >= ahead:
                        sp.wait_ge(*arrival(js[i - ahead], e))
                    load_piece(j, e, e)

            sp.wait_ge(s["merged_ok"], KD)
            sp.wait_ge(s["unit_done"], unit_no[("wob", KD - 1)])
            load_first(range(10), 0)
            sp.wait_ge(s["unit_done"], len(units))
            load_first((0, 1, 4, 5), 1, 2)
            sp.wait_ge(s["acc_done"], 16 * (NT + 1))
            sp.wait_ge(s["c_ok"], NT)
            load_first((2, 3, 6, 7), 1, 2)
            for t in range(NT):
                sp.wait_ge(s["pp_ok"], t + 1)
                sp.dma_start(pp_rows_v[:, t, :], pp_out[t][:, :]).then_inc(pp_written[t], 16)
            sp.wait_ge(s["xg_in"], 16)
            for t in range(NT):
                sp.wait_ge(pp_written[t], 16)
            sp.wait_ge(s["tables_ok"], 1)
            load_first((8, 9), 1)
            first_expert = sp.value_load(perm_i[0:1, 0:1], min_val=0, max_val=1)
            for j in (10, 11):
                load_piece(j, first_expert, None)

            with sp.Fori(2, E) as pos_:
                two_back = sp.value_load(cum_i[0:1, bass.ds(pos_ - 1, 1)], min_val=1, max_val=MAX_BLOCKS)
                last_expert = sp.value_load(perm_i[0:1, bass.ds(pos_ - 1, 1)], min_val=0, max_val=E - 1)
                expert = sp.value_load(perm_i[0:1, bass.ds(pos_, 1)], min_val=0, max_val=E - 1)
                side = sp.value_load(side_i[0:1, bass.ds(pos_, 1)], min_val=0, max_val=1)
                order = [(j, pos_) for j in range(4)] + [(j, pos_ - 1) for j in (10, 11)] + \
                    [(j, pos_) for j in range(4, 10)]
                seq = [(j, p_ - 1) for j, p_ in order[-3:]] + order
                for i, (j, p_) in enumerate(order):
                    if j == 0:
                        sp.wait_ge(s["hA_done"], two_back)
                    elif j == 4:
                        sp.wait_ge(s["hB_done"], two_back)
                    elif j == 8:
                        sp.wait_ge(s["mm2lo_done"], two_back)
                    elif j == 10:
                        sp.wait_ge(s["y_done"], two_back)
                    sp.wait_ge(*arrival(*seq[i]))
                    sp.sem_inc(s["load_turn"], 1)
                    load_piece(j, expert if j < 10 else last_expert, side)
            last_expert = sp.value_load(perm_i[0:1, E - 1:E], min_val=0, max_val=E - 1)
            one_back = sp.value_load(cum_i[0:1, E - 1:E], min_val=1, max_val=MAX_BLOCKS)
            sp.wait_ge(s["y_done"], one_back)
            sp.sem_inc(s["load_turn"], 1)
            for j in (10, 11):
                load_piece(j, last_expert, None)
            nb = sp.value_load(cum_i[0:1, E:E + 1], min_val=1, max_val=MAX_BLOCKS)
            wg_v = w_ple_gate[0].rearrange("(k p) n -> p k n", p=P)
            sp.wait_ge(s["hA_done"], nb)
            for n in range(2):
                sp.dma_start(wg[:, :, 512 * n:512 * n + 512], wg_v[:, :, 512 * n:512 * n + 512]).then_inc(wg_in[n], 16)
            sp.wait_ge(s["acc_done"], 16 * (NT + 1) + nb * 16)
            for t in range(NT):
                sp.dma_start(hf[:, t, :], acc_rows[t * P:(t + 1) * P, :]).then_inc(acc_in[t], 16)
            sp.dma_start(gf_bc, g_final.rearrange("(a d) -> a d", a=1).to_broadcast([P, D])).then_inc(s["pp_in"], 16)
            sp.dma_start(pp, pp_rows_v).then_inc(s["pp_in"], 16)
            for t in range(NT):
                for n in range(2):
                    sl = slice(512 * n, 512 * n + 512)
                    sp.wait_ge(s["out_ok"], 2 * t + n + 1)
                    sp.dma_start(out_v[:, t, sl], outs_sb[:, t, sl]).then_inc(s["out_written"], 16)
            sp.wait_ge(s["out_written"], 32 * NT)

        @block.tensor
        def _(pe):
            def wait_unit_bank(u):
                n = unit_no[u]
                if n > 2:
                    e, c = evac_of[units[n - 3]]
                    pe.wait_ge(s[e], c)

            pe.wait_ge(s["ident_ok"], 1)
            for t in range(NT):
                pe.wait_ge(s["xn_ok"], t + 1)
                for k in range(KD):
                    last = pe.transpose(ps[:, k, t * P:(t + 1) * P], xs[:, t, k * P:(k + 1) * P], ident[:, :])
            last.then_inc(s["xT_tr"], 1)
            def product_T(u, w, j, rhs, nk):
                for i, k in enumerate(aT_order if u == units[0] else range(nk)):
                    if u == units[0]:
                        if i == 0:
                            pe.wait_ge(s["aT_dve"], 1)
                        pe.wait_ge(s["aT_dve" if k % 2 else "aT_act"], i // 2 + 1)
                    last = pe.matmul(unit_bank(u), w[:, k, j * P:(j + 1) * P], rhs[:, k, :],
                                     start=(i == 0), stop=(i == nk - 1))
                return last

            def unit(u):
                g, j = u
                wait_unit_bank(u)
                if g in ("q", "k", "u", "ga0", "ga1", "gb0", "gb1"):
                    if j == 0:
                        ring_wait(pe, g)
                    last = product_T(u, ring_view(g), j, aT, KD)
                elif g in ("v", "vs"):
                    if j == 0:
                        ring_wait(pe, g)
                    w = ring_view(g)
                    for k in range(KD):
                        last = pe.matmul(unit_bank(u), aT[:, k, j * P:(j + 1) * P], w[:, k, :],
                                         start=(k == 0), stop=(k == KD - 1))
                elif g == "out":
                    pe.wait_ge(s["w_masked"], 2 * (j + 1))
                    for t in range(NT):
                        for i in range(2):
                            last = pe.matmul(unit_bank(u)[HD * i:HD * i + HD, t * P:],
                                             v[:, t, (2 * j + i) * HD:(2 * j + i + 1) * HD],
                                             att_e[i][:, OFF[t]:OFF[t] + (NT - t) * P],
                                             start=(t == 0), stop=(t == NT - 1), skip_group_check=True)
                elif g == "sv":
                    pe.wait_ge(s["vs_ok"], NT)
                    pe.wait_ge(s["wmT_ok"], 1)
                    for t in range(NT):
                        for i in range(2):
                            last = pe.matmul(unit_bank(u)[64 * i:64 * i + 64, t * P:(t + 1) * P],
                                             vs[:, t, (2 * j + i) * 64:(2 * j + i + 1) * 64],
                                             wmT[:, 2 * j + i, :], start=True, stop=True, skip_group_check=True)
                elif g == "woa":
                    if j == 0:
                        ring_wait(pe, g)
                        e, c = evac_of[("out", HP - 1)]
                        pe.wait_ge(s[e], c)
                    last = product_T(u, ring_view(g, KW), j, oaT, KW)
                elif g == "wob":
                    if j == 0:
                        ring_wait(pe, g)
                        pe.wait_ge(s["ob_ok"], GROUPS // 2)
                    last = product_T(u, ring_view(g, KW), j, obT, KW)
                else:
                    t, n = j // 2, j % 2
                    if j == 0:
                        ring_wait(pe, "wo0")
                        ring_wait(pe, "wo1")
                        pe.wait_ge(s["merged_ok"], KD)
                    for k in range(KD):
                        last = pe.matmul(unit_bank(u), merged[:, k, t * P:(t + 1) * P],
                                         ring_view(f"wo{k // 4}", 4)[:, k % 4, n * 512:(n + 1) * 512],
                                         start=(k == 0), stop=(k == KD - 1))
                last.then_inc(s["unit_done"], 1)

            for kind, a in pe_plan:
                if kind == "unit":
                    unit(a)
                    if a == ("q", 3):
                        pe.wait_ge(s["wm_in"], 16)
                        for g in range(GROUPS):
                            last = pe.transpose(ps[:, g // 4, (g % 4) * P:(g % 4 + 1) * P], wm_raw[:, g, :], ident[:, :])
                        last.then_inc(s["wm_tr"], 1)
                elif kind == "z":
                    e, c = evac_of[("q", a)]
                    pe.wait_ge(s[e], c)
                    e, c = evac_of[("k", a)]
                    pe.wait_ge(s[e], c)
                    if a == 0:
                        pe.wait_ge(s["wmT_ok"], 1)
                    else:
                        pe.wait_ge(s["w_ok"], 2 * a)
                    for t in (0, 1, 3, 2):
                        for i in range(2):
                            z = ps[:, 3 * i:3 * i + 3, :].rearrange("p b n -> p (b n)")
                            last = pe.matmul(z[:, OFF[t]:OFF[t] + (NT - t) * P],
                                             kT[HD * i:HD * i + HD, a, t * P:(t + 1) * P],
                                             qT[HD * i:HD * i + HD, a, t * P:],
                                             start=(t != 3), stop=False, skip_group_check=True)
                    last.then_inc(s["z_done"], 1)
                elif kind == "tri":
                    for i in range(2):
                        pe.wait_ge(s["sp_masked"], 2 * a + i + 1)
                        z = ps[:, 3 * i:3 * i + 3, :].rearrange("p b n -> p (b n)")
                        sp_ = att_s[i]
                        for t in range(NT):
                            own = sp_[:, OFF[t]:OFF[t] + (NT - t) * P]
                            parts = [(tri, own, t)]
                            if t < NT - 1:
                                parts.append((neg1, sp_[:, OFF[t + 1]:OFF[t + 1] + P], t + 1))
                            if t < NT - 2:
                                parts.append((neg1, sp_sum[i][t], t + 2))
                            for w, rhs, q in parts:
                                col = OFF[t] + (q - t) * P
                                last = pe.matmul(z[:, col:col + rhs.shape[1]], w[:, :], rhs, start=False,
                                                 stop=(q == parts[-1][2]), skip_group_check=True)
                        last.then_inc(s["tri_done"], 1)

            def c_transposes(t):
                pe.wait_ge(s["c_ok"], t + 1)
                for k in range(KD):
                    last = pe.transpose(ps[:, k // 4, (k % 4) * P:(k % 4 + 1) * P], xs[:, t, k * P:(k + 1) * P],
                                        ident[:, :])
                last.then_inc(s["c_tr"], 1)

            def logits(t):
                pe.wait_ge(s["cT_ok"], t + 1)
                for k in range(KD):
                    last = pe.matmul(logit_ps(t), cT[:, k, :], w_router_sb[:, k, :],
                                     start=(k == 0), stop=(k == KD - 1))
                last.then_inc(s["logit_done"], 1)

            wo = [("wo", j) for j in range(2 * NT)]
            for u in wo[0:4]:
                unit(u)
            c_transposes(0)
            unit(wo[4])
            logits(0)
            c_transposes(1)
            unit(wo[5])
            logits(1)
            unit(wo[6])
            c_transposes(2)
            unit(wo[7])
            logits(2)
            c_transposes(3)
            pe.wait_ge(s["p_in"], 32)
            pe.wait_ge(s["h_ok"], 2 * NT)
            for k in range(KP):
                for t in range(NT):
                    last = pe.transpose(ps[:, 6 + k, t * P:(t + 1) * P], p_sb[:, t, k * P:(k + 1) * P], ident[:, :])
            last.then_inc(s["p_tr"], 1)
            logits(3)

            pe.wait_ge(s["mask_ok"], 2)
            for t in range(NT):
                for t2 in range(t + 1):
                    pe.matmul(ps[:, 2, t * E:(t + 1) * E], (upper_b if t2 == t else ones_b)[:, :], mask_b[:, t2, :],
                              start=(t2 == 0), stop=(t2 == t))
            for t in range(NT):
                last = pe.matmul(ps[:, 2, NT * E:(NT + 1) * E], ones_b[:, :], mask_b[:, t, :],
                                 start=(t == 0), stop=(t == NT - 1))
            last.then_inc(s["rank_done"], 1)
            def projection(t, n):
                if n == 0 and t > 1:
                    pe.wait_ge(s["pp_ok"], t - 1)
                for k in range(KP):
                    last = pe.matmul(ps[:, 4 + 2 * (t % 2) + n, :], pT[:, k, t * P:(t + 1) * P],
                                     wproj[:, k, n * 512:(n + 1) * 512], start=(k == 0), stop=(k == KP - 1))
                if n == 1:
                    last.then_inc(s["pp_done"], 1)

            def table(t):
                pe.wait_ge(s["route_ok"], t + 1)
                for j in range(TOP_K * t, TOP_K * t + TOP_K):
                    for half in range(2):
                        last = pe.matmul(ps[64 * half:64 * half + 64, 0, 0:2 * NG], route[:, j, 0:SLOTS],
                                         route[:, j, SLOTS:SLOTS + 2 * NG], start=(j == 0),
                                         stop=(j == NT * TOP_K - 1), skip_group_check=True)
                return last

            pe.wait_ge(s["pT_ok"], 1)
            projection(0, 0)
            projection(0, 1)
            projection(1, 0)
            pe.wait_ge(s["place_ok"], 1)
            pe.matmul(place_sums, neg1[0:E, :], place_terms[0:E, :], start=True, stop=True).then_inc(s["place_done"], 1)
            projection(1, 1)
            projection(2, 0)
            table(0)
            projection(2, 1)
            table(1)
            table(2)
            table(3).then_inc(s["table_done"], 1)
            projection(3, 0)
            projection(3, 1)

            def x_transposes():
                for k in range(KD):
                    last = pe.transpose(ps[:, 3, k * SLOTS:(k + 1) * SLOTS], xg[0:SLOTS, k * P:(k + 1) * P],
                                        ident[0:SLOTS, 0:SLOTS])
                last.then_inc(s["tx_done"], 1)

            def act_transposes(g, b):
                pe.wait_ge(s["act_ok"], 2 * g + b + 1)
                for c in range(2):
                    last = pe.transpose(ps[:, 4 + b, c * P:(c + 1) * P], glu[:, b, c * P:(c + 1) * P], ident[:, :])
                last.then_inc(s["tA_done"], 1)

            def experts_block(g, e, n_load, side):
                pe.wait_ge(s["sel_ok"], e + 1)
                pe.wait_ge(s["xT_ok"], g + 1)
                for b in range(2):
                    for half in range(2):
                        col = DE * b + 512 * half
                        pe.matmul(ps[64 * half:64 * half + 64, b, :], sel_cur[:, side, :], bias_sb[:, col:col + 512],
                                  start=True, stop=False, skip_group_check=True)
                    for k in range(KD):
                        if b == 1 and k == 4:
                            act_transposes(g, 0)
                        if k % 2 == 0:
                            pe.wait_ge(w1_in[k // 2], 32 * n_load + 16 * (b + 1))
                        for half in range(2):
                            last = pe.matmul(ps[64 * half:64 * half + 64, b, :], xT[:, k, :],
                                             w1_buf[:, side, b, k, 512 * half:512 * half + 512],
                                             start=False, stop=(k == KD - 1), skip_group_check=True)
                    last.then_inc(s["hA_done" if b == 0 else "hB_done"], 1)
                pe.wait_ge(s["xg_in"], 16 * g + 32)
                pe.sem_inc(s["tx_turn"], 1)
                x_transposes()
                pe.wait_ge(s["y_ok"], g + 1)
                for half in range(2):
                    col = 2 * DE + 512 * half
                    pe.matmul(ps[64 * half:64 * half + 64, 2, :], sel_cur[:, side, :],
                              bias_sb[:, col:col + 512], start=True, stop=False, skip_group_check=True)
                for b in range(2):
                    pe.wait_ge(s["actT_ok"], 2 * g + b + 1)
                    w2 = (w2lo_buf[:, side], w2hi_buf)[b]
                    for k in range(4):
                        if b == 0 and k == 2:
                            act_transposes(g, 1)
                        if k % 2 == 0:
                            if b == 0:
                                pe.wait_ge(w2lo_in[k // 2], 16 * n_load + 16)
                            else:
                                pe.wait_ge(w2hi_in[k // 2], 16 * e + 16)
                        for half in range(2):
                            last = pe.matmul(ps[64 * half:64 * half + 64, 2, :],
                                             actT[:, b, k % 2, 64 * (k // 2):64 * (k // 2) + 64],
                                             w2[:, k, 512 * half:512 * half + 512],
                                             start=False, stop=(b == 1 and k == 3), skip_group_check=True)
                    last.then_inc(s["mm2lo_done" if b == 0 else "y_done"], 1)

            def expert(e, before_first):
                first = pe.value_load(cum_i[0:1, bass.ds(e, 1)], min_val=0, max_val=MAX_BLOCKS)
                end = pe.value_load(cum_i[0:1, bass.ds(e + 1, 1)], min_val=1, max_val=MAX_BLOCKS)
                n_load = pe.value_load(load_i[0:1, bass.ds(e, 1)], min_val=0, max_val=E - 1)
                side = pe.value_load(side_i[0:1, bass.ds(e, 1)], min_val=0, max_val=1)
                before_first()
                with pe.If(side == 0):
                    with pe.Fori(first, end) as g:
                        experts_block(g, e, n_load, 0)
                with pe.Else():
                    with pe.Fori(first, end) as g:
                        experts_block(g, e, n_load, 1)

            def first_transposes():
                pe.wait_ge(s["xg_in"], 16)
                x_transposes()

            pe.wait_ge(s["tables_ok"], 1)
            expert(0, first_transposes)
            with pe.Fori(1, E) as e:
                expert(e, lambda: None)

            def h_transposes(t):
                pe.wait_ge(acc_in[t], 16)
                if t > 1:
                    pe.wait_ge(s["h_lo"], t - 1)
                for k in range(KD):
                    last = pe.transpose(ps[:, tr_bank(t) + k // 4, (k % 4) * P:(k % 4 + 1) * P],
                                        hf[:, t, k * P:(k + 1) * P], ident[:, :])
                last.then_inc(s["h_tr"], 1)

            def gate(t):
                pe.wait_ge(s["h_hi_act"], t + 1)
                pe.wait_ge(s["h_hi_dve"], t + 1)
                for n in range(2):
                    sl = slice(512 * n, 512 * n + 512)
                    if t == 0:
                        pe.wait_ge(s["wg_ok"], n + 1)
                    if t:
                        pe.wait_ge(s["pg_sig"], 2 * (t - 1) + n + 1)
                    for k in range(KD):
                        pe.matmul(ps[:, 2 + n, :], h_hi[:, t, k, :], wg_hi[:, k, sl], start=(k == 0), stop=False)
                        pe.matmul(ps[:, 2 + n, :], h_hi[:, t, k, :], wg_lo[:, k, sl], start=False, stop=False)
                    pe.wait_ge(s["h_lo"], t + 1)
                    for k in range(KD):
                        last = pe.matmul(ps[:, 2 + n, :], h_lo[:, t, k, :], wg_hi[:, k, sl], start=False,
                                         stop=(k == KD - 1))
                    last.then_inc(s["pg_done"], 1)

            h_transposes(0)
            for t in range(NT):
                if t + 1 < NT:
                    h_transposes(t + 1)
                gate(t)

        @block.scalar
        def _(act):
            act.wait_ge(s["eps_ok"], 1)
            act.activation(small[:, 56:57], small[:, 57:58], ACT.Sqrt)
            for t in range(NT):
                act.wait_ge(x_in[t], 16)
                act.activation(junk, xs[:, t, :], ACT.Square, accum_out=small[:, t:t + 1]).then_inc(s["sq_done"], 1)
                act.wait_ge(s["rms_ok"], t + 1)
                act.activation(small[:, 4 + t:5 + t], small[:, 4 + t:5 + t], ACT.Sqrt).then_inc(s["sqrt_done"], 1)
            act.wait_ge(s["g_mix_in"], 16)
            act.wait_ge(s["xT_tr"], 1)
            for k in aT_order[0::2]:
                act.activation(aT[:, k, :], ps[:, k, :], ACT.Copy, scale=g_mix_c[:, k:k + 1]).then_inc(s["aT_act"], 1)

            def evac(u):
                g, j = u
                act.wait_ge(s["unit_done"], unit_no[u])
                bank = unit_bank(u)
                if g == "q":
                    ins = act.activation(qT[:, j, :], bank, ACT.Copy, scale=float(HD) ** -0.5)
                elif g == "v":
                    ins = act.activation(v[:, j, :], bank, ACT.Copy)
                elif g == "out":
                    ins = act.activation(oaT[:, j, :], bank, ACT.Copy)
                elif g == "vs":
                    ins = act.activation(vs[:, j, :], bank, ACT.Gelu_apprx_tanh)
                elif g == "u":
                    ins = act.activation(uT[:, j, :], bank, ACT.Gelu_apprx_tanh)
                else:
                    if g == "gb0" and j == 0:
                        act.wait_ge(s["bias_ok"], 1)
                    dst = gateA if g[1] == "a" else gateB
                    ins = act.activation(dst[:, 4 * int(g[2]) + j, :], bank, ACT.Exp, scale=-1.0)
                ins.then_inc(s["evac_act"], 1)

            for kind, a in pe_plan:
                if kind == "unit" and a[0] in ON_ACT:
                    evac(a)
                elif kind == "z":
                    for i in range(2):
                        z = ps[:, 3 * i:3 * i + 3, :].rearrange("p b n -> p (b n)")
                        if i == 0:
                            act.wait_ge(s["z_done"], a + 1)
                            if a:
                                act.wait_ge(s["unit_done"], unit_no[("out", a - 1)])
                        act.activation(att_e[i], z[:, 0:ATT], ACT.Abs).then_inc(s["abs_ok"], 1)
                        act.wait_ge(s["abs_ok"], 2 * a + i + 1)
                        act.activation(att_e[i], att_e[i], ACT.Exp, scale=-1.0).then_inc(s["exp_ok"], 1)
                        act.wait_ge(s["exp_ok"], 2 * a + i + 1)
                        act.activation(att_e[i], att_e[i], ACT.Ln, bias=1.0).then_inc(s["ln_ok"], 1)
                elif kind == "tri":
                    for i in range(2):
                        z = ps[:, 3 * i:3 * i + 3, :].rearrange("p b n -> p (b n)")
                        act.wait_ge(s["tri_done"], 2 * a + i + 1)
                        act.activation(att_e[i], z[:, 0:ATT], ACT.Exp).then_inc(s["w_ok"], 1)
                elif kind == "ln":
                    act.wait_ge(s["ln_stats"], 1)
                    act.activation(small[:, 12:16], small[:, 8:12], ACT.Sqrt).then_inc(s["ln_std"], 1)

            def square_h(t):
                act.wait_ge(s["h_ok"], 2 * (t + 1))
                act.activation(ps[:, 4:6, :].rearrange("p b n -> p (b n)"), h[:, t, :], ACT.Square,
                               accum_out=small[:, 20 + t:21 + t]).then_inc(s["h_sq"], 1)
                act.wait_ge(s["h_var"], t + 1)
                act.activation(small[:, 28 + t:29 + t], small[:, 24 + t:25 + t], ACT.Sqrt).then_inc(s["h_std"], 1)

            def cT_copy(t):
                act.wait_ge(s["c_tr"], t + 1)
                act.activation(cT[:, :, :].rearrange("p k t -> p (k t)"), ps[:, 0:2, :].rearrange("p b n -> p (b n)"),
                               ACT.Copy).then_inc(s["cT_ok"], 1)

            square_h(0)
            square_h(1)
            cT_copy(0)
            cT_copy(1)
            square_h(2)
            cT_copy(2)
            square_h(3)
            cT_copy(3)
            act.wait_ge(s["p_tr"], 1)
            act.activation(pT[:, :, :].rearrange("p k t -> p (k t)"), ps[:, 6:8, :].rearrange("p b n -> p (b n)"),
                           ACT.Copy).then_inc(s["pT_ok"], 1)
            for t in range(NT):
                if t in (0, NT - 1):
                    act.wait_ge(s["top_ok"], 1 + t // (NT - 1))
                last = act.activation(gates[:, t, :], top_v[:, t, 0:TOP_K], ACT.Exp, bias=nmax[:, t:t + 1],
                                      accum_out=gsum[:, t:t + 1])
            last.then_inc(s["gexp_ok"], 1)
            for t in range(NT):
                act.wait_ge(s["pp_done"], t + 1)
                act.activation(pp_out[t][:, :], ps[:, 4 + 2 * (t % 2):6 + 2 * (t % 2), :].rearrange("p b n -> p (b n)"),
                               ACT.Copy).then_inc(s["pp_ok"], 1)

            def x_copy():
                act.activation(xT[:, :, :].rearrange("p k s -> p (k s)"), ps[:, 3, :], ACT.Copy).then_inc(s["xT_ok"], 1)

            act.wait_ge(s["tx_done"], 1)
            x_copy()
            for t in range(NT):
                act.wait_ge(pp_written[t], 16)
            n_all = act.value_load(cum_i[0:1, E:E + 1], min_val=1, max_val=MAX_BLOCKS)
            with act.Fori(0, n_all) as g:
                for b in range(2):
                    act.wait_ge(s["glu_ok"], 2 * g + b + 1)
                    act.activation(sig[:, b, :], glu[:, b, :], ACT.Sigmoid, scale=SWIGLU_ALPHA).then_inc(s["sig_ok"], 1)
                    if b == 1:
                        act.wait_ge(s["tx_done"], g + 2)
                        x_copy()
                    act.wait_ge(s["tA_done"], 2 * g + b + 1)
                    act.activation(actT[:, b, :, :].rearrange("p c s -> p (c s)"), ps[:, 4 + b, 0:2 * P],
                                   ACT.Copy).then_inc(s["actT_ok"], 1)

            def round_wg(n):
                act.wait_ge(wg_in[n], 16)
                act.activation(wg_hi[:, :, 512 * n:512 * n + 512], wg[:, :, 512 * n:512 * n + 512],
                               ACT.Copy).then_inc(s["wg_hi_ok"], 1)

            def hT_copy(t):
                act.wait_ge(s["h_tr"], t + 1)
                for k in range(KD // 2):
                    last = act.activation(h_hi[:, t, k, :], ps[:, tr_bank(t), k * P:(k + 1) * P], ACT.Copy,
                                          scale=g_ple_c[:, k:k + 1])
                last.then_inc(s["h_hi_act"], 1)

            act.wait_ge(s["hB_done"], n_all)
            act.sem_inc(s["act_turn"], 1)
            round_wg(0)
            round_wg(1)
            hT_copy(0)
            hT_copy(1)
            for t in range(NT):
                act.wait_ge(acc_in[t], 16)
                if t:
                    act.wait_ge(s["t_sq"], t)
                act.activation(ps[:, 4:6, :].rearrange("p b n -> p (b n)"), hf[:, t, :], ACT.Square,
                               accum_out=small[:, 32 + t:33 + t]).then_inc(s["t_sq"], 1)
            act.wait_ge(s["t_var"], 1)
            act.activation(small[:, 40:40 + NT], small[:, 36:36 + NT], ACT.Sqrt).then_inc(s["t_std"], 1)
            act.wait_ge(s["t_rec"], 1)
            for t in range(NT):
                for n in range(2):
                    act.wait_ge(s["pg_done"], 2 * t + n + 1)
                    act.activation(sg[t % 2][:, 512 * n:512 * n + 512], ps[:, 2 + n, :], ACT.Sigmoid,
                                   scale=small[:, 32 + t:33 + t]).then_inc(s["pg_sig"], 1)
                    if n == 0 and t + 2 < NT:
                        hT_copy(t + 2)
                if t == NT - 1:
                    act.activation(small[:, 56:57], small[:, 36:37], ACT.Sqrt)
                for n in range(2):
                    act.wait_ge(s["h2_ok"], 2 * t + n + 1)
                    act.activation(ps[:, 4 + n, :], hf[:, t, 512 * n:512 * n + 512], ACT.Square,
                                   accum_out=small[:, 44 + 2 * n:45 + 2 * n]).then_inc(s["f_sq"], 1)
                act.wait_ge(s["f_var"], t + 1)
                act.activation(small[:, 52 + t:53 + t], small[:, 48 + t:49 + t], ACT.Sqrt).then_inc(s["f_std"], 1)

        @block.vector
        def _(dve):
            done = [0]

            def link(ins):
                done[0] += 1
                ins.then_inc(s["dve_step"], 1)
                dve.wait_ge(s["dve_step"], done[0])

            dve.memset(small[:, 57:58], 1.0).then_inc(s["eps_ok"], 1)
            link(dve.memset(zeros_e[:], 0.0))
            for t in range(NT):
                dve.wait_ge(s["sq_done"], t + 1)
                dve.tensor_scalar(small[:, 4 + t:5 + t], small[:, t:t + 1], 1.0 / D, EPS, ALU.mult,
                                  ALU.add).then_inc(s["rms_ok"], 1)
                dve.wait_ge(s["sqrt_done"], t + 1)
                link(dve.reciprocal(small[:, 16 + t:17 + t], small[:, 4 + t:5 + t]))
                dve.tensor_scalar(xs[:, t, :], xs[:, t, :], small[:, 16 + t:17 + t], None,
                                  ALU.mult).then_inc(s["xn_ok"], 1)
            dve.wait_ge(s["g_mix_in"], 16)
            dve.wait_ge(s["xT_tr"], 1)
            for k in aT_order[1::2]:
                dve.tensor_scalar(aT[:, k, :], ps[:, k, :], g_mix_c[:, k:k + 1], None, ALU.mult).then_inc(s["aT_dve"], 1)
            dve.wait_ge(s["small_in"], 16 * (4 + GROUPS))
            dve.wait_ge(s["wm_tr"], 1)
            link(dve.tensor_copy(wmT[:, :, :].rearrange("p g t -> p (g t)"),
                                 ps[:, 0:2, :].rearrange("p b n -> p (b n)")))
            dve.memset(wmT[SGU_CHUNK:P, :, 0:SGU_CHUNK], 0.0).then_inc(s["wmT_ok"], 1)

            def evac(u):
                g, j = u
                dve.wait_ge(s["unit_done"], unit_no[u])
                bank = unit_bank(u)
                if g == "k":
                    dve.tensor_copy(kT[:, j, :], bank).then_inc(s["evac_dve"], 1)
                elif g == "sv":
                    b3 = bank.rearrange("p (t n) -> p t n", t=NT)
                    bias = sgu_b_bc[:, j:j + 1, :].to_broadcast([P, NT, P])
                    link(dve.scalar_tensor_tensor(out=b3, in0=b3, scalar=sgu_g_c[:, j:j + 1], in1=bias,
                                                  op0=ALU.mult, op1=ALU.add))
                    e, c = evac_of[("u", j)]
                    dve.wait_ge(s[e], c)
                    link(dve.tensor_tensor(obT[:, j, :], bank, uT[:, j, :], ALU.mult))
                    dve.sem_inc(s["ob_ok"], 1)
                    dve.sem_inc(s["evac_dve"], 1)
                elif g in ("woa", "wob"):
                    gt = gateA if g == "woa" else gateB
                    link(dve.tensor_tensor(gt[:, j, :], gt[:, j, :], bank, ALU.mult))
                    dve.sem_inc(s["evac_dve"], 1)
                    if g == "wob":
                        dve.tensor_tensor(merged[:, j, :], gateA[:, j, :], gateB[:, j, :],
                                          ALU.add).then_inc(s["merged_ok"], 1)

            def sigmoid(u):
                g, j = u
                e, c = evac_of[u]
                dve.wait_ge(s[e], c)
                gt = (gateA if g[1] == "a" else gateB)[:, 4 * int(g[2]) + j, :]
                link(dve.tensor_scalar(gt, gt, 1.0, None, ALU.add))
                link(dve.reciprocal(gt, gt))

            for kind, a in pe_plan:
                if kind == "unit" and a[0] not in ON_ACT:
                    evac(a)
                elif kind == "unit" and a[0] in ("ga0", "ga1", "gb0", "gb1"):
                    sigmoid(a)
                elif kind == "unit" and a == ("vs", 3):
                    dve.wait_ge(s["evac_act"], evac_of[a][1])
                    for t in range(NT):
                        link(dve.bn_stats(bn6[:, t, :], vs[:, t, :]))
                        link(dve.bn_aggr(bn2[:, t, :], bn6[:, t, :]))
                    dve.tensor_scalar(small[:, 8:12], bn2[:, :, 1], EPS, None, ALU.add).then_inc(s["ln_stats"], 1)
                elif kind == "ln":
                    dve.wait_ge(s["ln_std"], 1)
                    link(dve.reciprocal(small[:, 56:60], small[:, 12:16]))
                    for t in range(NT):
                        dve.tensor_scalar(vs[:, t, :], vs[:, t, :], bn2[:, t, 0:1], small[:, 56 + t:57 + t],
                                          ALU.subtract, ALU.mult).then_inc(s["vs_ok"], 1)
                elif kind == "z":
                    zs = [ps[:, 3 * i:3 * i + 3, :].rearrange("p b n -> p (b n)")[:, 0:ATT] for i in range(2)]
                    for i in range(2):
                        dve.wait_ge(s["ln_ok"], 2 * a + i + 1)
                        dve.scalar_tensor_tensor(out=att_s[i], in0=zs[i], scalar=0.0, in1=att_e[i],
                                                 op0=ALU.max, op1=ALU.add).then_inc(s["sp_ok"], 1)

            dve.wait_ge(s["x_again"], 16 * NT)
            dve.wait_ge(s["g_bc_in"], 16)
            for t in range(NT):
                for n in range(2):
                    u = ("wo", 2 * t + n)
                    dve.wait_ge(s["unit_done"], unit_no[u])
                    sl = slice(n * 512, (n + 1) * 512)
                    link(dve.tensor_tensor(h[:, t, sl], unit_bank(u), xs[:, t, sl], ALU.add))
                    dve.sem_inc(s["evac_dve"], 1)
                    dve.sem_inc(s["h_ok"], 1)
                dve.wait_ge(s["h_sq"], t + 1)
                dve.tensor_scalar(small[:, 24 + t:25 + t], small[:, 20 + t:21 + t], 1.0 / D, EPS, ALU.mult,
                                  ALU.add).then_inc(s["h_var"], 1)
                dve.wait_ge(s["h_std"], t + 1)
                link(dve.reciprocal(small[:, 60 + t % 2:61 + t % 2], small[:, 28 + t:29 + t]))
                dve.scalar_tensor_tensor(out=xs[:, t, :], in0=h[:, t, :], scalar=small[:, 60 + t % 2:61 + t % 2],
                                         in1=g_moe_bc[:, :], op0=ALU.mult, op1=ALU.mult).then_inc(s["c_ok"], 1)

            dve.wait_ge(s["const_pool"], 1)
            link(dve.tensor_copy(iota_f[:, :], iota_i[:, :]))
            for ts in (range(NT - 1), range(NT - 1, NT)):
                sl = slice(ts[0], ts[-1] + 1)
                dve.wait_ge(s["logit_done"], ts[-1] + 1)
                for t in ts:
                    last = dve.tensor_tensor(lg[:, t, :], logit_ps(t), b_router_bc[:, :], ALU.add)
                link(last)
                for t in ts:
                    last = dve.max(top_v[:, t, :], lg[:, t, :])
                link(last)
                dve.tensor_scalar(nmax[:, sl], top_v[:, sl, 0], -1.0, None, ALU.mult).then_inc(s["top_ok"], 1)
                for t in ts:
                    last = dve.max_index(top_i[:, t, :], top_v[:, t, :], lg[:, t, :])
                link(last)
                link(dve.tensor_copy(top_f[:, sl, :], top_i[:, sl, :]))
                for t in ts:
                    last = dve.tensor_tensor(onehot[:, t, :, :],
                                             top_f[:, t, 0:TOP_K].unsqueeze(2).to_broadcast([P, TOP_K, E]),
                                             iota_f[:, 0:E].unsqueeze(1).to_broadcast([P, TOP_K, E]), ALU.is_equal)
                link(last)
                for t in ts:
                    last = dve.tensor_reduce(mask[:, t, :], onehot[:, t, :, :].rearrange("p k e -> p e k"), AX_X,
                                             ALU.add)
                link(last)
                dve.tensor_copy(mask_b[:, sl, :], mask[:, sl, :]).then_inc(s["mask_ok"], 1)
            dve.wait_ge(s["gexp_ok"], 1)
            link(dve.reciprocal(grec[:, :], gsum[:, :]))
            link(dve.tensor_tensor(gates[:, :, :], gates[:, :, :], grec[:, :].unsqueeze(2).to_broadcast([P, NT, TOP_K]),
                                   ALU.mult))
            place, nb = mask[:, 0, :], mask[:, 1, :]
            dve.wait_ge(s["rank_done"], 1)
            cnt = ps[:, 2, NT * E:(NT + 1) * E]
            link(dve.tensor_scalar(n_blk[:, 1, :], cnt, float(SLOTS), 1.0, ALU.is_gt, ALU.add))
            for j in range(2, T // SLOTS):
                link(dve.scalar_tensor_tensor(out=nb if j == T // SLOTS - 1 else n_blk[:, j % 2, :], in0=cnt,
                                              scalar=float(SLOTS * j), in1=n_blk[:, (j - 1) % 2, :],
                                              op0=ALU.is_gt, op1=ALU.add))
            N2 = E - 2
            hv, cnt_h, hi_n, lo_n, t0, t1 = (heavy[:, i, 2:E] for i in range(6))
            n_h, n_l, n_m, x_h, x_h1 = (n_heavy[:, i:i + 1] for i in range(5))
            link(dve.tensor_scalar(hv, nb[:, 2:E], 1.0, None, ALU.is_gt))
            link(dve.tensor_tensor_scan(cnt_h, zeros_e[:, 2:E], hv, 0.0, ALU.add, ALU.add))
            dve.tensor_copy(n_h, heavy[:, 1, E - 1:E])
            link(dve.tensor_scalar(n_l, heavy[:, 1, E - 1:E], -1.0, float(N2), ALU.mult, ALU.add))
            link(dve.tensor_tensor(n_m, n_h, n_l, ALU.min))
            link(dve.tensor_tensor(x_h, n_h, n_m, ALU.subtract))
            dve.tensor_scalar(x_h1, x_h, -1.0, None, ALU.add)
            dve.tensor_tensor(hi_n, cnt_h, hv, ALU.subtract)
            dve.tensor_tensor(place[:, 0:1], nb[:, 1:2], nb[:, 0:1], ALU.is_lt)
            link(dve.tensor_tensor(place[:, 1:2], nb[:, 1:2], nb[:, 0:1], ALU.is_ge))
            link(dve.tensor_tensor(lo_n, iota_f[:, 0:N2], hi_n, ALU.subtract))
            dve.tensor_scalar(t0, hi_n, x_h1, 0.0, ALU.subtract, ALU.max)
            link(dve.tensor_scalar(t1, lo_n, n_m, None, ALU.min))
            dve.tensor_tensor(t0, t0, hi_n, ALU.add)
            link(dve.scalar_tensor_tensor(out=t1, in0=t1, scalar=x_h, in1=lo_n, op0=ALU.add, op1=ALU.add))
            link(dve.tensor_tensor(t0, t0, t1, ALU.subtract))
            link(dve.tensor_tensor(t0, t0, hv, ALU.mult))
            link(dve.scalar_tensor_tensor(out=place[:, 2:E], in0=t0, scalar=2.0, in1=t1, op0=ALU.add, op1=ALU.add))
            link(dve.tensor_tensor(mask[:, 2:4, :], mask[:, 0:2, :], ident[:, 0:E].unsqueeze(1).to_broadcast([P, 2, E]),
                                   ALU.mult))
            link(dve.tensor_reduce(place_col, mask[:, 2:4, :], AX_X, ALU.add))
            p_place, p_blocks = place_col[:, 0:1], place_col[:, 1:2]
            dve.tensor_scalar(place_terms[:, 0:E], place, p_place, p_blocks, ALU.is_gt, ALU.mult)
            dve.tensor_scalar(place_terms[:, E:2 * E + 1], iota_f[:, 0:E + 1], p_place, p_blocks, ALU.is_gt, ALU.mult)
            link(dve.tensor_scalar(place_terms[:, 2 * E + 1:3 * E + 1], iota_f[:, 0:E], p_place, tok1_f[:, 0:1],
                                   ALU.is_equal, ALU.mult))
            dve.sem_inc(s["place_ok"], 1)
            dve.wait_ge(s["place_done"], 1)
            link(dve.tensor_scalar(mask[:, 2, :], place_sums[:, 0:E], -float(SLOTS), None, ALU.mult))
            link(dve.tensor_tensor(posm[:, :, :], ps[:, 2, 0:NT * E].rearrange("p (t e) -> p t e", t=NT),
                                   mask[:, 2, :].unsqueeze(1).to_broadcast([P, NT, E]), ALU.add))
            dve.wait_ge(s["c_written"], 16 * NT)
            for t in range(NT):
                last = dve.tensor_tensor(onehot[:, t, :, :], onehot[:, t, :, :],
                                         posm[:, t, :].unsqueeze(1).to_broadcast([P, TOP_K, E]), ALU.mult)
            link(last)
            link(dve.tensor_reduce(pos[:, :], onehot[:, :, :, :].rearrange("p t k e -> p (t k) e"), AX_X, ALU.add))
            link(dve.tensor_copy(pos_i[:, 0, :], pos[:, :]))
            link(dve.tensor_scalar(pos_i[:, 1, :], pos_i[:, 0, :], 6, None, ALU.arith_shift_right))
            link(dve.tensor_scalar(pos_i[:, 2, :], pos_i[:, 0, :], SLOTS - 1, None, ALU.bitwise_and))
            link(dve.tensor_copy(pos_f[:, :, :], pos_i[:, 1:3, :]))
            for t in range(NT):
                ks = slice(TOP_K * t, TOP_K * t + TOP_K)
                shape = [P, TOP_K, NG]
                io = iota_f[:, :].unsqueeze(1).to_broadcast(shape)
                hot = route[:, ks, SLOTS:SLOTS + NG]
                dve.tensor_tensor(route[:, ks, 0:SLOTS], io, pos_f[:, 1, ks].unsqueeze(2).to_broadcast(shape),
                                  ALU.is_equal)
                link(dve.tensor_tensor(hot, io, pos_f[:, 0, ks].unsqueeze(2).to_broadcast(shape), ALU.is_equal))
                link(dve.tensor_tensor(route[:, ks, SLOTS + NG:SLOTS + 2 * NG], hot,
                                       gates[:, t, :].unsqueeze(2).to_broadcast(shape), ALU.mult))
                dve.tensor_scalar(hot, hot, tok1_f[:, t:t + 1], None, ALU.mult).then_inc(s["route_ok"], 1)
            dve.tensor_scalar(cum_i[:, :], place_sums[:, E:2 * E + 1], -1.0, None, ALU.mult)
            link(dve.tensor_scalar(cum_f[:, 0:E], place_sums[:, 2 * E + 1:3 * E + 1], -1.0, -1.0, ALU.mult, ALU.add))
            link(dve.tensor_scalar(side_i[:, :], iota_f[:, 0:E + 1], cum_f[:, 0:1], None, ALU.add))
            link(dve.tensor_scalar(side_i[:, :], side_i[:, :], 1, None, ALU.bitwise_and))
            dve.tensor_copy(load_i[:, 2:E], iota_i[:, 2:E])
            dve.tensor_copy(load_i[:, 0:2], cum_f[:, 0:2])
            dve.memset(perm_i[:, E:E + 1], 0)
            dve.tensor_copy(perm_i[:, 0:E], cum_f[:, 0:E])
            dve.wait_ge(s["table_done"], 1)
            tab = ps[:, 0, 0:NG]
            dve.tensor_scalar(g_idx[:, :], ps[0:SLOTS, 0, 0:1], -1.0, 0.0, ALU.add, ALU.max).then_inc(s["first_ok"], 1)
            dve.tensor_scalar(tok_idx[:, :], tab, -1.0, 0.0, ALU.add, ALU.max)
            dve.tensor_copy(gate_tab[:, :], ps[:, 0, NG:2 * NG])
            dve.tensor_scalar(tab_t[:, 0, :], tab, 0.0, pad_c[:, 0:1], ALU.is_equal, ALU.mult)
            link(dve.tensor_scalar(tab_t[:, 1, :], tab, 2.0, pad_c[:, 1:2], ALU.mult, ALU.add))
            link(dve.tensor_tensor(dst_idx[:, :], tab_t[:, 0, :], tab_t[:, 1, :], ALU.add))
            dve.sem_inc(s["tables_ok"], 1)
            dve.sem_inc(s["y_ok"], 1)

            def experts_block(g):
                for b in range(2):
                    hh = ps[:, b, :].rearrange("p (n two) -> p n two", two=2)
                    dve.wait_ge(s["hA_done" if b == 0 else "hB_done"], g + 1)
                    dve.tensor_scalar(glu[:, b, :], hh[:, :, 0], SWIGLU_LIMIT, None, ALU.min).then_inc(s["glu_ok"], 1)
                    dve.tensor_scalar(lin[:, b, :], hh[:, :, 1], SWIGLU_LIMIT, -SWIGLU_LIMIT, ALU.min,
                                      ALU.max).then_inc(s["moe_step"], 1)
                    dve.wait_ge(s["sig_ok"], 2 * g + b + 1)
                    dve.tensor_tensor(glu[:, b, :], glu[:, b, :], sig[:, b, :], ALU.mult).then_inc(s["moe_step"], 1)
                    dve.wait_ge(s["moe_step"], 4 * g + 2 * b + 2)
                    dve.scalar_tensor_tensor(out=glu[:, b, :], in0=lin[:, b, :], scalar=1.0, in1=glu[:, b, :],
                                             op0=ALU.add, op1=ALU.mult).then_inc(s["act_ok"], 1)
                dve.wait_ge(s["y_done"], g + 1)
                dve.wait_ge(s["acc_done"], 16 * g + 16 * (NT + 1))
                dve.tensor_scalar(y_sb[:, :], ps[:, 2, :], gate_tab[:, bass.ds(g, 1)], None,
                                  ALU.mult).then_inc(s["y_ok"], 1)

            def selector(e):
                side = dve.value_load(side_i[0:1, bass.ds(e, 1)], min_val=0, max_val=1)
                expert = dve.value_load(perm_i[0:1, bass.ds(e, 1)], min_val=0, max_val=E - 1)
                dve.tensor_copy(sel_cur[:, bass.ds(side, 1), :].rearrange("p o s -> p (o s)"),
                                sel_sb[:, bass.ds(expert, 1)].to_broadcast([96, SLOTS])).then_inc(s["sel_ok"], 1)

            n_all = dve.value_load(cum_i[0:1, E:E + 1], min_val=1, max_val=MAX_BLOCKS)
            selector(0)
            for t in range(NT):
                dve.wait_ge(pp_written[t], 16)
            with dve.Fori(0, E) as e:
                first = dve.value_load(cum_i[0:1, bass.ds(e, 1)], min_val=0, max_val=MAX_BLOCKS)
                end = dve.value_load(cum_i[0:1, bass.ds(e + 1, 1)], min_val=1, max_val=MAX_BLOCKS)
                selector(e + 1)
                with dve.Fori(first, end) as g:
                    experts_block(g)

            def h_parts(t):
                dve.wait_ge(s["h_tr"], t + 1)
                banks = [ps[:, tr_bank(t) + k // 4, (k % 4) * P:(k % 4 + 1) * P] for k in range(KD)]
                for k in range(KD // 2, KD):
                    last = dve.tensor_scalar(h_hi[:, t, k, :], banks[k], g_ple_c[:, k:k + 1], None, ALU.mult)
                last.then_inc(s["h_hi_dve"], 1)
                dve.wait_ge(s["h_hi_dve"], t + 1)
                for k in list(range(KD // 2, KD)) + list(range(KD // 2)):
                    if k == 0:
                        dve.wait_ge(s["h_hi_act"], t + 1)
                    last = dve.scalar_tensor_tensor(out=h_lo[:, t, k, :], in0=banks[k], scalar=g_ple_c[:, k:k + 1],
                                                    in1=h_hi[:, t, k, :].bitcast(F32), op0=ALU.mult, op1=ALU.subtract)
                last.then_inc(s["h_lo"], 1)

            dve.wait_ge(s["y_done"], n_all)
            for n in range(2):
                sl = slice(512 * n, 512 * n + 512)
                dve.wait_ge(s["wg_hi_ok"], n + 1)
                dve.tensor_tensor(wg_lo[:, :, sl], wg[:, :, sl], wg_hi[:, :, sl].bitcast(F32),
                                  ALU.subtract).then_inc(s["wg_ok"], 1)
            h_parts(0)
            h_parts(1)
            dve.wait_ge(s["t_sq"], NT)
            dve.tensor_scalar(small[:, 36:36 + NT], small[:, 32:32 + NT], 1.0 / D, EPS, ALU.mult,
                              ALU.add).then_inc(s["t_var"], 1)
            dve.wait_ge(s["t_std"], 1)
            dve.reciprocal(small[:, 32:32 + NT], small[:, 40:40 + NT]).then_inc(s["t_rec"], 1)
            for t in range(NT):
                if 2 <= t + 1 < NT:
                    h_parts(t + 1)
                if t == 0:
                    dve.wait_ge(s["pp_in"], 32)
                for n in range(2):
                    sl = slice(512 * n, 512 * n + 512)
                    dve.wait_ge(s["pg_sig"], 2 * t + n + 1)
                    link(dve.tensor_tensor(sg[t % 2][:, sl], sg[t % 2][:, sl], pp[:, t, sl], ALU.mult))
                    dve.tensor_tensor(hf[:, t, sl], hf[:, t, sl], sg[t % 2][:, sl], ALU.add).then_inc(s["h2_ok"], 1)
                dve.wait_ge(s["f_sq"], 2 * t + 2)
                link(dve.tensor_tensor(small[:, 48 + t:49 + t], small[:, 44:45], small[:, 46:47], ALU.add))
                dve.tensor_scalar(small[:, 48 + t:49 + t], small[:, 48 + t:49 + t], 1.0 / D, EPS, ALU.mult,
                                  ALU.add).then_inc(s["f_var"], 1)
                dve.wait_ge(s["f_std"], t + 1)
                link(dve.reciprocal(small[:, 63:64], small[:, 52 + t:53 + t]))
                for n in range(2):
                    sl = slice(512 * n, 512 * n + 512)
                    dve.scalar_tensor_tensor(out=outs_sb[:, t, sl], in0=hf[:, t, sl], scalar=small[:, 63:64],
                                             in1=gf_bc[:, sl], op0=ALU.mult, op1=ALU.mult).then_inc(s["out_ok"], 1)

        @block.gpsimd
        def _(pool):
            done = [0]

            def link(ins):
                done[0] += 1
                ins.then_inc(s["pool_step"], 1)
                pool.wait_ge(s["pool_step"], done[0])

            link(pool.memset(ident[:], 0.0))
            pool.affine_select(out=ident[:], in_=ident[:], pattern=[[-1, P]], compare_op=ALU.not_equal, fill=1.0,
                               base=0, channel_multiplier=1).then_inc(s["ident_ok"], 1)
            pool.memset(neg1[:], -1.0)
            pool.memset(tri[:], -1.0)
            pool.memset(ones_b[:], 1.0)
            pool.memset(upper_b[:], 1.0)
            link(pool.memset(sel_sb[:], 0.0))
            link(pool.affine_select(out=tri[:], in_=tri[:], pattern=[[-1, P]], compare_op=ALU.is_ge, fill=0.0,
                                    base=0, channel_multiplier=1))
            link(pool.affine_select(out=upper_b[:], in_=upper_b[:], pattern=[[1, P]], compare_op=ALU.is_gt, fill=0.0,
                                    base=0, channel_multiplier=-1))
            for j in range(3):
                v_ = sel_sb[32 * j:32 * j + 32, :]
                link(pool.affine_select(out=v_, in_=v_, pattern=[[-1, E]], compare_op=ALU.not_equal, fill=1.0,
                                        base=0, channel_multiplier=1))
            link(pool.iota(iota_i[:], pattern=[[1, NG]], base=0, channel_multiplier=0))
            link(pool.iota(pad_i[:, 0:NT], pattern=[[P, NT]], base=1, channel_multiplier=1))
            for half in range(2):
                sl = slice(64 * half, 64 * half + 64)
                link(pool.iota(pad_i[sl, 4:5], pattern=[[1, 1]], base=2 * T + 2, channel_multiplier=2))
                link(pool.iota(pad_i[sl, 5:6], pattern=[[1, 1]], base=half - 2, channel_multiplier=0))
            pool.tensor_copy(tok1_f[:, :], pad_i[:, 0:NT])
            link(pool.tensor_copy(pad_c[:, :], pad_i[:, 4:6]))
            pool.sem_inc(s["const_pool"], 1)

            pool.wait_ge(s["bias_in"], 16 * 6)
            link(pool.tensor_copy(bias_sb[:, :], bias_f32[0:96, :]))
            for j in (1, 2):
                for r in range(j, 3):
                    rows = slice(32 * r, 32 * r + 32)
                    link(pool.tensor_tensor(bias_f32[rows, :], bias_f32[rows, :], bias_sb[rows, :], ALU.subtract))
                    link(pool.tensor_copy(bias_sb[rows, :], bias_f32[rows, :]))
            pool.sem_inc(s["bias_ok"], 1)

            pool.dma_start(acc_rows[T:ROWS, :], x[0, 0:SLOTS, :]).then_inc(s["acc_done"], 16)

            def mask_diagonals(a):
                for t in range(NT):
                    d = a[:, OFF[t]:OFF[t] + P]
                    last = pool.affine_select(out=d, in_=d, pattern=[[1, P]], compare_op=ALU.is_gt, fill=0.0,
                                              base=0, channel_multiplier=-1)
                return last

            for hp in range(HP):
                for i in range(2):
                    pool.wait_ge(s["sp_ok"], 2 * hp + i + 1)
                    link(mask_diagonals(att_s[i]))
                    a, sums = att_s[i], sp_sum[i]
                    q3 = slice(P, 2 * P)
                    pool.tensor_tensor(sums[0][:, 0:P], a[:, OFF[1] + P:OFF[1] + 2 * P], a[:, OFF[2]:OFF[2] + P], ALU.add)
                    link(pool.tensor_tensor(sums[1], a[:, OFF[2] + P:OFF[2] + 2 * P], a[:, OFF[3]:OFF[3] + P], ALU.add))
                    pool.tensor_tensor(sums[0][:, q3], a[:, OFF[1] + 2 * P:OFF[1] + 3 * P], sums[1],
                                       ALU.add).then_inc(s["sp_masked"], 1)
                for i in range(2):
                    pool.wait_ge(s["w_ok"], 2 * hp + i + 1)
                    mask_diagonals(att_e[i]).then_inc(s["w_masked"], 1)
            for t in range(NT):
                pool.wait_ge(s["h_ok"], 2 * (t + 1))
                pool.dma_start(acc_rows[t * P:(t + 1) * P, :], h[:, t, :]).then_inc(s["acc_done"], 16)
                pool.wait_ge(s["c_ok"], t + 1)
                pool.dma_start(c_rows[t * P:(t + 1) * P, :], xs[:, t, :]).then_inc(s["c_written"], 16)

            def gather():
                pool.indirect_dma_start(out=xg[0:SLOTS, :], out_offset=None, in_=c_rows,
                                        in_offset=bass.IndirectOffsetOnAxis(ap=g_idx[:, 0:1], axis=0),
                                        ).then_inc(s["xg_in"], 16)

            pool.wait_ge(s["c_written"], 16 * NT)
            pool.wait_ge(pp_written[0], 16)
            pool.wait_ge(s["first_ok"], 1)
            gather()
            pool.wait_ge(s["tables_ok"], 1)
            base = done[0]

            def gather_next(g, n):
                pool.wait_ge(s["tx_done"], g + 1)
                pool.tensor_copy(g_idx[:, :], tok_idx[0:SLOTS, bass.ds(g + 1, 1)]).then_inc(s["pool_step"], 1)
                pool.wait_ge(s["pool_step"], base + n)
                pool.sem_inc(s["dma_turn"], 1)
                gather()

            def scatter(g, n):
                pool.wait_ge(s["acc_done"], 16 * g + 16 * (NT + 1))
                pool.tensor_copy(s_idx[:, :], dst_idx[:, bass.ds(g, 1)]).then_inc(s["pool_step"], 1)
                pool.wait_ge(s["pool_step"], base + n)
                pool.wait_ge(s["y_ok"], g + 2)
                pool.sem_inc(s["dma_turn"], 1)
                pool.indirect_dma_start(out=acc_halves, out_offset=bass.IndirectOffsetOnAxis(ap=s_idx[:, 0:1], axis=0),
                                        in_=y_sb[:, :], in_offset=None, compute_op=ALU.add).then_inc(s["acc_done"], 16)

            gather_next(0, 1)
            n_all = pool.value_load(cum_i[0:1, E:E + 1], min_val=E, max_val=MAX_BLOCKS)
            with pool.Fori(1, n_all) as g:
                gather_next(g, 2 * g)
                scatter(g - 1, 2 * g + 1)
            scatter(n_all - 1, 2 * n_all)


_INS = ["x", "p", "g_mix", "w_in", "w_out_a", "w_out_b", "w_out", "sgu_norm", "sgu_w", "sgu_b", "g_moe", "w_router",
        "b_router", "w1", "b1", "w2", "b2", "g_ple", "w_ple_gate", "w_ple_proj", "g_final"]


def kernel(**inputs):
    import numpy as _np
    import concourse.bacc as _bacc
    from concourse import mybir as _mybir
    from concourse.bass_utils import run_bass_kernel_spmd as _run

    nc = _bacc.Bacc("TRN2", target_bir_lowering=False, num_devices=1)
    arrays, args = {}, []
    for name in _INS:
        a = _np.ascontiguousarray(inputs[name])
        arrays[f"in_{name}_dram"] = a
        args.append(nc.dram_tensor(f"in_{name}_dram", a.shape, _mybir.dt.from_np(a.dtype), kind="ExternalInput").ap())
    shape = inputs["x"].shape
    args.append(nc.dram_tensor("out_0_dram", shape, _mybir.dt.float32, kind="ExternalOutput").ap())
    hybrid_block(nc, *args)
    r = _run(nc, [arrays], core_ids=[0])
    return r.results[0]["out_0_dram"]
```
